# Optimizing a Trainium2 kernel written in Bass

```python
import jax, jax.numpy as jnp
from jax import lax
import numpy as np

D_MODEL = 1024
BATCH = 1
SEQ = 512
DEPTH = 2
DEC_BATCH = 8
DEC_SEQ = 4
PAST_LEN = 256
PAGE_SIZE = 128

HEAD_DIM = 64
N_HEADS_A = 6
N_KV_A = 2
N_HEADS_B = 6
N_IDX_HEADS = 4
IDX_DIM = 64
TOPK_MAX = 256
POOL_WINDOWS = (2, 4, 8, 16)
N_POOL_GROUPS = 4
POOL_GROUP_DIM = 64
POOL_STATE = 15
WIDTH_A = N_HEADS_A * HEAD_DIM
WIDTH_KV_A = N_KV_A * HEAD_DIM
WIDTH_B = N_HEADS_B * HEAD_DIM
WIDTH_C = N_POOL_GROUPS * POOL_GROUP_DIM
MIX_WIDTH = WIDTH_A + WIDTH_B + WIDTH_C
IN_SPLITS = (WIDTH_A, WIDTH_KV_A, WIDTH_KV_A, N_IDX_HEADS * IDX_DIM, IDX_DIM, N_IDX_HEADS, WIDTH_B, WIDTH_B, WIDTH_B, WIDTH_C)
IN_WIDTH = sum(IN_SPLITS)
D_FF = 2816
CONV_WIDTH = 3
PLE_DIM = 256
ROPE_THETA = 10000.0
Q_BLOCK = 128
EPS = 1e-6

kernel_name = 'hybrid_dsa_stickbreak_pool_decoder_step'

def rmsnorm(x, g):
    xf = x.astype(jnp.float32)
    r = lax.rsqrt(jnp.mean(xf * xf, axis=-1, keepdims=True) + EPS)
    return (xf * r).astype(x.dtype) * g

def rope(x, pos):
    half = x.shape[-1] // 2
    inv = ROPE_THETA ** (-jnp.arange(half, dtype=jnp.float32) / half)
    ang = pos.astype(jnp.float32)[:, None] * inv[None, :]
    cos = jnp.cos(ang)[:, None, :]
    sin = jnp.sin(ang)[:, None, :]
    xf = x.astype(jnp.float32)
    x1, x2 = xf[..., :half], xf[..., half:]
    return jnp.concatenate([x1 * cos - x2 * sin, x2 * cos + x1 * sin], axis=-1).astype(x.dtype)

def split_columns(proj):
    out, start = [], 0
    for w in IN_SPLITS:
        out.append(proj[..., start:start + w])
        start += w
    return out

def gather_pages(pool, page_table):
    g = pool[page_table]
    return g.reshape(g.shape[0], g.shape[1] * g.shape[2], *g.shape[3:])

def sweep_query_blocks(fn, q_pos, *q_arrays):
    T = q_pos.shape[0]
    qb = min(Q_BLOCK, T)
    nb = T // qb
    blocks = tuple(jnp.moveaxis(a.reshape(a.shape[0], nb, qb, *a.shape[2:]), 1, 0) for a in q_arrays)
    out = lax.map(lambda args: fn(*args), (q_pos.reshape(nb, qb),) + blocks)
    out = jnp.moveaxis(out, 0, 1)
    return out.reshape(out.shape[0], T, *out.shape[3:])

def dsa_block(q_pos, q, qi, wi, k, v, ki, k_pos, topk):
    s_idx = jnp.einsum('bqhd,bsd->bqhs', qi, ki).astype(jnp.float32) * IDX_DIM ** -0.5
    score = jnp.einsum('bqhs,bqh->bqs', jax.nn.relu(s_idx), wi.astype(jnp.float32))
    causal = k_pos[None, :] <= q_pos[:, None]
    score = jnp.where(causal[None], score, -jnp.inf)
    _, sel = lax.top_k(score, topk)
    k_sel = jax.vmap(lambda kb, ib: kb[ib])(k, sel)
    v_sel = jax.vmap(lambda vb, ib: vb[ib])(v, sel)
    valid = k_pos[sel] <= q_pos[None, :, None]
    B, Tq, HA, dh = q.shape
    qg = q.reshape(B, Tq, N_KV_A, HA // N_KV_A, dh)
    logits = jnp.einsum('bqngd,bqknd->bqngk', qg, k_sel).astype(jnp.float32) * dh ** -0.5
    logits = jnp.where(valid[:, :, None, None, :], logits, -jnp.inf)
    attn = jax.nn.softmax(logits, axis=-1).astype(v.dtype)
    o = jnp.einsum('bqngk,bqknd->bqngd', attn, v_sel)
    return o.reshape(B, Tq, HA * dh)

def stick_breaking_block(q_pos, q, k, v, k_pos):
    z = jnp.einsum('bqhd,bshd->bhqs', q, k).astype(jnp.float32) * q.shape[-1] ** -0.5
    strict = (k_pos[None, :] < q_pos[:, None])[None, None]
    log_rem = jnp.where(strict, jax.nn.log_sigmoid(-z), 0.0)
    rev = lax.cumsum(log_rem, axis=3, reverse=True)
    log_a = jnp.where(strict, z + rev, -jnp.inf)
    a = jnp.exp(log_a).astype(v.dtype)
    return jnp.einsum('bhqs,bshd->bqhd', a, v)

def pool_mix(u_ext, pos, w_pool, pool_scale):
    B = u_ext.shape[0]
    T = u_ext.shape[1] - POOL_STATE
    uf = u_ext.astype(jnp.float32)
    cs = jnp.concatenate([jnp.zeros((B, 1, WIDTH_C), jnp.float32), jnp.cumsum(uf, axis=1)], axis=1)
    u = uf[:, POOL_STATE:]
    means = []
    for g, w in enumerate(POOL_WINDOWS):
        c0, c1 = g * POOL_GROUP_DIM, (g + 1) * POOL_GROUP_DIM
        upper = cs[:, POOL_STATE + 1:, c0:c1]
        lower = cs[:, POOL_STATE + 1 - w:POOL_STATE + 1 - w + T, c0:c1]
        cnt = jnp.minimum(w, pos + 1).astype(jnp.float32)[None, :, None]
        means.append((upper - lower) / cnt)
    pooled = (jnp.concatenate(means, axis=-1) - u).astype(u_ext.dtype)
    pg = pooled.reshape(B, T, N_POOL_GROUPS, POOL_GROUP_DIM)
    y = jnp.einsum('btgc,gcd->btgd', pg, w_pool).reshape(B, T, WIDTH_C)
    return y * pool_scale

def conv_ffn(f, gate_prefix, w_up, conv_w, conv_b, w_down):
    up = f @ w_up
    gate, val = up[..., :D_FF], up[..., D_FF:]
    g_ext = jnp.concatenate([gate_prefix, gate], axis=1)
    T = gate.shape[1]
    conv = conv_b + g_ext[:, 0:T] * conv_w[0]
    for j in range(1, CONV_WIDTH):
        conv = conv + g_ext[:, j:j + T] * conv_w[j]
    y = (jax.nn.silu(conv) * val) @ w_down
    return y, g_ext[:, -(CONV_WIDTH - 1):]

def trunk_layer(h, p, pos0, past, weights):
    (g_attn, w_in, g_q_a, g_k_a, w_pool, pool_scale, w_out,
     g_ffn, w_up, conv_w, conv_b, w_down, g_ple, w_ple_gate, w_ple_proj) = weights
    B, T, _ = h.shape
    pos = pos0 + jnp.arange(T, dtype=jnp.int32)
    a = rmsnorm(h, g_attn)
    qa, ka, va, qi, ki, wi, qb, kb, vb, u = split_columns(a @ w_in)
    qa = rope(rmsnorm(qa.reshape(B, T, N_HEADS_A, HEAD_DIM), g_q_a), pos)
    ka = rope(rmsnorm(ka.reshape(B, T, N_KV_A, HEAD_DIM), g_k_a), pos)
    va = va.reshape(B, T, N_KV_A, HEAD_DIM)
    qi = rope(qi.reshape(B, T, N_IDX_HEADS, IDX_DIM), pos)
    ki = rope(ki[:, :, None, :], pos)[:, :, 0]
    wi = wi * N_IDX_HEADS ** -0.5
    qb = qb.reshape(B, T, N_HEADS_B, HEAD_DIM)
    kb = kb.reshape(B, T, N_HEADS_B, HEAD_DIM)
    vb = vb.reshape(B, T, N_HEADS_B, HEAD_DIM)
    if past is None:
        ka_f, va_f, ki_f, kb_f, vb_f = ka, va, ki, kb, vb
        pool_prefix = jnp.zeros((B, POOL_STATE, WIDTH_C), u.dtype)
        conv_prefix = jnp.zeros((B, CONV_WIDTH - 1, D_FF), h.dtype)
    else:
        pa_k, pa_v, pi_k, pb_k, pb_v, pool_prefix, conv_prefix = past
        ka_f = jnp.concatenate([pa_k, ka], axis=1)
        va_f = jnp.concatenate([pa_v, va], axis=1)
        ki_f = jnp.concatenate([pi_k, ki], axis=1)
        kb_f = jnp.concatenate([pb_k, kb], axis=1)
        vb_f = jnp.concatenate([pb_v, vb], axis=1)
    L = ka_f.shape[1]
    k_pos = jnp.arange(L, dtype=jnp.int32)
    topk = min(TOPK_MAX, L // 4)
    o_a = sweep_query_blocks(
        lambda qp, q_, qi_, wi_: dsa_block(qp, q_, qi_, wi_, ka_f, va_f, ki_f, k_pos, topk),
        pos, qa, qi, wi)
    o_b = sweep_query_blocks(
        lambda qp, q_: stick_breaking_block(qp, q_, kb_f, vb_f, k_pos), pos, qb)
    u_ext = jnp.concatenate([pool_prefix, u], axis=1)
    o_c = pool_mix(u_ext, pos, w_pool, pool_scale)
    mix = jnp.concatenate([o_a, o_b.reshape(B, T, WIDTH_B), o_c], axis=-1)
    h = h + mix @ w_out
    y_ffn, new_conv = conv_ffn(rmsnorm(h, g_ffn), conv_prefix, w_up, conv_w, conv_b, w_down)
    h = h + y_ffn
    h = h + jax.nn.sigmoid(rmsnorm(h, g_ple) @ w_ple_gate) * (p @ w_ple_proj)
    return h, (ka, va, ki, kb, vb, u_ext[:, -POOL_STATE:], new_conv)

def setup_inputs(seed: int = 0) -> dict:
    key = jax.random.key(seed)
    ks = jax.random.split(key, 32)
    n_pages = PAST_LEN // PAGE_SIZE
    n_pool = (DEC_BATCH * n_pages * 5) // 4

    def nrm(k, shape, s=1.0):
        return s * jax.random.normal(k, shape, jnp.float32)

    def gain(k, shape):
        return 1.0 + 0.05 * jax.random.normal(k, shape, jnp.float32)

    page_table = jax.random.permutation(ks[0], n_pool)[:DEC_BATCH * n_pages].reshape(DEC_BATCH, n_pages).astype(jnp.int32)
    return {
        'x_prompt': nrm(ks[1], (BATCH, SEQ, D_MODEL)),
        'x_sample': nrm(ks[2], (DEC_BATCH, DEC_SEQ, D_MODEL)),
        'cache_a_k': nrm(ks[3], (DEPTH, n_pool, PAGE_SIZE, N_KV_A, HEAD_DIM)),
        'cache_a_v': nrm(ks[4], (DEPTH, n_pool, PAGE_SIZE, N_KV_A, HEAD_DIM)),
        'cache_idx_k': nrm(ks[5], (DEPTH, n_pool, PAGE_SIZE, IDX_DIM)),
        'cache_b_k': nrm(ks[6], (DEPTH, n_pool, PAGE_SIZE, N_HEADS_B, HEAD_DIM)),
        'cache_b_v': nrm(ks[7], (DEPTH, n_pool, PAGE_SIZE, N_HEADS_B, HEAD_DIM)),
        'state_pool': nrm(ks[8], (DEPTH, DEC_BATCH, POOL_STATE, WIDTH_C)),
        'state_conv': nrm(ks[9], (DEPTH, DEC_BATCH, CONV_WIDTH - 1, D_FF)),
        'page_table': page_table,
        'p_prompt': nrm(ks[10], (DEPTH, BATCH, SEQ, PLE_DIM)),
        'p_sample': nrm(ks[11], (DEPTH, DEC_BATCH, DEC_SEQ, PLE_DIM)),
        'g_attn': gain(ks[12], (DEPTH, D_MODEL)),
        'w_in': nrm(ks[13], (DEPTH, D_MODEL, IN_WIDTH), D_MODEL ** -0.5),
        'g_q_a': gain(ks[14], (DEPTH, HEAD_DIM)),
        'g_k_a': gain(ks[15], (DEPTH, HEAD_DIM)),
        'w_pool': nrm(ks[16], (DEPTH, N_POOL_GROUPS, POOL_GROUP_DIM, POOL_GROUP_DIM), POOL_GROUP_DIM ** -0.5),
        'pool_scale': gain(ks[17], (DEPTH, WIDTH_C)),
        'w_out': nrm(ks[18], (DEPTH, MIX_WIDTH, D_MODEL), MIX_WIDTH ** -0.5),
        'g_ffn': gain(ks[19], (DEPTH, D_MODEL)),
        'w_up': nrm(ks[20], (DEPTH, D_MODEL, 2 * D_FF), D_MODEL ** -0.5),
        'conv_w': nrm(ks[21], (DEPTH, CONV_WIDTH, D_FF), CONV_WIDTH ** -0.5),
        'conv_b': nrm(ks[22], (DEPTH, D_FF), 0.02),
        'w_down': nrm(ks[23], (DEPTH, D_FF, D_MODEL), D_FF ** -0.5),
        'g_ple': gain(ks[24], (DEPTH, D_MODEL)),
        'w_ple_gate': nrm(ks[25], (DEPTH, D_MODEL, D_MODEL), D_MODEL ** -0.5),
        'w_ple_proj': nrm(ks[26], (DEPTH, PLE_DIM, D_MODEL), PLE_DIM ** -0.5),
    }

def reference(x_prompt, x_sample, cache_a_k, cache_a_v, cache_idx_k, cache_b_k, cache_b_v,
              state_pool, state_conv, page_table, p_prompt, p_sample,
              g_attn, w_in, g_q_a, g_k_a, w_pool, pool_scale, w_out,
              g_ffn, w_up, conv_w, conv_b, w_down, g_ple, w_ple_gate, w_ple_proj):
    h_p = x_prompt
    h_s = x_sample
    rows_p = []
    rows_s = []
    for l in range(DEPTH):
        weights = (g_attn[l], w_in[l], g_q_a[l], g_k_a[l], w_pool[l], pool_scale[l], w_out[l],
                   g_ffn[l], w_up[l], conv_w[l], conv_b[l], w_down[l], g_ple[l], w_ple_gate[l], w_ple_proj[l])
        h_p, st_p = trunk_layer(h_p, p_prompt[l], 0, None, weights)
        past = (gather_pages(cache_a_k[l], page_table), gather_pages(cache_a_v[l], page_table),
                gather_pages(cache_idx_k[l], page_table), gather_pages(cache_b_k[l], page_table),
                gather_pages(cache_b_v[l], page_table), state_pool[l], state_conv[l])
        h_s, st_s = trunk_layer(h_s, p_sample[l], PAST_LEN, past, weights)
        rows_p.append(st_p)
        rows_s.append(st_s)

    def stack(rows, i):
        return jnp.stack([r[i] for r in rows], axis=0)

    a_k_p, a_v_p, idx_k_p = stack(rows_p, 0), stack(rows_p, 1), stack(rows_p, 2)
    b_k_p, b_v_p = stack(rows_p, 3), stack(rows_p, 4)
    pool_p, conv_p = stack(rows_p, 5), stack(rows_p, 6)
    a_k_s, a_v_s, idx_k_s = stack(rows_s, 0), stack(rows_s, 1), stack(rows_s, 2)
    b_k_s, b_v_s = stack(rows_s, 3), stack(rows_s, 4)
    pool_s, conv_s = stack(rows_s, 5), stack(rows_s, 6)
    return (h_p, h_s, a_k_p, a_v_p, idx_k_p, b_k_p, b_v_p, pool_p, conv_p,
            a_k_s, a_v_s, idx_k_s, b_k_s, b_v_s, pool_s, conv_s)


_drawn_inputs = setup_inputs


def setup_inputs(seed=0):
    import zlib

    import numpy as np

    out = dict(_drawn_inputs(seed))
    spreads = {}
    factors = {'g_q_a': 5.397, 'conv_b': 4.114, 'g_ple': 4.206}
    for name, (base, spread) in spreads.items():
        noise = np.random.default_rng([zlib.crc32(name.encode()), seed]).standard_normal(out[name].shape)
        drawn = base * np.exp(spread * noise) if base else spread * noise
        out[name] = __import__('jax').numpy.asarray(drawn.astype(out[name].dtype))
    for name, factor in factors.items():
        out[name] = (out[name] * factor).astype(out[name].dtype)
    return out
```

```python
from contextlib import ExitStack

import concourse.bass as bass
import numpy as np
from concourse import mybir

F32 = mybir.dt.float32
F32R = mybir.dt.float32r
BF16 = mybir.dt.bfloat16
I32 = mybir.dt.int32
ALU = mybir.AluOpType
ACT = mybir.ActivationFunctionType
AX = mybir.AxisListType

P = 128
D = 1024
KD = D // P
LAYERS = 2
TP = 512
NB = 8
NS = 4
TS = NB * NS
T = TP + TS
HALF = T // 2
PAST = 256
PAGE = 128
NPAGES = NB * PAST // PAGE
NPOOL = NPAGES * 5 // 4
HD = 64
DFF = 2816
KF = DFF // P
PLE = 256
EPS = 1e-6
TOKW = [P, P, P, P, TS]
TILES = len(TOKW)

CHUNK = [(0, 512), (512, 964), (964, 1348), (1348, 1732), (1732, 2116)]
U0 = 2116

UNIT = 1024
U_IN, U_U, U_OUT, U_UP, U_DOWN, U_PROJ, U_GATE = 0, 20, 22, 30, 74, 98, 100
UNITS = 108
RAW, SPLIT = 4, 2
DOWN_K = [8, 8, 6]

TOPK_P, TOPK_S = 128, 65
MASKED = -3.0e38
TAKEN = -3.4e38
CUT = -3.2e38
PADDED = -3.1e38
NEG = -1.0e30
KEYS_S = PAST + TS
ROUNDS = TOPK_P // 8

GROUP_K = (2, 3, 5, 6, 7)

C_ID, C_NTRI, C_NONE, C_ONE, C_M01, C_BB, C_BA, C_INVW, C_INV16, C_EPS, C_1 = 0, 128, 256, 384, 512, 640, 768, 896, 898, 930, 931
NC = 932
ACT_STEPS, DVE_STEPS = 26, 198
D_COS, D_SIN, D_MA, D_MB, D_BB = 0, 320, 640, 928, 1120
ND = 1152
V_ATTN, V_FFN, V_PLE, V_CW, V_CB, V_PS = 0, 8, 16, 24, 90, 112
NV = 114
F_QA, F_KA, F_QI, F_KI, F_QB, F_KB = 0, 3, 4, 6, 7, 10
CH_BLOCKS = [(F_QA, 4), (F_QI, 3), (F_QB, 3), (F_KB, 3)]


def shape_constants():
    p, c = np.arange(P)[:, None], np.arange(P)[None, :]
    a = np.zeros((P, NC), np.float32)
    a[:, C_ID:C_ID + P] = p == c
    a[:, C_NTRI:C_NTRI + P] = -(p >= c).astype(np.float32)
    a[:, C_NONE:C_NONE + P] = -1.0
    a[:, C_ONE:C_ONE + P] = 1.0
    a[:, C_M01:C_M01 + P] = p < c
    a[:, C_BB:C_BB + P] = np.where(p < c, 0.0, NEG)
    a[:, C_BA:C_BA + P] = np.where(c <= p, 0.0, NEG)
    for m in range(2):
        for half in range(2):
            w = 2 ** (2 * m + half + 1)
            r = slice(64 * half, 64 * half + 64)
            a[r, C_INVW + m] = 1.0 / w
            a[r, C_INV16 + 16 * m:C_INV16 + 16 * m + 16] = 1.0 / np.minimum(w, np.arange(16) + 1)
    a[:, C_EPS] = EPS
    a[:, C_1] = 1.0
    d = np.zeros((P, ND), np.float32)
    inv = (np.float32(10000.0) ** (-np.arange(32, dtype=np.float32) / np.float32(32))).astype(np.float32)
    for t in range(TILES):
        pos = t * P + np.arange(P) if t < 4 else PAST + np.arange(P) % NS
        ang = (pos.astype(np.float32)[:, None] * inv[None]).astype(np.float32)
        cs, sn = np.cos(ang), np.sin(ang)
        d[:, D_COS + 64 * t:D_COS + 64 * t + 64] = np.concatenate([cs, cs], 1)
        d[:, D_SIN + 64 * t:D_SIN + 64 * t + 64] = np.concatenate([-sn, sn], 1)
    q = np.arange(TS)
    same = q[:, None] // NS == q[None] // NS
    qt, kt = q[:, None] % NS, q[None] % NS
    d[:TS, D_MA + PAST:D_MA + KEYS_S] = np.where(same & (kt <= qt), 0.0, MASKED)
    strict = (same & (qt < kt)).astype(np.float32)
    for h in range(6):
        d[:TS, D_MB + TS * h:D_MB + TS * h + TS] = strict
    d[:TS, D_BB:D_BB + TS] = np.where(strict > 0, 0.0, NEG)
    return a, d


class Steps:

    def __init__(self, layer, per_layer):
        self.n, self.base = 0, layer * per_layer

    def step(self):
        self.n += 1
        return 1

    def value(self, n=None):
        return self.base + (self.n if n is None else n)


def build(nc, t_in, t_out):
    ctx = ExitStack()
    with ctx:
        def sb(name, shape, dt=F32, where=None):
            return (where or ctx).enter_context(nc.sbuf_tensor(name, shape, dt))

        hT = sb("hT", [P, KD, T])
        aH = sb("aH", [P, KD, T], F32R)
        aL = sb("aL", [P, KD, T], F32R)
        w_raw = [sb(f"w_raw{i}", [P, UNIT]) for i in range(RAW)]
        w_H = [sb(f"w_H{i}", [P, UNIT], F32R) for i in range(SPLIT)]
        w_L = [sb(f"w_L{i}", [P, UNIT], F32R) for i in range(SPLIT)]
        con = sb("con", [P, NC])
        con_bf = sb("con_bf", [P, 3, P], BF16)
        id3_bf = sb("id3_bf", [TS, 3 * TS], BF16)
        pages = sb("pages", [1, NPAGES], I32)
        vecT = sb("vecT", [P, NV])
        vec_raw = sb("vec_raw", [P, P])
        a_tmp = sb("a_tmp", [P, 2, T])
        r_all = sb("r_all", [P, T])

        att = ExitStack()
        featT = sb("featT", [P, 13, T], F32, att)
        V = sb("V", [P, TILES, 512], F32, att)
        dcon = sb("dcon", [P, ND], F32, att)
        wi = sb("wi", [P, TILES, 4], F32, att)
        part = ExitStack()
        score = sb("score", [P, 2, TP], F32, part)
        relu_s = sb("relu_s", [P, 2, TP], F32, part)
        bias_p = sb("bias_p", [P, 3, TP], BF16, part)
        prob = sb("prob", [P, 2, TP], F32, part)
        probT = sb("probT", [P, 4, 3, P], F32, part)
        stat = sb("stat", [P, 2, 4], F32, part)
        m8 = sb("m8", [P, 8], F32, part)
        u_p = sb("u_p", [P, 2, 15 + TP], F32, part)
        u_s = sb("u_s", [P, 2, NB, 15 + NS], F32, part)
        first16 = sb("first16", [P, 16], F32, part)
        u_c = sb("u_c", [P, 2, NB * 15], F32, part)
        pw = [sb(f"pw{i}", [P, 15 + TP + NB * 19], F32, part) for i in range(2)]
        pooled = sb("pooled", [P, 2, T], F32, part)
        w_pool = sb("w_pool", [P, 2, HD], F32, part)
        pst_tok = sb("pst_tok", [P, 2 * P], F32, part)
        u_tok = sb("u_tok", [P, 512], F32, part)
        stage = ExitStack()
        x_tok = sb("x_tok", [P, TILES, 512], F32, stage)
        r_tok = sb("r_tok", [P, TILES, 512], F32, stage)
        t1 = sb("t1", [P, 512], F32, stage)
        t2 = sb("t2", [P, 512], F32, stage)
        gains = sb("gains", [P, 2, HD], F32, stage)
        hstat = sb("hstat", [P, TILES, 8], F32, stage)
        stage.close()
        stick = ExitStack()
        LW = 1280
        Lb = sb("Lb", [P, 2, LW], F32, stick)
        Ab = sb("Ab", [P, LW], F32, stick)
        stick.close()
        part.close()
        dec = ExitStack()
        KP = sb("KP", [P, 3, 576], F32, dec)
        KT = sb("KT", [P, 2, 640], F32, dec)
        VP = sb("VP", [P, 3, 512], F32, dec)
        qim = sb("qim", [HD, NB, P], F32, dec)
        qam = sb("qam", [P, NB, 96], F32, dec)
        qbm = sb("qbm", [P, 3, 2, TS], F32, dec)
        wic = sb("wic", [P, 1], F32, dec)
        rel_d = sb("rel_d", [P, KEYS_S], F32, dec)
        sco_d = sb("sco_d", [TS, KEYS_S + 8], F32, dec)
        m8d = sb("m8d", [TS, 16], F32, dec)
        bias_d = sb("bias_d", [TS, KEYS_S], BF16, dec)
        P_d = sb("P_d", [96, 2, KEYS_S], F32, dec)
        st_d = sb("st_d", [96, 2, 4], F32, dec)
        PT_d = sb("PT_d", [P, 2, 3, 96], F32, dec)
        L_d = sb("L_d", [P, 384], F32, dec)
        L_n = sb("L_n", [TS, 192], F32, dec)
        A_d = sb("A_d", [P, 384], F32, dec)
        A_n = sb("A_n", [TS, 192], F32, dec)
        bb_n = sb("bb_n", [TS, TS], BF16, dec)
        dec.close()
        att.close()
        ffn = ExitStack()
        stT = sb("stT", [P, KF, 2 * NB], F32, ffn)
        keepT = sb("keepT", [P, KF, 2 + 2 * NB], F32, ffn)
        GW = 2 + TP + 6 * NB
        G = sb("G", [P, 2, GW], F32, ffn)
        Cv = sb("Cv", [P, 2, GW - 2], F32, ffn)
        acts = ExitStack()
        actH = sb("actH", [P, KF, T], F32R, acts)
        actL = sb("actL", [P, KF, T], F32R, acts)
        acts.close()
        st_tok = sb("st_tok", [2 * NB, DFF], F32, ffn)
        ffn.close()
        ple = ExitStack()
        sb("ple_skip", [P, KF * (2 + 4 * NB) + 2 * GW + 2 * (GW - 2)], F32, ple)
        p_tok = sb("p_tok", [P, TILES, PLE], F32, ple)
        pH = sb("pH", [P, 2, T], F32R, ple)
        pL = sb("pL", [P, 2, T], F32R, ple)
        projT = sb("projT", [P, KD, T], F32, ple)
        sig = sb("sig", [P, 2, T], F32, ple)
        keep_tok = sb("keep_tok", [2 + 2 * NB, DFF], F32, ple)
        ple.close()
        edge = ExitStack()
        xy = sb("xy", [P, 5, D], F32, edge)
        edge.close()
        ps = ctx.enter_context(nc.psum_tensor("ps", [P, 8, 512], F32))

        per_layer = {}

        def sg(name, per=1):
            s = ctx.enter_context(nc.semaphore(name))
            per_layer[s.name] = per
            return s

        con_ld, x_ld, page_ld, con_cast = sg("con_ld"), sg("x_ld"), sg("page_ld"), sg("con_cast")
        emb_tr, y_tr, y_ev, y_out = sg("emb_tr"), sg("y_tr"), sg("y_ev"), sg("y_out")
        emb_ev = sg("emb_ev")
        unit_dmas = [3 if U_OUT <= u < U_UP else 1 for u in range(UNITS)]
        w_ld = [sg(f"w_ld{s}", 16 * sum(unit_dmas[s::RAW])) for s in range(RAW)]
        w_hi, w_lo, w_used = sg("w_hi", UNITS), sg("w_lo", UNITS), sg("w_used", UNITS)
        vec_ld, vec_tr, vec_ev = sg("vec_ld", 6 * 16), sg("vec_tr", 1), sg("vec_ev", 1)
        lay_ld = sg("lay_ld", 6 * 16)
        h_new = sg("h_new", 24)
        n_sq, n_ss, n_std, n_rec = sg("n_sq", 24), sg("n_ss", 24), sg("n_std", 3), sg("n_rec", 3)
        a_t, a_hi, a_lo = sg("a_t", 24), sg("a_hi", 24), sg("a_lo", 24)
        p_mm, p_ev = sg("p_mm", 20), sg("p_ev", 15)
        rope_ok, plain_ok = sg("rope_ok", 10), sg("plain_ok", 10)
        hs_one = sg("hs_one", 1)
        hs_ss, hs_std = sg("hs_ss", 1), sg("hs_std", 1)
        t_mm, t_ev = sg("t_mm", 20), sg("t_ev", 20)
        ak_out, ix_out, bk_out, kv_out = sg("ak_out", 80), sg("ix_out", 80), sg("bk_out", 80), sg("kv_out", 160)
        u_ev = sg("u_ev", 2)
        ph_tr, ph_ev, u_zero = sg("ph_tr", 1), sg("ph_ev", 1), sg("u_zero", 1)
        u_cp = sg("u_cp", 1)
        uo_tr, uo_ev, uo_out = sg("uo_tr", 1), sg("uo_ev", 1), sg("uo_out", 32)
        pooled_ok, y_mm, y_hi, y_lo = sg("pooled_ok", 2), sg("y_mm", 2), sg("y_hi", 2), sg("y_lo", 2)
        b_z, b_min, b_ln, b_max, b_diag = sg("b_z", 6), sg("b_min", 24), sg("b_ln", 24), sg("b_max", 24), sg("b_diag", 24)
        b_tri, b_exp, b_o, b_hi, b_lo = sg("b_tri", 6), sg("b_exp", 24), sg("b_o", 6), sg("b_hi", 6), sg("b_lo", 6)
        i_mm, i_relu, i_sc, i_diag, sel_ok = sg("i_mm", 12), sg("i_relu", 12), sg("i_sc", 12), sg("i_diag", 3), sg("sel_ok", 3)
        q_mm, q_max, q_exp, q_rec, q_norm = sg("q_mm", 24), sg("q_max", 24), sg("q_exp", 24), sg("q_rec", 24), sg("q_norm", 24)
        pt_mm, pt_ev, o_mm, o_hi, o_lo = sg("pt_mm", 24), sg("pt_ev", 24), sg("o_mm", 8), sg("o_hi", 8), sg("o_lo", 8)
        d_zero, d_q = sg("d_zero", 1), sg("d_q", 1)
        kp_ld = [sg(f"kp_ld{s}", 48 * len(range(s, NPAGES, 3))) for s in range(3)]
        vp_ld = [sg(f"vp_ld{s}", 32 * len(range(s, NPAGES, 3))) for s in range(3)]
        kt_mm, kt_ev, kq_mm = sg("kt_mm", NPAGES), sg("kt_ev", NPAGES), sg("kq_mm", NPAGES)
        d_new, d_relu, d_rel, d_sum, d_bias = sg("d_new", 1), sg("d_relu", 1), sg("d_rel", 1), sg("d_sum", 1), sg("d_bias", 1)
        d_log, d_max, d_exp, d_nrm, d_ptm, d_pte = sg("d_log", 1), sg("d_max", 2), sg("d_exp", 2), sg("d_nrm", 2), sg("d_ptm", 1), sg("d_pte", 1)
        d_min, d_ln, d_sp, d_tri, d_A = sg("d_min", 1), sg("d_ln", 1), sg("d_sp", 1), sg("d_tri", 1), sg("d_A", 1)
        vp_use, d_hi, d_lo = sg("vp_use", NPAGES), sg("d_hi", 2), sg("d_lo", 2)
        st_ld, st_tr, st_ev, g_zero = sg("st_ld", 16), sg("st_tr", 1), sg("st_ev", 1), sg("g_zero", 1)
        g_ev, g_pre, c_1, c_2, c_3 = sg("g_ev", KF), sg("g_pre", KF), sg("c_1", KF), sg("c_2", KF), sg("c_3", KF)
        s_g, s_mul = sg("s_g", KF), sg("s_mul", KF)
        v_mul, f_hi, f_lo, g_keep = sg("v_mul", KF), sg("f_hi", KF), sg("f_lo", KF), sg("g_keep", KF)
        p_ld, pp_tr, pp_hi, pp_lo = sg("p_ld", 32), sg("pp_tr", 1), sg("pp_hi", 3), sg("pp_lo", 3)
        pr_mm, pr_ev, gt_sig = sg("pr_mm", 6), sg("pr_ev", 8), sg("gt_sig", 8)
        kp_tr, kp_ev, kp_out = sg("kp_tr", 6), sg("kp_ev", 6), sg("kp_out", 32)
        dve_step, act_step = sg("dve_step", 0), sg("act_step", 0)

        held = sg("held", 0)

        ident = con[:, C_ID:C_ID + P]
        ntri, nones, ones = con[:, C_NTRI:C_NTRI + P], con[:, C_NONE:C_NONE + P], con[:, C_ONE:C_ONE + P]
        eps, one = con[:, C_EPS:C_EPS + 1], con[:, C_1:C_1 + 1]
        id_bf, bb_bf, ba_bf = con_bf[:, 0, :], con_bf[:, 1, :], con_bf[:, 2, :]

        def hold(eng):
            eng.sem_inc(held, 1)

        U_BANK = [(4, 5), (6, 0)]

        def act_at(of, f):
            return of[:, bass.ds(f, 1), :].rearrange("p o n -> p (o n)")

        def halves(ap2):
            return ap2.rearrange("p (h n) -> p h n", h=2)

        def psh(b):
            return ps[:, b:b + 2, 0:HALF]

        def vec(row):
            return vecT[:, row:row + 1]

        def vec_at(row, f):
            return vecT[:, bass.ds(f + row, 1)]

        def ld_value(u):
            return 16 * sum(unit_dmas[u % RAW:u + 1:RAW])

        def unit_cols(u):
            if u < U_U:
                a, b = CHUNK[u // 4]
                return [(0, b - a), (512, 512 + b - a)]
            if U_DOWN <= u < U_PROJ and (u - U_DOWN) % 3 == 2:
                return [(0, DOWN_K[2] * P)]
            return [(0, UNIT)]

        BN = [TP - P * i for i in range(4)]
        BOFF = [0, 512, 896, 1152]
        BPS = [(0, 0), (1, 0), (2, 0), (1, 384)]

        def bz(h, i, c0=0, n=None):
            b, o = BPS[i]
            n = BN[i] - c0 if n is None else n
            return ps[:, 3 * (h % 2) + b, o + c0:o + c0 + n]

        block = ctx.enter_context(nc.Block())
        @block.sync
        def _(sp):
            sp.dma_start(con[:], t_in["con"]).then_inc(con_ld, 16)
            sp.dma_start(pages[:], t_in["page_table"].rearrange("b n -> (b n)").rearrange("(o n) -> o n", o=1)).then_inc(page_ld, 16)
            sp.dma_start(xy[:, 0:4, :], t_in["x_prompt"].rearrange("o (t p) d -> p (o t) d", p=P)).then_inc(x_ld, 16)
            sp.dma_start(xy[0:TS, 4, :], t_in["x_sample"].rearrange("b s d -> (b s) d")).then_inc(x_ld, 16)
            sp.wait_ge(page_ld, 16)
            with sp.Fori(0, LAYERS) as l:
                L = bass.ds(l, 1)

                def at(s, n):
                    return l * per_layer[s.name] + n

                def load_unit(u, i=0, per_turn=0):
                    sp.wait_ge(w_lo, at(w_lo, u + i * per_turn + 1))
                    hold(sp)
                    slot, raw = u % RAW, w_raw[u % RAW]
                    k8 = raw[:, :].rearrange("p (k n) -> p k n", k=8)
                    if u < U_U:
                        a, b = CHUNK[u // 4]
                        src = [(raw[:, :].rearrange("p (k n) -> p k n", k=2)[:, :, 0:b - a],
                                t_in["w_in"][L, 2 * P * (u % 4):2 * P * (u % 4 + 1), a:b].rearrange("o (k p) n -> p (o k) n", p=P))]
                    elif u < U_OUT:
                        c = U0 + P * (u - U_U)
                        src = [(k8, t_in["w_in"][L, :, c:c + P].rearrange("o (k p) n -> p (o k) n", p=P))]
                    elif u < U_UP:
                        m = u - U_OUT
                        w = t_in["w_out"][L, :, m * P:m * P + P]
                        src = [(k8[HD * n:HD * n + HD, 0:3, :],
                                w[:, 3 * HD * n:3 * HD * (n + 1), :].rearrange("o (j p) n -> p (o j) n", p=HD)) for n in range(2)]
                        src.append((k8[:, 3:8, :], w[:, 3 * P:, :].rearrange("o (k p) n -> p (o k) n", p=P)))
                    elif u < U_DOWN:
                        f2, val = (u - U_UP) // 2, (u - U_UP) % 2
                        cols = bass.ds(i * (P * per_turn // 2) + (f2 * P + val * DFF), P)
                        src = [(k8, t_in["w_up"][L, :, cols].rearrange("o (k p) n -> p (o k) n", p=P))]
                    elif u < U_PROJ:
                        m, part_ = divmod(u - U_DOWN, 3)
                        nk = DOWN_K[part_]
                        cols = bass.ds(i * (P * per_turn // 3) + m * P, P)
                        src = [(k8[:, 0:nk, :], t_in["w_down"][L, D * part_:D * part_ + nk * P, cols].rearrange("o (k p) n -> p (o k) n", p=P))]
                    elif u < U_GATE:
                        q = u - U_PROJ
                        src = [(raw[:, :].rearrange("p (k n) -> p k n", k=2),
                                t_in["w_ple_proj"][L, :, 512 * q:512 * q + 512].rearrange("o (k p) n -> p (o k) n", p=P))]
                    else:
                        cols = slice(P * (u - U_GATE), P * (u - U_GATE) + P)
                        src = [(k8, t_in["w_ple_gate"][L, :, cols].rearrange("o (k p) n -> p (o k) n", p=P))]
                    assert len(src) == unit_dmas[u]
                    for to, of in src:
                        sp.dma_start(to, of).then_inc(w_ld[slot], 16)

                sp.wait_ge(w_lo, at(w_lo, 1))
                hold(sp)
                for name, row, n in (("g_attn", V_ATTN, KD), ("g_ffn", V_FFN, KD), ("g_ple", V_PLE, KD),
                                     ("conv_b", V_CB, KF), ("pool_scale", V_PS, 2)):
                    sp.dma_start(vec_raw[row:row + n, :], t_in[name][L, :].rearrange("o (k p) -> (o k) p", p=P)).then_inc(vec_ld, 16)
                sp.dma_start(vec_raw[V_CW:V_CW + 3 * KF, :], t_in["conv_w"][L, :, :].rearrange("o j (k p) -> (o j k) p", p=P)).then_inc(vec_ld, 16)
                for u in range(RAW):
                    load_unit(u)
                sp.wait_ge(h_new, at(h_new, KD))
                sp.dma_start(dcon[:], t_in["dcon"]).then_inc(lay_ld, 16)
                sp.dma_start(gains[:, 0, :], t_in["g_q_a"][L, :].rearrange("o d -> (o d)").partition_broadcast(P)).then_inc(lay_ld, 16)
                sp.dma_start(gains[:, 1, :], t_in["g_k_a"][L, :].rearrange("o d -> (o d)").partition_broadcast(P)).then_inc(lay_ld, 16)
                for m in range(2):
                    sp.dma_start(w_pool[:, m, :], t_in["w_pool"][L, 2 * m:2 * m + 2].rearrange("o h c d -> (o h c) d")).then_inc(lay_ld, 16)
                sp.dma_start(pst_tok[0:NB * 15, :], t_in["state_pool"][L].rearrange("o b r c -> (o b r) c")).then_inc(lay_ld, 16)
                for u in range(RAW, U_OUT + RAW):
                    load_unit(u)
                sp.wait_ge(y_hi, at(y_hi, 2))
                hold(sp)
                sp.wait_ge(y_lo, at(y_lo, 2))
                hold(sp)
                sp.wait_ge(uo_out, at(uo_out, 32))
                hold(sp)
                for pg in range(NPAGES):
                    if pg >= 3:
                        sp.wait_ge(kt_mm, at(kt_mm, pg - 2))
                        hold(sp)
                    r = sp.value_load(pages[0:1, pg:pg + 1], min_val=0, max_val=NPOOL - 1)
                    R = bass.ds(r, 1)
                    to = KP[:, pg % 3, :]
                    sp.dma_start(to[:, 0:128], t_in["cache_a_k"][L, R].rearrange("o a p n d -> (o a p) (n d)")).then_inc(kp_ld[pg % 3], 16)
                    sp.dma_start(to[:, 128:512], t_in["cache_b_k"][L, R].rearrange("o a p n d -> (o a p) (n d)")).then_inc(kp_ld[pg % 3], 16)
                    sp.dma_start(to[:, 512:576], t_in["cache_idx_k"][L, R].rearrange("o a p d -> (o a p) d")).then_inc(kp_ld[pg % 3], 16)
                for pg in range(NPAGES):
                    if pg >= 3:
                        sp.wait_ge(vp_use, at(vp_use, pg - 2))
                        hold(sp)
                    r = sp.value_load(pages[0:1, pg:pg + 1], min_val=0, max_val=NPOOL - 1)
                    R = bass.ds(r, 1)
                    to = VP[:, pg % 3, :]
                    sp.dma_start(to[:, 0:128], t_in["cache_a_v"][L, R].rearrange("o a p n d -> (o a p) (n d)")).then_inc(vp_ld[pg % 3], 16)
                    sp.dma_start(to[:, 128:512], t_in["cache_b_v"][L, R].rearrange("o a p n d -> (o a p) (n d)")).then_inc(vp_ld[pg % 3], 16)
                sp.wait_ge(d_hi, at(d_hi, 2))
                hold(sp)
                sp.wait_ge(d_lo, at(d_lo, 2))
                hold(sp)
                sp.dma_start(st_tok[:], t_in["state_conv"][L].rearrange("o b r c -> (o b r) c")).then_inc(st_ld, 16)
                for u in range(U_OUT + RAW, U_UP):
                    load_unit(u)
                with sp.Fori(0, KF // 2) as i:
                    for j in range(4):
                        load_unit(U_UP + j, i, 4)
                with sp.Fori(0, 2) as i:
                    for j in range(12):
                        load_unit(U_DOWN + j, i, 12)
                for u in range(U_PROJ, U_PROJ + RAW):
                    load_unit(u)
                sp.wait_ge(w_used, at(w_used, SPLIT + U_PROJ))
                hold(sp)
                sp.dma_start(p_tok[:, 0:4, :], t_in["p_prompt"][L].rearrange("o b (t p) c -> p (o b t) c", p=P)).then_inc(p_ld, 16)
                sp.dma_start(p_tok[0:TS, 4, :], t_in["p_sample"][L].rearrange("o b s c -> (o b s) c")).then_inc(p_ld, 16)
                for u in range(U_PROJ + RAW, UNITS):
                    load_unit(u)
                sp.wait_ge(kp_out, at(kp_out, 32))
                hold(sp)
                sp.wait_ge(kv_out, at(kv_out, 10 * 16))
                hold(sp)
            for t in range(TILES):
                sp.wait_ge(y_ev, 2 * t + 2)
                if t < 4:
                    sp.dma_start(t_out["y_prompt"][0, P * t:P * t + P, :], xy[:, t, :]).then_inc(y_out, 16)
                else:
                    sp.dma_start(t_out["y_sample"].rearrange("b s d -> (b s) d"), xy[0:TS, 4, :]).then_inc(y_out, 16)
            sp.wait_ge(y_out, 16 * TILES)

        @block.gpsimd
        def _(pool):
            with pool.Fori(0, LAYERS) as l:
                L = bass.ds(l, 1)

                def at(s, n):
                    return l * per_layer[s.name] + n

                def store(name, t, inner, src, landed):
                    if t < 4:
                        to = t_out[name + "_p"][L, 0, P * t:P * t + P].rearrange(f"o p {inner} -> (o p) {'(n d)' if inner == 'n d' else 'd'}")
                    else:
                        to = t_out[name + "_s"][L].rearrange(f"o b s {inner} -> (o b s) {'(n d)' if inner == 'n d' else 'd'}")
                    pool.dma_start(to, src[0:TOKW[t]]).then_inc(landed, 16)

                pool.wait_ge(h_new, at(h_new, KD))
                hold(pool)
                pool.memset(u_p[:, :, 0:15], 0.0).then_inc(u_zero, 1)
                for t in range(TILES):
                    pool.wait_ge(rope_ok, at(rope_ok, t + 1))
                    hold(pool)
                    store("a_k", t, "n d", r_tok[:, t, 384:512], ak_out)
                for t in range(TILES):
                    pool.wait_ge(p_ev, at(p_ev, 5 + t + 1))
                    hold(pool)
                    store("a_v", t, "n d", V[:, t, 0:128], kv_out)
                    pool.wait_ge(rope_ok, at(rope_ok, 5 + t + 1))
                    hold(pool)
                    store("idx_k", t, "d", r_tok[:, t, 256:320], ix_out)
                for t in range(TILES):
                    pool.wait_ge(plain_ok, at(plain_ok, 5 + t + 1))
                    hold(pool)
                    store("b_k", t, "n d", r_tok[:, t, 0:384], bk_out)
                for t in range(TILES):
                    pool.wait_ge(p_ev, at(p_ev, 10 + t + 1))
                    hold(pool)
                    store("b_v", t, "n d", V[:, t, 128:512], kv_out)
                pool.wait_ge(uo_ev, at(uo_ev, 1))
                hold(pool)
                pool.dma_start(t_out["pool_s"][L].rearrange("o b r c -> (o b r) c"), u_tok[0:NB * 15, 0:256]).then_inc(uo_out, 16)
                pool.dma_start(t_out["pool_p"][L, 0].rearrange("o r c -> (o r) c"), u_tok[0:15, 256:512]).then_inc(uo_out, 16)

                def causal(t):
                    pool.wait_ge(i_sc, at(i_sc, 4 * t))
                    hold(pool)
                    blk = score[:, (t - 1) % 2, P * t:P * t + P]
                    pool.affine_select(out=blk, in_=blk, compare_op=ALU.is_ge, fill=MASKED, base=0,
                                       pattern=[[-1, P]], channel_multiplier=1).then_inc(i_diag, 1)

                def diag(h):
                    for i in range(4):
                        pool.wait_ge(b_max, at(b_max, 4 * h + i + 1))
                        hold(pool)
                        blk = Lb[:, h % 2, BOFF[i]:BOFF[i] + P]
                        pool.tensor_tensor(blk, blk, con[:, C_M01:C_M01 + P], ALU.mult).then_inc(b_diag, 1)

                causal(1)
                diag(0)
                diag(1)
                for h in range(6):
                    if h + 2 < 6:
                        diag(h + 2)
                    if h in (1, 3):
                        causal(2 + h // 2)
                for m in range(24):
                    t = m // 6
                    pool.wait_ge(q_rec, at(q_rec, m + 1))
                    hold(pool)
                    pr = prob[:, m % 2, 0:P * (t + 1)]
                    pool.tensor_scalar(pr, pr, stat[:, m % 2, 3:4], None, ALU.mult).then_inc(q_norm, 1)

                pool.wait_ge(y_hi, at(y_hi, 2))
                hold(pool)
                pool.wait_ge(y_lo, at(y_lo, 2))
                hold(pool)
                pool.wait_ge(uo_out, at(uo_out, 32))
                hold(pool)
                pool.memset(qim[:], 0.0)
                pool.memset(qbm[:], 0.0)
                pool.memset(qam[:], 0.0).then_inc(d_zero, 1)
                pool.wait_ge(d_hi, at(d_hi, 2))
                hold(pool)
                pool.wait_ge(d_lo, at(d_lo, 2))
                hold(pool)
                pool.memset(G[:, :, 0:2], 0.0).then_inc(g_zero, 1)
                pool.wait_ge(st_ev, at(st_ev, 1))
                hold(pool)

                with pool.Fori(0, KF // 2) as i:
                    for slot in range(2):
                        f = 2 * i + slot
                        g_s = G[:, slot, 2 + TP:].rearrange("p (b s) -> p b s", s=6)
                        pool.wait_ge(v_mul, at(v_mul, f + 1))
                        hold(pool)
                        pool.tensor_copy(g_s[:, :, 0:2], stT[:, bass.ds(f, 1), :].rearrange("p o (b s) -> p (o b) s", s=2)).then_inc(g_pre, 1)
                        pool.wait_ge(g_ev, at(g_ev, f + 1))
                        hold(pool)
                        kf = keepT[:, bass.ds(f, 1), :].rearrange("p o n -> p (o n)")
                        pool.tensor_copy(kf[:, 0:2], G[:, slot, TP:TP + 2])
                        pool.tensor_copy(kf[:, 2:18].rearrange("p (b s) -> p b s", s=2), g_s[:, :, 4:6]).then_inc(g_keep, 1)
                pool.wait_ge(kp_ev, at(kp_ev, 6))
                hold(pool)
                pool.dma_start(t_out["conv_p"][L, 0].rearrange("o r c -> (o r) c"), keep_tok[0:2, :]).then_inc(kp_out, 16)
                pool.dma_start(t_out["conv_s"][L].rearrange("o b r c -> (o b r) c"), keep_tok[2:18, :]).then_inc(kp_out, 16)
                pool.wait_ge(kv_out, at(kv_out, 10 * 16))
                hold(pool)
                pool.wait_ge(kp_out, at(kp_out, 32))
                hold(pool)

        @block.scalar
        def _(act):
            with act.Fori(0, LAYERS) as l:
                steps = Steps(l, ACT_STEPS)

                def at(s, n):
                    return l * per_layer[s.name] + n

                def copy(out, in_, scale=1.0):
                    return act.activation(out, in_, ACT.Copy, scale=scale)

                def split(u, i=0, per_turn=0):
                    n = u + i * per_turn
                    act.wait_ge(w_ld[u % RAW], at(w_ld[u % RAW], (per_turn // RAW * 16) * i + ld_value(u)))
                    act.wait_ge(w_used, at(w_used, n + 1))
                    cols = unit_cols(u)
                    for a, b in cols:
                        ins = copy(w_H[u % SPLIT][:, a:b], w_raw[u % RAW][:, a:b])
                    ins.then_inc(w_hi, 1)

                def norm(i):
                    for k in range(KD):
                        act.wait_ge(h_new, at(h_new, 8 * i + k + 1))
                        if k >= 2:
                            act.wait_ge(n_ss, at(n_ss, 8 * i + k - 1))
                        act.activation(a_tmp[:, k % 2, :], hT[:, k, :], ACT.Square).then_inc(n_sq, 1)
                    act.wait_ge(n_ss, at(n_ss, 8 * i + 8))
                    act.activation(halves(r_all[:, :]), psh(6), ACT.Sqrt, bias=eps, scale=1.0 / D).then_inc(n_std, 1)
                    for k in range(KD):
                        act.wait_ge(a_t, at(a_t, 8 * i + k + 1))
                        copy(aH[:, k, :], a_tmp[:, k % 2, :]).then_inc(a_hi, 1)

                act.wait_ge(vec_tr, at(vec_tr, 1))
                copy(vecT[:, :], ps[:, 0, 0:NV]).then_inc(vec_ev, 1)
                split(0)
                split(1)
                norm(0)

                for c in range(5):
                    for j in range(4):
                        u = 4 * c + j
                        if c >= 1:
                            for t in range(TILES):
                                if GROUP_K[t] // 2 != j:
                                    continue
                                g, n = 5 * (c - 1) + t, TOKW[t]
                                f0, nb = CH_BLOCKS[c - 1]
                                act.wait_ge(t_mm, at(t_mm, g + 1))
                                out = featT[:, f0:f0 + nb, P * t:P * t + n]
                                in_ = ps[:, 7, 0:nb * P].rearrange("p (b q) -> p b q", q=P)[:, :, 0:n]
                                copy(out, in_, 0.125 if c == 3 else 1.0).then_inc(t_ev, 1)
                        if j < 3:
                            split(u + 2)
                    width = CHUNK[c][1] - CHUNK[c][0]
                    for t in range(TILES):
                        i, n = 5 * c + t, TOKW[t]
                        if t < 4:
                            act.wait_ge(p_mm, at(p_mm, 4 * c + t + 1))
                        else:
                            act.wait_ge(w_used, at(w_used, 4 * c + 3 + SPLIT + 1))
                        src = ps[0:n, i % 7, :]
                        if c == 0:
                            copy(x_tok[0:n, t, :], src).then_inc(p_ev, 1)
                        elif c == 1:
                            act.wait_ge(rope_ok, at(rope_ok, t + 1))
                            copy(V[0:n, t, 0:128], src[:, 0:128])
                            copy(x_tok[0:n, t, 0:324], src[:, 128:452]).then_inc(p_ev, 1)
                        elif c == 2:
                            act.wait_ge(t_mm, at(t_mm, 5 + t + 1))
                            act.wait_ge(ix_out, at(ix_out, 5 * 16))
                            copy(r_tok[0:n, t, 0:384], src[:, 0:384]).then_inc(plain_ok, 1)
                        elif c == 3:
                            act.wait_ge(t_mm, at(t_mm, 10 + t + 1))
                            copy(r_tok[0:n, t, 0:384], src[:, 0:384]).then_inc(plain_ok, 1)
                        else:
                            copy(V[0:n, t, 128:512], src[:, 0:384]).then_inc(p_ev, 1)
                    split(4 * c + 5)
                    if c == 0:
                        act.wait_ge(hs_ss, at(hs_ss, 1))
                        act.activation(hstat[:, :, :], hstat[:, :, :], ACT.Sqrt, bias=eps, scale=1.0 / HD).then_inc(hs_std, 1)
                act.wait_ge(ph_tr, at(ph_tr, 1))
                for m in range(2):
                    ins = copy(u_s[:, m, :, 0:15], ps[:, 7, 128 * m:128 * m + 120].rearrange("p (b r) -> p b r", r=15))
                ins.then_inc(ph_ev, 1)
                for m in range(2):
                    act.wait_ge(w_used, at(w_used, U_U + m + SPLIT + 1))
                    b = U_BANK[m]
                    copy(u_p[:, m, 15:15 + HALF], ps[:, b[0], 0:HALF])
                    copy(u_p[:, m, 15 + HALF:15 + TP], ps[:, b[1], 0:TP - HALF])
                    copy(u_s[:, m, :, 15:19], ps[:, b[1], TP - HALF:HALF].rearrange("p (b s) -> p b s", s=NS)).then_inc(u_ev, 1)
                    split(U_U + m + 2)

                def relu(t, e0, e1):
                    for e in range(e0, e1):
                        n = 4 * (t - 1) + e
                        act.wait_ge(i_mm, at(i_mm, n + 1))
                        if n >= 2:
                            act.wait_ge(i_sc, at(i_sc, n - 1))
                        act.activation(relu_s[:, n % 2, 0:P * (t + 1)], ps[:, 7, 0:P * (t + 1)], ACT.Relu,
                                       scale=0.125).then_inc(i_relu, 1)

                def softplus(h):
                    first = steps.n
                    for i in range(4):
                        blk = Lb[:, h % 2, BOFF[i]:BOFF[i] + BN[i]]
                        act.wait_ge(b_min, at(b_min, 4 * h + i + 1))
                        act.activation(blk, blk, ACT.Exp).then_inc(act_step, steps.step())
                    for i in range(4):
                        blk = Lb[:, h % 2, BOFF[i]:BOFF[i] + BN[i]]
                        act.wait_ge(act_step, steps.value(first + i + 1))
                        act.activation(blk, blk, ACT.Ln, bias=one).then_inc(b_ln, 1)

                relu(1, 0, 4)
                softplus(0)
                softplus(1)
                for h in range(6):
                    act.wait_ge(b_tri, at(b_tri, h + 1))
                    if h >= 1:
                        act.wait_ge(b_o, at(b_o, h))
                    for i in range(4):
                        act.activation(Ab[:, BOFF[i]:BOFF[i] + BN[i]], bz(h, i), ACT.Exp).then_inc(b_exp, 1)
                    if h + 2 < 6:
                        softplus(h + 2)
                    half = slice(HD * (h % 2), HD * (h % 2) + HD)
                    act.wait_ge(b_o, at(b_o, h + 1))
                    copy(aH[half, 3 + h // 2, 0:TP], ps[half, 6, :]).then_inc(b_hi, 1)
                    if h < 4:
                        relu(2 + h // 2, 2 * (h % 2), 2 * (h % 2) + 2)

                for m in range(25):
                    if m < 24:
                        t = m // 6
                        W = P * (t + 1)
                        act.wait_ge(q_max, at(q_max, m + 1))
                        if m >= 2:
                            act.wait_ge(pt_mm, at(pt_mm, m - 1))
                        act.activation(prob[:, m % 2, 0:W], ps[:, m % 2, 0:W], ACT.Exp, bias=stat[:, m % 2, 1:2],
                                       scale=0.125, accum_out=stat[:, m % 2, 2:3]).then_inc(q_exp, 1)
                    if m >= 1:
                        c = m - 1
                        t, g, j = c // 6, c // 3, c % 3
                        act.wait_ge(pt_mm, at(pt_mm, c + 1))
                        if j == 0 and g >= 1:
                            act.wait_ge(o_mm, at(o_mm, g))
                        copy(probT[:, 0:t + 1, j, :], ps[:, 2 + c % 2, 0:P * (t + 1)].rearrange("p (b q) -> p b q", q=P)).then_inc(pt_ev, 1)
                    if m >= 4 and m % 3 == 1:
                        o_copy_g = m // 3 - 1
                        n = o_copy_g % 2
                        half = slice(HD * n, HD * n + HD)
                        act.wait_ge(o_mm, at(o_mm, o_copy_g + 1))
                        copy(aH[half, 0:3, P * (o_copy_g // 2):P * (o_copy_g // 2) + P],
                             ps[half, 4 + n, 0:384].rearrange("p (j q) -> p j q", q=P)).then_inc(o_hi, 1)
                g, n, half = 7, 1, slice(HD, P)
                act.wait_ge(o_mm, at(o_mm, 8))
                copy(aH[half, 0:3, P * 3:P * 4], ps[half, 5, 0:384].rearrange("p (j q) -> p j q", q=P)).then_inc(o_hi, 1)

                for m in range(2):
                    act.wait_ge(y_mm, at(y_mm, m + 1))
                    act.activation(halves(aH[:, 6 + m, :]), psh(2 * m), ACT.Copy, scale=vec(V_PS + m)).then_inc(y_hi, 1)

                for pg in range(NPAGES):
                    act.wait_ge(kt_mm, at(kt_mm, pg + 1))
                    if pg == 0:
                        act.wait_ge(y_lo, at(y_lo, 2))
                    if pg >= 2:
                        act.wait_ge(kq_mm, at(kq_mm, pg - 1))
                    copy(KT[0:HD, pg % 2, 512:640], ps[0:HD, 7 - 3 * (pg % 2), 0:128])
                    copy(KT[:, pg % 2, 0:512], ps[:, 5 + pg % 2, :]).then_inc(kt_ev, 1)
                act.wait_ge(d_new, at(d_new, 1))
                act.activation(rel_d[:, :], ps[:, 0, 0:KEYS_S], ACT.Relu, scale=0.125).then_inc(d_relu, 1)
                act.wait_ge(d_min, at(d_min, 1))
                act.activation(L_d[:, :], L_d[:, :], ACT.Exp).then_inc(act_step, steps.step())
                act.activation(L_n[:, :], L_n[:, :], ACT.Exp).then_inc(act_step, steps.step())
                act.wait_ge(act_step, steps.value())
                act.activation(L_d[:, :], L_d[:, :], ACT.Ln, bias=one)
                act.activation(L_n[:, :], L_n[:, :], ACT.Ln, bias=con[0:TS, C_1:C_1 + 1]).then_inc(d_ln, 1)
                act.wait_ge(d_tri, at(d_tri, 1))
                act.activation(A_d[:, :], ps[:, 3, 0:384], ACT.Exp)
                act.activation(A_n[:, :], ps[0:TS, 4, 0:192], ACT.Exp).then_inc(d_A, 1)
                for n in range(2):
                    act.wait_ge(d_max, at(d_max, n + 1))
                    act.activation(P_d[:, n, :], ps[0:96, 1 + n, 0:KEYS_S], ACT.Exp, bias=st_d[:, n, 1:2], scale=0.125,
                                   accum_out=st_d[:, n, 2:3]).then_inc(d_exp, 1)
                act.wait_ge(d_ptm, at(d_ptm, 1))
                for n in range(2):
                    copy(PT_d[:, n, 0:2, :], ps[:, 5 + n, 0:192].rearrange("p (b q) -> p b q", q=96))
                    ins = copy(PT_d[0:TS, n, 2, :], ps[0:TS, 5 + n, 192:288])
                ins.then_inc(d_pte, 1)
                act.wait_ge(vp_use, at(vp_use, NPAGES))
                for n in range(2):
                    copy(aH[:, 3 * n:3 * n + 3, TP:T], ps[:, 3 * n, 0:96].rearrange("p (j q) -> p j q", q=TS)).then_inc(d_hi, 1)

                for m in range(KD):
                    u = U_OUT + m
                    split(u + 2)
                norm(1)
                act.wait_ge(st_tr, at(st_tr, 1))
                copy(stT[:, :, :], ps[:, 5, 0:KF * 2 * NB].rearrange("p (f b) -> p f b", b=2 * NB)).then_inc(st_ev, 1)

                def ffn(slot, f, k, uo, i=0, per_turn=0):
                    split(U_UP + uo + 2, i, per_turn)
                    b = 4 * slot
                    act.wait_ge(w_used, at(w_used, 2 * f + U_UP + SPLIT + 1))
                    act.wait_ge(g_pre, at(g_pre, f + 1))
                    copy(G[:, slot, 2:2 + HALF], ps[:, b, 0:HALF])
                    copy(G[:, slot, 2 + HALF:2 + TP], ps[:, b + 1, 0:TP - HALF])
                    g_s = G[:, slot, 2 + TP:].rearrange("p (b s) -> p b s", s=6)
                    copy(g_s[:, :, 2:6], ps[:, b + 1, TP - HALF:HALF].rearrange("p (b s) -> p b s", s=NS)).then_inc(g_ev, 1)
                    act.wait_ge(g_ev, at(g_ev, f + 1))
                    act.activation(Cv[:, slot, :], G[:, slot, 0:GW - 2], ACT.Identity, bias=vec_at(V_CB, f),
                                   scale=vec_at(V_CW, f)).then_inc(c_1, 1)
                    act.wait_ge(c_3, at(c_3, f + 1))
                    act.wait_ge(g_keep, at(g_keep, f + 1))
                    act.activation(G[:, slot, 2:GW], Cv[:, slot, :], ACT.Sigmoid).then_inc(s_g, 1)
                    split(U_UP + uo + 3, i, per_turn)
                    act.wait_ge(v_mul, at(v_mul, f + 3))
                    copy(act_at(actH, f), a_tmp[:, slot, :]).then_inc(f_hi, 1)

                act.wait_ge(g_zero, at(g_zero, 1))
                with act.Fori(0, KF // 2) as i:
                    for j in range(2):
                        ffn(j, 2 * i + j, j, 2 * j, i, 4)
                with act.Fori(0, 2) as i:
                    for j in range(12):
                        split(U_DOWN + j + 2, i, 12)

                act.wait_ge(pp_tr, at(pp_tr, 1))
                for b in range(3):
                    nt = 2 if b < 2 else 1
                    n = nt * P if b < 2 else TS
                    src = ps[:, b, 0:nt * 256].rearrange("p (t k q) -> p k t q", k=2, q=P)
                    if b < 2:
                        ins = copy(pH[:, :, 256 * b:256 * b + 256].rearrange("p k (t q) -> p k t q", q=P), src)
                    else:
                        ins = copy(pH[:, :, TP:T], ps[:, b, 0:256].rearrange("p (k q) -> p k q", q=P)[:, :, 0:TS])
                    ins.then_inc(pp_hi, 1)
                for q in range(2):
                    for mm in range(4):
                        m = 4 * q + mm
                        if mm < 3:
                            act.wait_ge(pr_mm, at(pr_mm, 3 * q + mm + 1))
                        else:
                            act.wait_ge(w_used, at(w_used, U_PROJ + q + SPLIT + 1))
                        copy(halves(projT[:, m, :]), psh(2 * (m % 4))).then_inc(pr_ev, 1)
                    split(U_PROJ + q + 2)
                norm(2)
                for m in range(KD):
                    if m + 2 < KD:
                        split(U_GATE + m + 2)
                    act.wait_ge(w_used, at(w_used, U_GATE + m + SPLIT + 1))
                    if m >= 2:
                        act.wait_ge(h_new, at(h_new, 3 * KD + m - 1))
                    act.activation(halves(sig[:, m % 2, :]), psh(2 * (m % 3)), ACT.Sigmoid).then_inc(gt_sig, 1)
                assert steps.n == ACT_STEPS, steps.n

        @block.vector
        def _(dve):

            dve.sem_inc(w_lo, RAW)
            dve.sem_inc(v_mul, 2)
            dve.wait_ge(con_ld, 16)
            dve.tensor_copy(con_bf[:, 0, :], ident)
            for j in range(3):
                dve.tensor_copy(id3_bf[:, TS * j:TS * j + TS], con[0:TS, C_ID:C_ID + TS])
            dve.tensor_copy(con_bf[:, 1, :], con[:, C_BB:C_BB + P])
            dve.tensor_copy(con_bf[:, 2, :], con[:, C_BA:C_BA + P]).then_inc(con_cast, 1)
            for t in range(TILES):
                for b in range(2):
                    i, n = 2 * t + b, TOKW[t]
                    dve.wait_ge(emb_tr, i + 1)
                    ins = dve.tensor_copy(hT[:, 4 * b:4 * b + 4, P * t:P * t + n],
                                          ps[:, i % 8, :].rearrange("p (k q) -> p k q", q=P)[:, :, 0:n])
                    ins.then_inc((emb_ev if i < 2 else h_new), 1)
            with dve.Fori(0, LAYERS) as l:
                steps = Steps(l, DVE_STEPS)

                def at(s, n):
                    return l * per_layer[s.name] + n

                def split(u, i=0, per_turn=0):
                    dve.wait_ge(w_hi, at(w_hi, u + i * per_turn + 1))
                    for a, b in unit_cols(u):
                        ins = dve.tensor_tensor(w_L[u % SPLIT][:, a:b], w_raw[u % RAW][:, a:b],
                                                w_H[u % SPLIT][:, a:b].bitcast(F32), ALU.subtract)
                    ins.then_inc(w_lo, 1)

                def lo(out, full, hi):
                    return dve.tensor_tensor(out, full, hi.bitcast(F32), ALU.subtract)

                def norm(i):
                    dve.wait_ge(n_std, at(n_std, i + 1))
                    dve.reciprocal(r_all[:, :], r_all[:, :]).then_inc(n_rec, 1)
                    dve.wait_ge(n_rec, at(n_rec, i + 1))
                    for k in range(KD):
                        if k >= 2:
                            dve.wait_ge(a_lo, at(a_lo, 8 * i + k - 1))
                        dve.scalar_tensor_tensor(a_tmp[:, k % 2, :], hT[:, k, :], vec((V_ATTN, V_FFN, V_PLE)[i] + k), r_all[:, :],
                                                 ALU.mult, ALU.mult).then_inc(a_t, 1)
                        if k >= 1:
                            dve.wait_ge(a_hi, at(a_hi, 8 * i + k))
                            lo(aL[:, k - 1, :], a_tmp[:, (k - 1) % 2, :], aH[:, k - 1, :]).then_inc(a_lo, 1)
                    dve.wait_ge(a_hi, at(a_hi, 8 * i + 8))
                    lo(aL[:, 7, :], a_tmp[:, 1, :], aH[:, 7, :]).then_inc(a_lo, 1)

                split(0)
                split(1)
                dve.wait_ge(vec_ev, at(vec_ev, 1))
                norm(0)
                dve.memset(hstat[:, :, :], 1.0).then_inc(hs_one, 1)
                dve.wait_ge(lay_ld, at(lay_ld, 6 * 16))

                def head_squares(t):
                    n = TOKW[t]
                    dve.wait_ge(p_ev, at(p_ev, t + 1))
                    dve.tensor_tensor(t1[0:n, :], x_tok[0:n, t, :], x_tok[0:n, t, :], ALU.mult).then_inc(dve_step, steps.step())
                    dve.wait_ge(dve_step, steps.value())
                    total = dve.tensor_reduce(hstat[0:n, t, :], t1[0:n, :].rearrange("p (h d) -> p h d", d=HD), AX.X, ALU.add)
                    if t < TILES - 1:
                        total.then_inc(dve_step, steps.step())
                        dve.wait_ge(dve_step, steps.value())
                    else:
                        total.then_inc(hs_ss, 1)

                def rotate(t, heads, parts):
                    n = TOKW[t]
                    w = heads * HD
                    if (heads, t) != (8, 0):
                        dve.wait_ge(rope_ok, at(rope_ok, t if heads == 8 else 5 + t))
                    x = x_tok[0:n, t, 0:w].rearrange("p (h d) -> p h d", d=HD)
                    cs = dcon[0:n, D_COS + 64 * t:D_COS + 64 * t + 64].unsqueeze(1).to_broadcast([n, heads, HD])
                    sn = dcon[0:n, D_SIN + 64 * t:D_SIN + 64 * t + 64].unsqueeze(1)
                    a = t1[0:n, 0:w].rearrange("p (h d) -> p h d", d=HD)
                    b = t2[0:n, 0:w].rearrange("p (h d) -> p h d", d=HD)
                    dve.tensor_tensor(a, x, cs, ALU.mult)
                    dve.tensor_tensor(b[:, :, 0:32], x[:, :, 32:64], sn[:, :, 0:32].to_broadcast([n, heads, 32]), ALU.mult)
                    dve.tensor_tensor(b[:, :, 32:64], x[:, :, 0:32], sn[:, :, 32:64].to_broadcast([n, heads, 32]), ALU.mult).then_inc(dve_step, steps.step())
                    dve.wait_ge(dve_step, steps.value())
                    for out, a0, a1, order in parts:
                        i0, i1 = t1[0:n, a0:a1], t2[0:n, a0:a1]
                        if order:
                            i0, i1 = (v.rearrange("p (n j d) -> p n j d", n=2, j=3) for v in (i0, i1))
                            out = out.rearrange("p (j n d) -> p n j d", n=2, j=3)
                        ins = dve.tensor_tensor(out, i0, i1, ALU.add)
                    ins.then_inc(rope_ok, 1)

                def qk(t):
                    n = TOKW[t]
                    x = x_tok[0:n, t, :].rearrange("p (h d) -> p h d", d=HD)
                    dve.tensor_tensor(x, x, hstat[0:n, t, :].unsqueeze(2).to_broadcast([n, 8, HD]), ALU.mult).then_inc(dve_step, steps.step())
                    dve.wait_ge(dve_step, steps.value())
                    dve.tensor_tensor(x[:, 0:6, :], x[:, 0:6, :], gains[0:n, 0, :].unsqueeze(1).to_broadcast([n, 6, HD]), ALU.mult)
                    dve.tensor_tensor(x[:, 6:8, :], x[:, 6:8, :], gains[0:n, 1, :].unsqueeze(1).to_broadcast([n, 2, HD]), ALU.mult).then_inc(dve_step, steps.step())
                    dve.wait_ge(dve_step, steps.value())
                    rotate(t, 8, [(r_tok[0:n, t, 0:384], 0, 384, True), (r_tok[0:n, t, 384:512], 384, 512, False)])

                def index(t):
                    n = TOKW[t]
                    dve.wait_ge(t_mm, at(t_mm, t + 1))
                    if t == 0:
                        dve.wait_ge(ak_out, at(ak_out, 5 * 16))
                    dve.tensor_scalar(wi[0:n, t, :], x_tok[0:n, t, 320:324], 0.5, None, ALU.mult)
                    rotate(t, 5, [(r_tok[0:n, t, 0:320], 0, 320, False), (r_tok[0:n, t, 320:384], 256, 320, False)])

                for c in range(5):
                    for j in range(4):
                        if c == 1:
                            for t in ((0,), (1,), (2,), (3, 4))[j]:
                                qk(t)
                        if c == 2:
                            for t in ((0,), (1,), (2,), (3, 4))[j]:
                                dve.wait_ge(p_ev, at(p_ev, 5 + t + 1))
                                index(t)
                        if j < 3:
                            split(4 * c + j + 2)
                    if c == 0:
                        dve.wait_ge(hs_one, at(hs_one, 1))
                        for t in range(TILES):
                            head_squares(t)
                    split(4 * c + 5)
                    if c == 0:
                        dve.wait_ge(hs_std, at(hs_std, 1))
                        dve.reciprocal(hstat[:, :, :], hstat[:, :, :]).then_inc(dve_step, steps.step())
                        dve.wait_ge(dve_step, steps.value())
                split(U_OUT)
                split(U_OUT + 1)
                dve.wait_ge(u_ev, at(u_ev, 2))
                dve.wait_ge(ph_ev, at(ph_ev, 1))
                for m in range(2):
                    ins = dve.tensor_copy(u_c[:, m, :].rearrange("p (b r) -> p b r", r=15), u_s[:, m, :, NS:])
                ins.then_inc(u_cp, 1)
                dve.wait_ge(uo_tr, at(uo_tr, 1))
                dve.tensor_copy(u_tok[0:NB * 15, 0:256], ps[0:NB * 15, 7, 0:256])
                dve.tensor_copy(u_tok[0:15, 256:512], ps[0:15, 7, 256:512]).then_inc(uo_ev, 1)

                def weigh(t, e0, e1):
                    W = P * (t + 1)
                    sc = score[:, (t - 1) % 2, 0:W]
                    for e in range(e0, e1):
                        n = 4 * (t - 1) + e
                        dve.wait_ge(i_relu, at(i_relu, n + 1))
                        if e == 0:
                            ins = dve.tensor_scalar(sc, relu_s[:, n % 2, 0:W], wi[:, t, 0:1], None, ALU.mult)
                        else:
                            dve.wait_ge(i_sc, at(i_sc, n))
                            ins = dve.scalar_tensor_tensor(sc, relu_s[:, n % 2, 0:W], wi[:, t, e:e + 1], sc, ALU.mult, ALU.add)
                        ins.then_inc(i_sc, 1)

                def select(t, r0, r1):
                    sc = score[:, (t - 1) % 2, 0:P * (t + 1)]
                    if r0 == 0:
                        dve.wait_ge(i_diag, at(i_diag, t))
                    hold(dve)
                    for _ in range(r0, r1):
                        dve.max(m8[:, :], sc).then_inc(dve_step, steps.step())
                        dve.wait_ge(dve_step, steps.value())
                        hold(dve)
                        dve.match_replace(sc, m8[:, :], sc, TAKEN).then_inc(dve_step, steps.step())
                        dve.wait_ge(dve_step, steps.value())
                        hold(dve)
                    if r1 == ROUNDS:
                        dve.tensor_scalar(bias_p[:, t - 1, 0:P * (t + 1)], sc, CUT, NEG, ALU.is_gt, ALU.mult).then_inc(sel_ok, 1)

                def clamp(h):
                    dve.wait_ge(b_z, at(b_z, h + 1))
                    for i in range(4):
                        dve.tensor_scalar(Lb[:, h % 2, BOFF[i]:BOFF[i] + BN[i]], bz(h, i), 40.0, None, ALU.min).then_inc(b_min, 1)

                def soft_max0(h):
                    for i in range(4):
                        blk = Lb[:, h % 2, BOFF[i]:BOFF[i] + BN[i]]
                        dve.wait_ge(b_ln, at(b_ln, 4 * h + i + 1))
                        dve.tensor_tensor(blk, blk, bz(h, i), ALU.max).then_inc(b_max, 1)

                dve.wait_ge(bk_out, at(bk_out, 5 * 16))
                weigh(1, 0, 4)
                for h in range(2):
                    clamp(h)
                    soft_max0(h)
                for h in range(6):
                    t, r = 1 + h // 2, 8 * (h % 2)
                    if h + 2 < 6:
                        clamp(h + 2)
                    select(t, r, r + 4)
                    if h + 2 < 6:
                        soft_max0(h + 2)
                    half = slice(HD * (h % 2), HD * (h % 2) + HD)
                    dve.wait_ge(b_hi, at(b_hi, h + 1))
                    lo(aL[half, 3 + h // 2, 0:TP], ps[half, 6, :], aH[half, 3 + h // 2, 0:TP]).then_inc(b_lo, 1)
                    if h < 4:
                        weigh(2 + h // 2, 2 * (h % 2), 2 * (h % 2) + 2)
                    select(t, r + 4, r + 8)

                def row_max(m):
                    t = m // 6
                    dve.wait_ge(q_mm, at(q_mm, m + 1))
                    if m >= 2:
                        dve.wait_ge(q_exp, at(q_exp, m - 1))
                    dve.tensor_reduce(stat[:, m % 2, 0:1], ps[:, m % 2, 0:P * (t + 1)], AX.X, ALU.max).then_inc(dve_step, steps.step())
                    dve.wait_ge(dve_step, steps.value())
                    dve.tensor_scalar(stat[:, m % 2, 1:2], stat[:, m % 2, 0:1], -0.125, None, ALU.mult).then_inc(q_max, 1)

                row_max(0)
                for m in range(24):
                    if m + 1 < 24:
                        row_max(m + 1)
                    dve.wait_ge(q_exp, at(q_exp, m + 1))
                    if m >= 2:
                        dve.wait_ge(q_norm, at(q_norm, m - 1))
                    dve.reciprocal(stat[:, m % 2, 3:4], stat[:, m % 2, 2:3]).then_inc(q_rec, 1)
                    if m >= 4 and m % 3 == 1:
                        g = m // 3 - 1
                        n = g % 2
                        half = slice(HD * n, HD * n + HD)
                        cols = slice(P * (g // 2), P * (g // 2) + P)
                        dve.wait_ge(o_hi, at(o_hi, g + 1))
                        lo(aL[half, 0:3, cols], ps[half, 4 + n, 0:384].rearrange("p (j q) -> p j q", q=P), aH[half, 0:3, cols]).then_inc(o_lo, 1)

                for m in range(2):
                    UN = 15 + TP
                    if m:
                        dve.wait_ge(pooled_ok, at(pooled_ok, m))
                    dve.wait_ge(u_ev, at(u_ev, m + 1))
                    dve.wait_ge(ph_ev, at(ph_ev, 1))
                    dve.wait_ge(u_zero, at(u_zero, 1))
                    up, us = u_p[:, m, :], u_s[:, m, :, :]

                    def view(x):
                        return x[:, 0:UN], x[:, UN:].rearrange("p (b r) -> p b r", r=19)

                    src = (up, us)
                    for s in range(2 * m + 2):
                        sh = 1 << s
                        dst = view(pw[s % 2])
                        keep_low = s == 2 * m + 1
                        rows = slice(HD, P) if keep_low else slice(0, P)
                        dve.tensor_tensor(dst[0][rows, 2 * sh - 1:], src[0][rows, 2 * sh - 1:], src[0][rows, sh - 1:UN - sh], ALU.add)
                        dve.tensor_tensor(dst[1][rows, :, 2 * sh - 1:], src[1][rows, :, 2 * sh - 1:], src[1][rows, :, sh - 1:19 - sh], ALU.add).then_inc(dve_step, steps.step())
                        dve.wait_ge(dve_step, steps.value())
                        low, src = src, dst
                    for rows, s2 in ((slice(0, HD), low), (slice(HD, P), src)):
                        dve.scalar_tensor_tensor(pooled[rows, m, 0:TP], s2[0][rows, 15:], con[rows, C_INVW + m:C_INVW + m + 1],
                                                 up[rows, 15:], ALU.mult, ALU.subtract)
                        dve.tensor_tensor(first16[rows, :], s2[0][rows, 15:31],
                                          con[rows, C_INV16 + 16 * m:C_INV16 + 16 * m + 16], ALU.mult).then_inc(dve_step, steps.step())
                        dve.scalar_tensor_tensor(pooled[rows, m, TP:].rearrange("p (b s) -> p b s", s=NS), s2[1][rows, :, 15:],
                                                 con[rows, C_INVW + m:C_INVW + m + 1], us[rows, :, 15:], ALU.mult, ALU.subtract).then_inc(dve_step, steps.step())
                        dve.wait_ge(dve_step, steps.value())
                        ins = dve.tensor_tensor(pooled[rows, m, 0:16], first16[rows, :], up[rows, 15:31], ALU.subtract)
                    ins.then_inc(pooled_ok, 1)
                dve.wait_ge(o_hi, at(o_hi, 8))
                lo(aL[HD:P, 0:3, P * 3:P * 4], ps[HD:P, 5, 0:384].rearrange("p (j q) -> p j q", q=P), aH[HD:P, 0:3, P * 3:P * 4]).then_inc(o_lo, 1)
                for m in range(2):
                    dve.wait_ge(y_hi, at(y_hi, m + 1))
                    dve.scalar_tensor_tensor(halves(aL[:, 6 + m, :]), psh(2 * m), vec(V_PS + m), halves(aH[:, 6 + m, :]).bitcast(F32),
                                             ALU.mult, ALU.subtract).then_inc(y_lo, 1)

                dve.wait_ge(d_zero, at(d_zero, 1))
                flat_qi = qim[:, :, :].rearrange("p b n -> p (b n)")
                for e in range(4):
                    rows = slice(HD * (e % 2), HD * (e % 2) + HD)
                    dst = bass.AP(qim, flat_qi.offset + TS * e, [list(flat_qi.ap[0]), [P + NS, NB], [1, NS]])
                    dve.tensor_copy(dst, featT[rows, F_QI + e // 2, TP:T].rearrange("p (b s) -> p b s", s=NS))
                    dve.tensor_copy(wic[TS * e:TS * e + TS, :], wi[0:TS, 4, e:e + 1])
                flat_qa = qam[:, :, :].rearrange("p b n -> p (b n)")
                for j in range(3):
                    dst = bass.AP(qam, flat_qa.offset + TS * j, [list(flat_qa.ap[0]), [96 + NS, NB], [1, NS]])
                    ins = dve.tensor_copy(dst, featT[:, F_QA + j, TP:T].rearrange("p (b s) -> p b s", s=NS))
                for i in range(2):
                    rows = slice(HD * i, HD * i + HD)
                    dve.tensor_copy(qbm[rows, :, i, :], featT[rows, F_QB:F_QB + 3, TP:T])
                dve.tensor_copy(bb_n[:, :], dcon[0:TS, D_BB:D_BB + TS])
                dve.memset(m8d[:, :], PADDED)
                dve.memset(sco_d[:, KEYS_S:], PADDED).then_inc(dve_step, steps.step())
                dve.wait_ge(dve_step, steps.value())
                dve.tensor_copy(st_d[:, 0, 3:4], con[0:96, C_1:C_1 + 1]).then_inc(d_q, 1)
                dve.wait_ge(d_new, at(d_new, 1))
                dve.tensor_scalar(L_d[:, :], ps[:, 3, 0:384], 40.0, None, ALU.min)
                dve.tensor_scalar(L_n[:, :], ps[0:TS, 4, 0:192], 40.0, None, ALU.min).then_inc(d_min, 1)
                dve.wait_ge(d_relu, at(d_relu, 1))
                dve.tensor_scalar(rel_d[:, :], rel_d[:, :], wic[:, 0:1], None, ALU.mult).then_inc(d_rel, 1)
                dve.wait_ge(d_ln, at(d_ln, 1))
                dve.tensor_tensor(L_d[:, :], L_d[:, :], ps[:, 3, 0:384], ALU.max)
                dve.tensor_tensor(L_n[:, :], L_n[:, :], ps[0:TS, 4, 0:192], ALU.max).then_inc(dve_step, steps.step())
                dve.wait_ge(dve_step, steps.value())
                dve.tensor_tensor(L_n[:, :], L_n[:, :], dcon[0:TS, D_MB:D_MB + 192], ALU.mult).then_inc(d_sp, 1)
                dve.wait_ge(d_sum, at(d_sum, 1))
                dve.tensor_tensor(sco_d[:, 0:KEYS_S], ps[0:TS, 7, 0:KEYS_S], dcon[0:TS, D_MA:D_MA + KEYS_S], ALU.add).then_inc(dve_step, steps.step())
                dve.wait_ge(dve_step, steps.value())
                hold(dve)
                for _ in range(TOPK_S // 8):
                    dve.max(m8d[:, 0:8], sco_d[:, :]).then_inc(dve_step, steps.step())
                    dve.wait_ge(dve_step, steps.value())
                    hold(dve)
                    dve.match_replace(sco_d[:, :], m8d[:, 0:8], sco_d[:, :], TAKEN).then_inc(dve_step, steps.step())
                    dve.wait_ge(dve_step, steps.value())
                    hold(dve)
                dve.max(m8d[:, 0:8], sco_d[:, :]).then_inc(dve_step, steps.step())
                dve.wait_ge(dve_step, steps.value())
                hold(dve)
                dve.tensor_copy(m8d[:, 8:9], m8d[:, 0:1]).then_inc(dve_step, steps.step())
                dve.wait_ge(dve_step, steps.value())
                hold(dve)
                dve.match_replace(sco_d[:, :], m8d[:, 8:16], sco_d[:, :], TAKEN).then_inc(dve_step, steps.step())
                dve.wait_ge(dve_step, steps.value())
                hold(dve)
                dve.tensor_scalar(bias_d[:, :], sco_d[:, 0:KEYS_S], CUT, NEG, ALU.is_gt, ALU.mult).then_inc(d_bias, 1)
                dve.wait_ge(d_log, at(d_log, 1))
                for n in range(2):
                    dve.tensor_reduce(st_d[:, n, 0:1], ps[0:96, 1 + n, 0:KEYS_S], AX.X, ALU.max).then_inc(dve_step, steps.step())
                    dve.wait_ge(dve_step, steps.value())
                    dve.tensor_scalar(st_d[:, n, 1:2], st_d[:, n, 0:1], -0.125, None, ALU.mult).then_inc(d_max, 1)
                for n in range(2):
                    dve.wait_ge(d_exp, at(d_exp, n + 1))
                    dve.reciprocal(st_d[:, n, 3:4], st_d[:, n, 2:3]).then_inc(dve_step, steps.step())
                    dve.wait_ge(dve_step, steps.value())
                    dve.tensor_scalar(P_d[:, n, :], P_d[:, n, :], st_d[:, n, 3:4], None, ALU.mult).then_inc(d_nrm, 1)
                for n in range(2):
                    dve.wait_ge(d_hi, at(d_hi, n + 1))
                    lo(aL[:, 3 * n:3 * n + 3, TP:T], ps[:, 3 * n, 0:96].rearrange("p (j q) -> p j q", q=TS), aH[:, 3 * n:3 * n + 3, TP:T]).then_inc(d_lo, 1)

                for m in range(KD):
                    split(U_OUT + m + 2)
                    dve.wait_ge(w_used, at(w_used, U_OUT + m + SPLIT + 1))
                    dve.tensor_tensor(halves(hT[:, m, :]), halves(hT[:, m, :]), psh(2 * (m % 3)), ALU.add).then_inc(h_new, 1)
                norm(1)

                def ffn(slot, f, uo, i):
                    split(U_UP + uo + 2, i, 4)
                    dve.wait_ge(c_1, at(c_1, f + 1))
                    dve.scalar_tensor_tensor(Cv[:, slot, :], G[:, slot, 1:GW - 1], vec_at(V_CW + KF, f), Cv[:, slot, :],
                                             ALU.mult, ALU.add).then_inc(c_2, 1)
                    dve.wait_ge(c_2, at(c_2, f + 1))
                    dve.scalar_tensor_tensor(Cv[:, slot, :], G[:, slot, 2:GW], vec_at(V_CW + 2 * KF, f), Cv[:, slot, :],
                                             ALU.mult, ALU.add).then_inc(c_3, 1)
                    dve.wait_ge(s_g, at(s_g, f + 1))
                    dve.tensor_tensor(Cv[:, slot, :], Cv[:, slot, :], G[:, slot, 2:GW], ALU.mult).then_inc(s_mul, 1)
                    split(U_UP + uo + 3, i, 4)
                    dve.wait_ge(s_mul, at(s_mul, f + 1))
                    dve.wait_ge(w_used, at(w_used, 2 * f + U_UP + 1 + SPLIT + 1))
                    b = 4 * slot + 2
                    dve.tensor_tensor(a_tmp[:, slot, 0:HALF], Cv[:, slot, 0:HALF], ps[:, b, 0:HALF], ALU.mult)
                    dve.tensor_tensor(a_tmp[:, slot, HALF:TP], Cv[:, slot, HALF:TP], ps[:, b + 1, 0:TP - HALF], ALU.mult)
                    c_s = Cv[:, slot, TP:].rearrange("p (b s) -> p b s", s=6)
                    dve.tensor_tensor(a_tmp[:, slot, TP:T].rearrange("p (b s) -> p b s", s=NS), c_s[:, :, 2:6],
                                      ps[:, b + 1, TP - HALF:HALF].rearrange("p (b s) -> p b s", s=NS), ALU.mult).then_inc(v_mul, 1)
                    dve.wait_ge(f_hi, at(f_hi, f + 1))
                    lo(act_at(actL, f), a_tmp[:, slot, :], act_at(actH, f)).then_inc(f_lo, 1)

                with dve.Fori(0, KF // 2) as i:
                    for j in range(2):
                        ffn(j, 2 * i + j, 2 * j, i)
                with dve.Fori(0, 2) as i:
                    for j in range(4):
                        for q in range(3):
                            split(U_DOWN + 3 * j + q + 2, i, 12)
                        dve.wait_ge(w_used, at(w_used, 12 * i + U_DOWN + 3 * j + 2 + SPLIT + 1))
                        h = hT[:, bass.ds(4 * i + j, 1), :].rearrange("p o (h n) -> p (o h) n", h=2)
                        dve.tensor_tensor(h, h, psh(2 * (j % 4)), ALU.add).then_inc(h_new, 1)

                for b in range(3):
                    dve.wait_ge(pp_hi, at(pp_hi, b + 1))
                    if b < 2:
                        q = slice(256 * b, 256 * b + 256)
                        for k in range(2):
                            ins = lo(pL[:, k, q].rearrange("p (t q) -> p t q", q=P),
                                     ps[:, b, :].rearrange("p (t k q) -> p k t q", k=2, q=P)[:, k],
                                     pH[:, k, q].rearrange("p (t q) -> p t q", q=P))
                    else:
                        ins = lo(pL[:, :, TP:T], ps[:, b, 0:256].rearrange("p (k q) -> p k q", q=P)[:, :, 0:TS], pH[:, :, TP:T])
                    ins.then_inc(pp_lo, 1)
                for b in range(6):
                    dve.wait_ge(kp_tr, at(kp_tr, b + 1))
                    w = 512 if b < 5 else 256
                    dve.tensor_copy(keep_tok[:, 512 * b:512 * b + w], ps[0:18, 3 + b % 5, 0:w]).then_inc(kp_ev, 1)
                for q in range(2):
                    split(U_PROJ + q + 2)
                norm(2)
                for m in range(KD):
                    if m + 2 < KD:
                        split(U_GATE + m + 2)
                    dve.wait_ge(gt_sig, at(gt_sig, m + 1))
                    dve.tensor_tensor(sig[:, m % 2, :], sig[:, m % 2, :], projT[:, m, :], ALU.mult).then_inc(dve_step, steps.step())
                    dve.wait_ge(dve_step, steps.value())
                    dve.tensor_tensor(hT[:, m, :], hT[:, m, :], sig[:, m % 2, :], ALU.add).then_inc(h_new, 1)
                assert steps.n == DVE_STEPS, steps.n
            for i in range(2 * TILES):
                t, b, n = i // 2, i % 2, TOKW[i // 2]
                dve.wait_ge(y_tr, i + 1)
                dve.tensor_copy(xy[0:n, t, 512 * b:512 * b + 512], ps[0:n, i % 8, :]).then_inc(y_ev, 1)

        @block.tensor
        def _(pe):
            pe.sem_inc(w_used, SPLIT)
            pe.wait_ge(con_ld, 16)
            pe.wait_ge(x_ld, 32)
            for i in range(2 * TILES):
                t, b, n = i // 2, i % 2, TOKW[i // 2]
                if i >= 8:
                    pe.wait_ge(emb_ev, i - 7)
                for k in range(4):
                    mm = pe.transpose(ps[:, i % 8, P * k:P * k + n], xy[0:n, t, P * (4 * b + k):P * (4 * b + k) + P], ident[0:n, 0:n])
                mm.then_inc(emb_tr, 1)
            pe.wait_ge(con_cast, 1)
            with pe.Fori(0, LAYERS) as l:
                def at(s, n):
                    return l * per_layer[s.name] + n

                def tri_product(out, wh, wl, xh, xl, start, stop):
                    pe.matmul(out, wh, xh, start=start, stop=False)
                    pe.matmul(out, wh, xl, start=False, stop=False)
                    return pe.matmul(out, wl, xh, start=False, stop=stop)

                def dense(bank, u, blocks, xH, xL, first, last, c0=0, stride=P):
                    H, Lo = w_H[u % SPLIT], w_L[u % SPLIT]
                    for n, k in enumerate(blocks):
                        w = slice(c0 + stride * n, c0 + stride * n + P)
                        for half in range(2):
                            x = slice(HALF * half, HALF * half + HALF)
                            mm = tri_product(ps[:, bank + half, 0:HALF], H[:, w], Lo[:, w], xH[:, k, x], xL[:, k, x],
                                             first and n == 0, last and n == len(blocks) - 1)
                    return mm

                def norm(i):
                    for k in range(KD):
                        pe.wait_ge(n_sq, at(n_sq, 8 * i + k + 1))
                        pe.matmul(ps[:, 6, 0:HALF], ones, a_tmp[:, k % 2, 0:HALF], start=k == 0, stop=k == KD - 1)
                        pe.matmul(ps[:, 7, 0:HALF], ones, a_tmp[:, k % 2, HALF:T], start=k == 0, stop=k == KD - 1).then_inc(n_ss, 1)

                pe.wait_ge(vec_ld, at(vec_ld, 6 * 16))
                pe.wait_ge(h_new, at(h_new, KD))
                pe.transpose(ps[:, 0, 0:NV], vec_raw[0:NV, :], ident[0:NV, 0:NV]).then_inc(vec_tr, 1)
                norm(0)

                def proj_free(i):
                    c, t = divmod(i, 5)
                    if c < 2:
                        pe.wait_ge(p_ev, at(p_ev, i + 1))
                    elif c < 4:
                        pe.wait_ge(plain_ok, at(plain_ok, i - 10 + 1))
                    else:
                        pe.wait_ge(p_ev, at(p_ev, 10 + t + 1))

                def turn(c, t):
                    g, n = 5 * c + t, TOKW[t]
                    if c < 2:
                        pe.wait_ge(rope_ok, at(rope_ok, 5 * c + t + 1))
                    else:
                        pe.wait_ge(plain_ok, at(plain_ok, 5 * (c - 2) + t + 1))
                    if g >= 1:
                        pe.wait_ge(t_ev, at(t_ev, g))
                    else:
                        pe.wait_ge(n_rec, at(n_rec, 1))
                    if t == TILES - 1:
                        hold(pe)
                    for b in range(CH_BLOCKS[c][1]):
                        mm = pe.transpose(ps[:, 7, P * b:P * b + n], r_tok[0:n, t, P * b:P * b + P], ident[0:n, 0:n])
                    mm.then_inc(t_mm, 1)

                pe.wait_ge(a_lo, at(a_lo, 8))
                for c in range(5):
                    w = CHUNK[c][1] - CHUNK[c][0]
                    for k in range(KD):
                        u = 4 * c + k // 2
                        pe.wait_ge(w_lo, at(w_lo, RAW + u + 1))
                        wh, wl = (x[u % SPLIT][:, 512 * (k % 2):512 * (k % 2) + w] for x in (w_H, w_L))
                        for t in range(TILES):
                            i, n = 5 * c + t, TOKW[t]
                            if k == 0:
                                if i >= 7:
                                    proj_free(i - 7)
                            tok = slice(P * t, P * t + n)
                            mm = tri_product(ps[0:n, i % 7, 0:w], aH[:, k, tok], aL[:, k, tok], wh, wl, k == 0, k == KD - 1)
                            if k == KD - 1 and t < TILES - 1:
                                mm.then_inc(p_mm, 1)
                        if k % 2:
                            mm.then_inc(w_used, 1)
                        if c >= 1 and k in GROUP_K:
                            turn(c - 1, GROUP_K.index(k))
                pe.wait_ge(lay_ld, at(lay_ld, 6 * 16))
                pe.wait_ge(t_ev, at(t_ev, 20))
                for m in range(2):
                    mm = pe.transpose(ps[:, 7, P * m:P * m + 120], pst_tok[0:120, P * m:P * m + P], ident[0:120, 0:120])
                mm.then_inc(ph_tr, 1)
                for m in range(2):
                    u = U_U + m
                    pe.wait_ge(w_lo, at(w_lo, RAW + u + 1))
                    proj_free(19 if m == 0 else 24)
                    H, Lo = w_H[u % SPLIT], w_L[u % SPLIT]
                    for half in range(2):
                        x = slice(HALF * half, HALF * half + HALF)
                        for k in range(KD):
                            wk = slice(P * k, P * k + P)
                            mm = tri_product(ps[:, U_BANK[m][half], 0:HALF], H[:, wk], Lo[:, wk], aH[:, k, x], aL[:, k, x], k == 0, k == KD - 1)
                    mm.then_inc(w_used, 1)
                pe.wait_ge(u_cp, at(u_cp, 1))
                for m in range(2):
                    pe.transpose(ps[0:120, 7, P * m:P * m + P], u_c[:, m, :], ident)
                    mm = pe.transpose(ps[0:15, 7, 256 + P * m:256 + P * m + P], u_p[:, m, TP:TP + 15], ident)
                mm.then_inc(uo_tr, 1)

                def index(t, e0, e1):
                    for e in range(e0, e1):
                        n = 4 * (t - 1) + e
                        if n == 0:
                            pe.wait_ge(uo_ev, at(uo_ev, 1))
                        else:
                            pe.wait_ge(i_relu, at(i_relu, n))
                        rows = slice(HD * (e % 2), HD * (e % 2) + HD)
                        pe.matmul(ps[:, 7, 0:P * (t + 1)], featT[rows, F_QI + e // 2, P * t:P * t + P], featT[rows, F_KI, 0:P * (t + 1)],
                                  start=True, stop=True).then_inc(i_mm, 1)

                def logits(h):
                    rows = slice(HD * (h % 2), HD * (h % 2) + HD)
                    if h >= 2:
                        pe.wait_ge(b_exp, at(b_exp, 4 * (h - 1)))
                    for i in range(4):
                        mm = pe.matmul(bz(h, i), featT[rows, F_KB + h // 2, P * i:P * i + P], featT[rows, F_QB + h // 2, P * i:TP],
                                       start=i != 3, stop=True, skip_group_check=True)
                    mm.then_inc(b_z, 1)

                def remainders(h):
                    pe.wait_ge(b_diag, at(b_diag, 4 * h + 4))
                    for i in range(4):
                        pe.matmul(bz(h, i), ntri, Lb[:, h % 2, BOFF[i]:BOFF[i] + BN[i]], start=False, stop=False, skip_group_check=True)
                        for j in range(i + 1, 4):
                            pe.matmul(bz(h, i, P * (j - i)), nones, Lb[:, h % 2, BOFF[j]:BOFF[j] + BN[j]], start=False, stop=False, skip_group_check=True)
                        mm = pe.matmul(bz(h, i, 0, P), id_bf, bb_bf, start=False, stop=True, skip_group_check=True)
                    mm.then_inc(b_tri, 1)

                def b_out(h):
                    if h >= 1:
                        pe.wait_ge(b_lo, at(b_lo, h))
                    for i in range(4):
                        pe.wait_ge(b_exp, at(b_exp, 4 * h + i + 1))
                        mm = pe.matmul(ps[HD * (h % 2):HD * (h % 2) + HD, 6, P * i:TP], V[:, i, P + HD * h:P + HD * h + HD],
                                       Ab[:, BOFF[i]:BOFF[i] + BN[i]], start=i == 0, stop=i == 3, skip_group_check=True)
                    mm.then_inc(b_o, 1)

                index(1, 0, 4)
                logits(0)
                logits(1)
                remainders(0)
                for h in range(6):
                    b_out(h)
                    if h + 2 < 6:
                        logits(h + 2)
                    if h + 1 < 6:
                        remainders(h + 1)
                    if h < 4:
                        index(2 + h // 2, 2 * (h % 2), 2 * (h % 2) + 2)

                def a_logits(m):
                    t, n, j = m // 6, m % 6 // 3, m % 3
                    rows, W = slice(HD * n, HD * n + HD), P * (t + 1)
                    if m >= 2:
                        pe.wait_ge(q_exp, at(q_exp, m - 1))
                    else:
                        pe.wait_ge(b_exp, at(b_exp, 24))
                    if m % 6 == 0 and t >= 1:
                        pe.wait_ge(sel_ok, at(sel_ok, t))
                    pe.matmul(ps[:, m % 2, 0:W], featT[rows, F_QA + j, P * t:P * t + P], featT[rows, F_KA, 0:W], start=True, stop=False)
                    pe.matmul(ps[:, m % 2, 0:W], id_bf, ba_bf if t == 0 else bias_p[:, t - 1, 0:W], start=False, stop=True).then_inc(q_mm, 1)

                def a_out(g):
                    t, n = g // 2, g % 2
                    pe.wait_ge(pt_ev, at(pt_ev, 3 * g + 3))
                    if g >= 2:
                        pe.wait_ge(o_lo, at(o_lo, g - 1))
                    for b in range(t + 1):
                        mm = pe.matmul(ps[HD * n:HD * n + HD, 4 + n, 0:384], V[:, b, HD * n:HD * n + HD], probT[:, b, :, :],
                                       start=b == 0, stop=b == t)
                    mm.then_inc(o_mm, 1)

                a_logits(0)
                a_logits(1)
                for m in range(24):
                    pe.wait_ge(q_norm, at(q_norm, m + 1))
                    if m >= 2:
                        pe.wait_ge(pt_ev, at(pt_ev, m - 1))
                    for b in range(m // 6 + 1):
                        mm = pe.transpose(ps[:, 2 + m % 2, P * b:P * b + P], prob[:, m % 2, P * b:P * b + P], ident)
                    mm.then_inc(pt_mm, 1)
                    if m + 2 < 24:
                        a_logits(m + 2)
                    if m >= 3 and m % 3 == 0:
                        a_out(m // 3 - 1)
                a_out(7)
                for m in range(2):
                    pe.wait_ge(pooled_ok, at(pooled_ok, m + 1))
                    hold(pe)
                    for g in range(2):
                        rows = slice(HD * g, HD * g + HD)
                        for half in range(2):
                            mm = pe.matmul(ps[rows, 2 * m + half, 0:HALF], w_pool[rows, m, :], pooled[rows, m, HALF * half:HALF * half + HALF],
                                           start=True, stop=True)
                    mm.then_inc(y_mm, 1)

                pe.wait_ge(o_lo, at(o_lo, 8))
                pe.wait_ge(y_lo, at(y_lo, 2))

                def page_turn(pg):
                    pe.wait_ge(kp_ld[pg % 3], at(kp_ld[pg % 3], 48 * (pg // 3 + 1)))
                    hold(pe)
                    if pg >= 2:
                        pe.wait_ge(kt_ev, at(kt_ev, pg - 1))
                        hold(pe)
                    pe.transpose(ps[0:HD, 7 - 3 * (pg % 2), 0:P], KP[:, pg % 3, 512:576], ident)
                    for b in range(4):
                        mm = pe.transpose(ps[:, 5 + pg % 2, P * b:P * b + P], KP[:, pg % 3, P * b:P * b + P], ident)
                    mm.then_inc(kt_mm, 1)

                def page_logits(pg):
                    b, p = pg // 2, pg % 2
                    kt = KT[:, pg % 2, :]
                    pe.wait_ge(kt_ev, at(kt_ev, pg + 1))
                    cols = slice(P * p, P * p + P)
                    pe.matmul(ps[:, 0, cols], qim[:, b, :], kt[0:HD, 512:640], start=pg == 0, stop=True, skip_group_check=True)
                    for n in range(2):
                        rows = slice(HD * n, HD * n + HD)
                        pe.matmul(ps[0:96, 1 + n, cols], qam[rows, b, :], kt[rows, 0:128], start=pg == 0, stop=True, skip_group_check=True)
                    for j in range(3):
                        out = ps[:, 3, 192 * p + 2 * TS * j:192 * p + 2 * TS * j + 2 * TS].rearrange("p (i q) -> p i q", q=TS)
                        mm = pe.matmul(out[:, :, NS * b:NS * b + NS], kt[:, P + P * j:P + P * j + P], qbm[:, j, :, NS * b:NS * b + NS],
                                       start=pg == 0 and j == 0, stop=True, skip_group_check=True)
                    mm.then_inc(kq_mm, 1)

                page_turn(0)
                pe.wait_ge(d_q, at(d_q, 1))
                for pg in range(NPAGES):
                    if pg + 1 < NPAGES:
                        page_turn(pg + 1)
                    page_logits(pg)
                pe.wait_ge(kq_mm, at(kq_mm, NPAGES))
                hold(pe)
                for e in range(4):
                    rows = slice(HD * (e % 2), HD * (e % 2) + HD)
                    pe.matmul(ps[TS * e:TS * e + TS, 0, PAST:KEYS_S], featT[rows, F_QI + e // 2, TP:T], featT[rows, F_KI, TP:T],
                              start=False, stop=True, skip_group_check=True)
                for n in range(2):
                    rows = slice(HD * n, HD * n + HD)
                    for j in range(3):
                        pe.matmul(ps[TS * j:TS * j + TS, 1 + n, PAST:KEYS_S], featT[rows, F_QA + j, TP:T], featT[rows, F_KA, TP:T],
                                  start=False, stop=True, skip_group_check=True)
                for j in range(3):
                    mm = pe.matmul(ps[0:TS, 4, 2 * TS * j:2 * TS * j + 2 * TS], featT[:, F_KB + j, TP:T], qbm[:, j, :, :],
                                   start=j == 0, stop=True, skip_group_check=True)
                mm.then_inc(d_new, 1)
                pe.wait_ge(d_rel, at(d_rel, 1))
                for e in range(4):
                    mm = pe.matmul(ps[0:TS, 7, 0:KEYS_S], ident[:, TS * e:TS * e + TS], rel_d[:, :], start=e == 0, stop=e == 3)
                mm.then_inc(d_sum, 1)
                pe.wait_ge(d_sp, at(d_sp, 1))
                L0, L1 = L_d[:, 0:192], L_d[:, 192:384]
                z0, z1, zn = ps[:, 3, 0:192], ps[:, 3, 192:384], ps[0:TS, 4, 0:192]
                g = dict(start=False, stop=True, skip_group_check=True)
                pe.matmul(z1, ntri, L1, **g)
                pe.matmul(z1, nones[0:TS, :], L_n[:, :], **g)
                pe.matmul(z0, ntri, L0, **g)
                pe.matmul(z0, nones, L1, **g)
                pe.matmul(z0, nones[0:TS, :], L_n[:, :], **g)
                pe.matmul(zn, ntri[0:TS, 0:TS], L_n[:, :], **g)
                pe.matmul(zn.rearrange("p (h q) -> p h q", q=TS), id_bf[0:TS, 0:TS], bb_n[:, :].unsqueeze(1).to_broadcast([TS, 6, TS]), **g).then_inc(d_tri, 1)
                pe.wait_ge(d_bias, at(d_bias, 1))
                for n in range(2):
                    mm = pe.matmul(ps[0:96, 1 + n, 0:KEYS_S], id3_bf[:, :], bias_d[:, :], **g)
                mm.then_inc(d_log, 1)
                pe.wait_ge(d_nrm, at(d_nrm, 2))
                for n in range(2):
                    for p in range(2):
                        pe.transpose(ps[:, 5 + n, 96 * p:96 * p + 96], P_d[:, n, P * p:P * p + P], ident[0:96, 0:96])
                    mm = pe.transpose(ps[0:TS, 5 + n, 192:288], P_d[:, n, PAST:KEYS_S], ident[0:96, 0:96])
                mm.then_inc(d_ptm, 1)
                pe.wait_ge(d_pte, at(d_pte, 1))
                pe.wait_ge(d_A, at(d_A, 1))
                for n in range(2):
                    pe.matmul(ps[HD * n:HD * n + HD, 0, 0:96], V[0:TS, 4, HD * n:HD * n + HD], PT_d[0:TS, n, 2, :],
                              start=True, stop=True, skip_group_check=True)
                for h in range(6):
                    half, j = h % 2, h // 2
                    pe.matmul(ps[HD * half:HD * half + HD, 3, TS * j:TS * j + TS], V[0:TS, 4, P + HD * h:P + HD * h + HD],
                              A_n[:, TS * h:TS * h + TS], start=j == 0, stop=True, skip_group_check=True)
                for pg in range(NPAGES):
                    b, p = pg // 2, pg % 2
                    v = VP[:, pg % 3, :]
                    pe.wait_ge(vp_ld[pg % 3], at(vp_ld[pg % 3], 32 * (pg // 3 + 1)))
                    for n in range(2):
                        out = ps[HD * n:HD * n + HD, 0, 0:96].rearrange("p (j b s) -> p j b s", b=NB, s=NS)[:, :, b, :]
                        pe.matmul(out, v[:, HD * n:HD * n + HD], PT_d[:, n, p, :].rearrange("p (j b s) -> p j b s", b=NB, s=NS)[:, :, b, :], **g)
                    for h in range(6):
                        half, j = h % 2, h // 2
                        c, a = TS * j + NS * b, 192 * p + TS * h + NS * b
                        mm = pe.matmul(ps[HD * half:HD * half + HD, 3, c:c + NS], v[:, P + HD * h:P + HD * h + HD], A_d[:, a:a + NS], **g)
                    mm.then_inc(vp_use, 1)
                pe.wait_ge(d_lo, at(d_lo, 2))
                for m in range(KD):
                    u = U_OUT + m
                    pe.wait_ge(w_lo, at(w_lo, RAW + u + 1))
                    if m >= 3:
                        pe.wait_ge(h_new, at(h_new, KD + m - 2))
                    dense(2 * (m % 3), u, range(KD), aH, aL, True, True).then_inc(w_used, 1)
                norm(1)
                pe.wait_ge(st_ld, at(st_ld, 16))
                hold(pe)
                for f in range(KF):
                    mm = pe.transpose(ps[:, 5, 16 * f:16 * f + 16], st_tok[:, P * f:P * f + P], ident[0:16, 0:16])
                mm.then_inc(st_tr, 1)
                pe.wait_ge(a_lo, at(a_lo, 16))
                pe.wait_ge(st_ev, at(st_ev, 1))
                hold(pe)
                with pe.Fori(0, KF // 2) as i:
                    for j in range(4):
                        n = 4 * i + j
                        pe.wait_ge(w_lo, at(w_lo, RAW + U_UP + n + 1))
                        if j % 2 == 0:
                            pe.wait_ge(v_mul, at(v_mul, 2 * i + j // 2 + 1))
                        dense(2 * j, j, range(KD), aH, aL, True, True).then_inc(w_used, 1)
                pe.wait_ge(f_lo, at(f_lo, KF))
                hold(pe)
                with pe.Fori(0, 2) as i:
                    for j in range(4):
                        for q in range(3):
                            u = U_DOWN + 3 * j + q
                            pe.wait_ge(w_lo, at(w_lo, i * 12 + RAW + u + 1))
                            if q == 0:
                                pe.wait_ge(h_new, at(h_new, 4 * i + 2 * KD + j - 3))
                            mm = dense(2 * j, u, range(8 * q, 8 * q + DOWN_K[q]), actH, actL, q == 0, q == 2)
                            mm.then_inc(w_used, 1)
                pe.wait_ge(p_ld, at(p_ld, 32))
                pe.wait_ge(h_new, at(h_new, 3 * KD))
                hold(pe)
                for t in range(TILES):
                    n = TOKW[t]
                    for k in range(2):
                        c = 256 * (t % 2) + P * k
                        mm = pe.transpose(ps[:, t // 2, c:c + n], p_tok[0:n, t, P * k:P * k + P], ident[0:n, 0:n])
                mm.then_inc(pp_tr, 1)
                pe.wait_ge(g_keep, at(g_keep, KF))
                for b in range(6):
                    if b == 5:
                        pe.wait_ge(kp_ev, at(kp_ev, 1))
                    for f in range(4 * b, min(4 * b + 4, KF)):
                        mm = pe.transpose(ps[0:18, 3 + b % 5, P * (f % 4):P * (f % 4) + P], keepT[:, f, :], ident)
                    mm.then_inc(kp_tr, 1)
                pe.wait_ge(pp_lo, at(pp_lo, 3))
                pe.wait_ge(kp_ev, at(kp_ev, 6))
                for q in range(2):
                    u = U_PROJ + q
                    pe.wait_ge(w_lo, at(w_lo, RAW + u + 1))
                    for mm_ in range(4):
                        m = 4 * q + mm_
                        if m >= 4:
                            pe.wait_ge(pr_ev, at(pr_ev, m - 3))
                        mm = dense(2 * (m % 4), u, range(2), pH, pL, True, True, c0=P * mm_, stride=512)
                        mm.then_inc((w_used if mm_ == 3 else pr_mm), 1)
                pe.wait_ge(pr_ev, at(pr_ev, 8))
                norm(2)
                pe.wait_ge(a_lo, at(a_lo, 24))
                for m in range(KD):
                    u = U_GATE + m
                    pe.wait_ge(w_lo, at(w_lo, RAW + u + 1))
                    if m >= 3:
                        pe.wait_ge(gt_sig, at(gt_sig, m - 2))
                    dense(2 * (m % 3), u, range(KD), aH, aL, True, True).then_inc(w_used, 1)
            pe.wait_ge(h_new, KD + LAYERS * per_layer[h_new.name])
            for i in range(2 * TILES):
                t, b, n = i // 2, i % 2, TOKW[i // 2]
                if i >= 8:
                    pe.wait_ge(y_ev, i - 7)
                for k in range(4):
                    mm = pe.transpose(ps[0:n, i % 8, P * k:P * k + P], hT[:, 4 * b + k, P * t:P * t + n], ident)
                mm.then_inc(y_tr, 1)


_INS = ["x_prompt", "x_sample", "cache_a_k", "cache_a_v", "cache_idx_k", "cache_b_k", "cache_b_v", "state_pool",
        "state_conv", "page_table", "p_prompt", "p_sample", "g_attn", "w_in", "g_q_a", "g_k_a", "w_pool",
        "pool_scale", "w_out", "g_ffn", "w_up", "conv_w", "conv_b", "w_down", "g_ple", "w_ple_gate", "w_ple_proj"]
_NEW = {"a_k": (2, HD), "a_v": (2, HD), "idx_k": (HD,), "b_k": (6, HD), "b_v": (6, HD)}


def _outputs():
    yield "y_prompt", (1, TP, D)
    yield "y_sample", (NB, NS, D)
    for kind, lead, rows in (("p", (LAYERS, 1), TP), ("s", (LAYERS, NB), NS)):
        for name, tail in _NEW.items():
            yield f"{name}_{kind}", lead + (rows,) + tail
        yield f"pool_{kind}", lead + (15, 256)
        yield f"conv_{kind}", lead + (2, DFF)


def kernel(**inputs):
    import concourse.bacc as bacc
    from concourse.bass_utils import run_bass_kernel_spmd

    nc = bacc.Bacc("TRN2", target_bir_lowering=False, num_devices=1)
    arrays, t_in, t_out = {}, {}, {}
    given = {name: np.ascontiguousarray(inputs[name]) for name in _INS}
    given["con"], given["dcon"] = shape_constants()
    for name, a in given.items():
        arrays[f"in_{name}"] = a
        t_in[name] = nc.dram_tensor(f"in_{name}", a.shape, mybir.dt.from_np(a.dtype), kind="ExternalInput").ap()
    for name, shape in _outputs():
        t_out[name] = nc.dram_tensor(f"out_{name}", shape, F32, kind="ExternalOutput").ap()
    build(nc, t_in, t_out)
    r = run_bass_kernel_spmd(nc, [arrays], core_ids=[0])
    return tuple(r.results[0][f"out_{name}"] for name, _ in _outputs())
```

```python
from contextlib import ExitStack

import concourse.bass as bass
import numpy as np
from concourse import mybir

F32 = mybir.dt.float32
F32R = mybir.dt.float32r
BF16 = mybir.dt.bfloat16
I32 = mybir.dt.int32
ALU = mybir.AluOpType
ACT = mybir.ActivationFunctionType
AX = mybir.AxisListType

P = 128
D = 1024
KD = D // P
LAYERS = 2
TP = 512
NB = 8
NS = 4
TS = NB * NS
T = TP + TS
HALF = T // 2
PAST = 256
PAGE = 128
NPAGES = NB * PAST // PAGE
NPOOL = NPAGES * 5 // 4
HD = 64
DFF = 2816
KF = DFF // P
PLE = 256
EPS = 1e-6
TOKW = [P, P, P, P, TS]
TILES = len(TOKW)

CHUNK = [(0, 512), (512, 964), (964, 1348), (1348, 1732), (1732, 2116)]
U0 = 2116

UNIT = 1024
U_IN, U_U, U_OUT, U_UP, U_DOWN, U_PROJ, U_GATE = 0, 20, 22, 30, 74, 98, 100
UNITS = 108
RAW, SPLIT = 4, 2
DOWN_K = [8, 8, 6]

TOPK_P, TOPK_S = 128, 65
MASKED = -3.0e38
TAKEN = -3.4e38
CUT = -3.2e38
PADDED = -3.1e38
NEG = -1.0e30
KEYS_S = PAST + TS
ROUNDS = TOPK_P // 8
SOFT = 4

GROUP_K = (2, 3, 5, 6, 7)

C_ID, C_NTRI, C_NONE, C_ONE, C_M01, C_BB, C_BA, C_INVW, C_INV16, C_EPS, C_1 = 0, 128, 256, 384, 512, 640, 768, 896, 898, 930, 931
NC = 932
ACT_STEPS, DVE_STEPS = 30, 221
D_COS, D_SIN, D_MA, D_MB, D_BB = 0, 320, 640, 928, 1120
ND = 1152
V_ATTN, V_FFN, V_PLE, V_CW, V_CB, V_PS = 0, 8, 16, 24, 90, 112
NV = 114
F_QA, F_KA, F_QI, F_KI, F_QB, F_KB = 0, 3, 4, 6, 7, 10
CH_BLOCKS = [(F_QA, 4), (F_QI, 3), (F_QB, 3), (F_KB, 3)]


def shape_constants():
    p, c = np.arange(P)[:, None], np.arange(P)[None, :]
    a = np.zeros((P, NC), np.float32)
    a[:, C_ID:C_ID + P] = p == c
    a[:, C_NTRI:C_NTRI + P] = -(p >= c).astype(np.float32)
    a[:, C_NONE:C_NONE + P] = -1.0
    a[:, C_ONE:C_ONE + P] = 1.0 / D
    a[:, C_M01:C_M01 + P] = p < c
    a[:, C_BB:C_BB + P] = np.where(p < c, 0.0, NEG)
    a[:, C_BA:C_BA + P] = np.where(c <= p, 0.0, NEG)
    for m in range(2):
        for half in range(2):
            w = 2 ** (2 * m + half + 1)
            r = slice(64 * half, 64 * half + 64)
            a[r, C_INVW + m] = 1.0 / w
            a[r, C_INV16 + 16 * m:C_INV16 + 16 * m + 16] = 1.0 / np.minimum(w, np.arange(16) + 1)
    a[:, C_EPS] = EPS
    a[:, C_1] = 1.0
    d = np.zeros((P, ND), np.float32)
    inv = (np.float32(10000.0) ** (-np.arange(32, dtype=np.float32) / np.float32(32))).astype(np.float32)
    for t in range(TILES):
        pos = t * P + np.arange(P) if t < 4 else PAST + np.arange(P) % NS
        ang = (pos.astype(np.float32)[:, None] * inv[None]).astype(np.float32)
        cs, sn = np.cos(ang), np.sin(ang)
        d[:, D_COS + 64 * t:D_COS + 64 * t + 64] = np.concatenate([cs, cs], 1)
        d[:, D_SIN + 64 * t:D_SIN + 64 * t + 64] = np.concatenate([-sn, sn], 1)
    q = np.arange(TS)
    same = q[:, None] // NS == q[None] // NS
    qt, kt = q[:, None] % NS, q[None] % NS
    d[:TS, D_MA + PAST:D_MA + KEYS_S] = np.where(same & (kt <= qt), 0.0, MASKED)
    strict = (same & (qt < kt)).astype(np.float32)
    for h in range(6):
        d[:TS, D_MB + TS * h:D_MB + TS * h + TS] = strict
    d[:TS, D_BB:D_BB + TS] = np.where(strict > 0, 0.0, NEG)
    return a, d


class Steps:

    def __init__(self, layer, per_layer):
        self.n, self.base = 0, layer * per_layer

    def step(self):
        self.n += 1
        return 1

    def value(self, n=None):
        return self.base + (self.n if n is None else n)


def build(nc, t_in, t_out):
    ctx = ExitStack()
    with ctx:
        def sb(name, shape, dt=F32, where=None):
            return (where or ctx).enter_context(nc.sbuf_tensor(name, shape, dt))

        hT = sb("hT", [P, KD, T])
        aH = sb("aH", [P, KD, T], F32R)
        aL = sb("aL", [P, KD, T], F32R)
        w_raw = [sb(f"w_raw{i}", [P, UNIT]) for i in range(RAW)]
        w_H = [sb(f"w_H{i}", [P, UNIT], F32R) for i in range(SPLIT)]
        w_L = [sb(f"w_L{i}", [P, UNIT], F32R) for i in range(SPLIT)]
        con = sb("con", [P, NC])
        con_bf = sb("con_bf", [P, 4, P], BF16)
        id3_bf = sb("id3_bf", [TS, 3 * TS], BF16)
        pages = sb("pages", [1, NPAGES], I32)
        vecT = sb("vecT", [P, NV])
        vec_raw = sb("vec_raw", [P, P])
        a_tmp = sb("a_tmp", [P, 2, T])
        r_all = sb("r_all", [P, T])

        att = ExitStack()
        featT = sb("featT", [P, 13, T], F32, att)
        V = sb("V", [P, TILES, 512], F32, att)
        dcon = sb("dcon", [P, ND], F32, att)
        wi = sb("wi", [P, TILES, 4], F32, att)
        part = ExitStack()
        score = sb("score", [P, 2, TP], F32, part)
        relu_s = sb("relu_s", [P, 2, TP], F32, part)
        bias_p = sb("bias_p", [P, 3, TP], BF16, part)
        probT = sb("probT", [P, 4, 3, P], F32, part)
        stat = sb("stat", [P, SOFT, 4], F32, part)
        m8 = sb("m8", [P, 8], F32, part)
        u_p = sb("u_p", [P, 2, 15 + TP], F32, part)
        u_s = sb("u_s", [P, 2, NB, 15 + NS], F32, part)
        first16 = sb("first16", [P, 16], F32, part)
        u_c = sb("u_c", [P, 2, NB * 15], F32, part)
        pw = [sb(f"pw{i}", [P, 15 + TP + NB * 19], F32, part) for i in range(2)]
        pooled = sb("pooled", [P, 2, T], F32, part)
        w_pool = sb("w_pool", [P, 2, HD], F32, part)
        pst_tok = sb("pst_tok", [P, 2 * P], F32, part)
        u_tok = sb("u_tok", [P, 512], F32, part)
        stage = ExitStack()
        x_tok = sb("x_tok", [P, TILES, 512], F32, stage)
        r_tok = sb("r_tok", [P, TILES, 512], F32, stage)
        t1 = sb("t1", [P, 512], F32, stage)
        t2 = sb("t2", [P, 512], F32, stage)
        gains = sb("gains", [P, 2, HD], F32, stage)
        hstat = sb("hstat", [P, TILES, 8], F32, stage)
        stage.close()
        stick = ExitStack()
        LW = 1280
        Lb = sb("Lb", [P, 2, LW], F32, stick)
        Ab = sb("Ab", [P, LW], F32, stick)
        stick.close()
        soft = ExitStack()
        prob = sb("prob", [P, SOFT, TP], F32, soft)
        soft.close()
        part.close()
        dec = ExitStack()
        KP = sb("KP", [P, 3, 576], F32, dec)
        KT = sb("KT", [P, 2, 640], F32, dec)
        VP = sb("VP", [P, NPAGES, 512], F32, dec)
        qim = sb("qim", [HD, NB, P], F32, dec)
        qam = sb("qam", [P, NB, 96], F32, dec)
        qbm = sb("qbm", [P, 3, 2, TS], F32, dec)
        wic = sb("wic", [P, 1], F32, dec)
        rel_d = sb("rel_d", [P, KEYS_S], F32, dec)
        sco_d = sb("sco_d", [TS, KEYS_S + 8], F32, dec)
        m8d = sb("m8d", [TS, 16], F32, dec)
        bias_d = sb("bias_d", [TS, KEYS_S], BF16, dec)
        P_d = sb("P_d", [96, 2, KEYS_S], F32, dec)
        st_d = sb("st_d", [96, 2, 4], F32, dec)
        PT_d = sb("PT_d", [P, 2, 3, 96], F32, dec)
        L_d = sb("L_d", [P, 384], F32, dec)
        L_n = sb("L_n", [TS, 192], F32, dec)
        A_d = sb("A_d", [P, 384], F32, dec)
        A_n = sb("A_n", [TS, 192], F32, dec)
        bb_n = sb("bb_n", [TS, TS], BF16, dec)
        dec.close()
        att.close()
        ffn = ExitStack()
        stT = sb("stT", [P, KF, 2 * NB], F32, ffn)
        keepT = sb("keepT", [P, KF, 2 + 2 * NB], F32, ffn)
        GW = 2 + TP + 6 * NB
        G = sb("G", [P, 2, GW], F32, ffn)
        Cv = sb("Cv", [P, 2, GW - 2], F32, ffn)
        acts = ExitStack()
        actH = sb("actH", [P, KF, T], F32R, acts)
        actL = sb("actL", [P, KF, T], F32R, acts)
        acts.close()
        st_tok = sb("st_tok", [2 * NB, DFF], F32, ffn)
        ffn.close()
        ple = ExitStack()
        sb("ple_skip", [P, KF * (2 + 4 * NB) + 2 * GW + 2 * (GW - 2)], F32, ple)
        p_tok = sb("p_tok", [P, TILES, PLE], F32, ple)
        pH = sb("pH", [P, 2, T], F32R, ple)
        pL = sb("pL", [P, 2, T], F32R, ple)
        projT = sb("projT", [P, KD, T], F32, ple)
        sig = sb("sig", [P, 2, T], F32, ple)
        keep_tok = sb("keep_tok", [2 + 2 * NB, DFF], F32, ple)
        ple.close()
        edge = ExitStack()
        xy = sb("xy", [P, 5, D], F32, edge)
        edge.close()
        ps = ctx.enter_context(nc.psum_tensor("ps", [P, 8, 512], F32))

        per_layer = {}

        def sg(name, per=1):
            s = ctx.enter_context(nc.semaphore(name))
            per_layer[s.name] = per
            return s

        con_ld, x_ld, page_ld, con_cast = sg("con_ld"), sg("x_ld"), sg("page_ld"), sg("con_cast")
        emb_tr, y_tr, y_ev, y_out = sg("emb_tr"), sg("y_tr"), sg("y_ev"), sg("y_out")
        emb_ev = sg("emb_ev")
        unit_dmas = [3 if U_OUT <= u < U_UP else 1 for u in range(UNITS)]
        w_ld = [sg(f"w_ld{s}", 16 * sum(unit_dmas[s::RAW])) for s in range(RAW)]
        w_hi, w_lo, w_used = sg("w_hi", UNITS), sg("w_lo", UNITS), sg("w_used", UNITS)
        vec_ld, vec_tr, vec_ev = sg("vec_ld", 6 * 16), sg("vec_tr", 1), sg("vec_ev", 1)
        lay_ld = sg("lay_ld", 6 * 16)
        h_new = sg("h_new", 24)
        n_sq, n_ss, n_rec = sg("n_sq", 24), sg("n_ss", 24), sg("n_rec", 3)
        a_t, a_hi, a_lo = sg("a_t", 24), sg("a_hi", 24), sg("a_lo", 24)
        p_mm, p_ev = sg("p_mm", 20), sg("p_ev", 15)
        rope_ok, plain_ok = sg("rope_ok", 10), sg("plain_ok", 10)
        hs_one = sg("hs_one", 1)
        hs_ss, hs_rec = sg("hs_ss", 1), sg("hs_rec", 1)
        t_mm, t_ev = sg("t_mm", 20), sg("t_ev", 20)
        ak_out, ix_out, bk_out, kv_out = sg("ak_out", 80), sg("ix_out", 80), sg("bk_out", 80), sg("kv_out", 160)
        u_ev = sg("u_ev", 2)
        ph_tr, ph_ev, u_zero = sg("ph_tr", 1), sg("ph_ev", 1), sg("u_zero", 1)
        u_cp = sg("u_cp", 1)
        uo_tr, uo_ev, uo_out = sg("uo_tr", 1), sg("uo_ev", 1), sg("uo_out", 32)
        pooled_ok, y_mm, y_hi, y_lo = sg("pooled_ok", 2), sg("y_mm", 2), sg("y_hi", 2), sg("y_lo", 2)
        b_z, b_min, b_ln, b_max, b_diag = sg("b_z", 6), sg("b_min", 24), sg("b_ln", 24), sg("b_max", 24), sg("b_diag", 24)
        b_tri, b_exp, b_o, b_hi, b_lo = sg("b_tri", 6), sg("b_exp", 24), sg("b_o", 6), sg("b_hi", 6), sg("b_lo", 6)
        i_mm, i_relu, i_sc, i_diag, sel_ok = sg("i_mm", 12), sg("i_relu", 12), sg("i_sc", 12), sg("i_diag", 3), sg("sel_ok", 3)
        q_mm, q_max, q_exp, q_norm = sg("q_mm", 24), sg("q_max", 24), sg("q_exp", 24), sg("q_norm", 24)
        pt_mm, pt_ev, o_mm, o_hi, o_lo = sg("pt_mm", 24), sg("pt_ev", 24), sg("o_mm", 8), sg("o_hi", 8), sg("o_lo", 8)
        d_zero, d_q = sg("d_zero", 1), sg("d_q", 1)
        kp_ld = [sg(f"kp_ld{s}", 48 * len(range(s, NPAGES, 3))) for s in range(3)]
        vp_ld = [sg(f"vp_ld{s}", 32 * 4) for s in range(NPAGES // 4)]
        kt_mm, kt_ev, kq_mm = sg("kt_mm", NPAGES), sg("kt_ev", NPAGES), sg("kq_mm", NPAGES)
        d_new, d_relu, d_rel, d_sum, d_bias = sg("d_new", 1), sg("d_relu", 1), sg("d_rel", 1), sg("d_sum", 1), sg("d_bias", 1)
        d_log, d_max, d_exp, d_nrm, d_ptm, d_pte = sg("d_log", 1), sg("d_max", 2), sg("d_exp", 2), sg("d_nrm", 2), sg("d_ptm", 1), sg("d_pte", 1)
        d_min, d_ln, d_sp, d_tri, d_A = sg("d_min", 1), sg("d_ln", 1), sg("d_sp", 1), sg("d_tri", 1), sg("d_A", 1)
        vp_use, d_hi, d_lo = sg("vp_use", NPAGES), sg("d_hi", 2), sg("d_lo", 2)
        st_ld, st_tr, st_ev, g_zero = sg("st_ld", 16), sg("st_tr", 1), sg("st_ev", 1), sg("g_zero", 1)
        g_ev, g_pre, c_1, c_2, c_3 = sg("g_ev", KF), sg("g_pre", KF), sg("c_1", KF), sg("c_2", KF), sg("c_3", KF)
        s_g, s_mul = sg("s_g", KF), sg("s_mul", KF)
        v_mul, f_hi, f_lo, g_keep = sg("v_mul", KF), sg("f_hi", KF), sg("f_lo", KF), sg("g_keep", KF)
        p_ld, pp_tr, pp_hi, pp_lo = sg("p_ld", 32), sg("pp_tr", 1), sg("pp_hi", 3), sg("pp_lo", 3)
        pr_mm, pr_ev, gt_sig = sg("pr_mm", 6), sg("pr_ev", 8), sg("gt_sig", 8)
        kp_tr, kp_ev, kp_out = sg("kp_tr", 6), sg("kp_ev", 6), sg("kp_out", 32)
        dve_step, act_step = sg("dve_step", 0), sg("act_step", 0)

        held = sg("held", 0)

        ident = con[:, C_ID:C_ID + P]
        ntri, nones, mean = con[:, C_NTRI:C_NTRI + P], con[:, C_NONE:C_NONE + P], con[:, C_ONE:C_ONE + P]
        eps, one = con[:, C_EPS:C_EPS + 1], con[:, C_1:C_1 + 1]
        id_bf, bb_bf, ba_bf = con_bf[:, 0, :], con_bf[:, 1, :], con_bf[:, 2, :]

        def hold(eng):
            eng.sem_inc(held, 1)

        DOWN_BANK = [0, 4, 6, 4]
        SUM_BANK = [6, 6, 2]
        PP_BANK, PROJ_BANK = [0, 1, 4], [0, 4, 6]
        KEEP_BANK = [6, 7, 6, 7, 6, 7]
        SOFT_BANK = [0, 1, 6, 7]
        U_BANK = [(4, 5), (6, 0)]

        def act_at(of, f):
            return of[:, bass.ds(f, 1), :].rearrange("p o n -> p (o n)")

        def halves(ap2):
            return ap2.rearrange("p (h n) -> p h n", h=2)

        def psh(b):
            return ps[:, b:b + 2, 0:HALF]

        def vec(row):
            return vecT[:, row:row + 1]

        def vec_at(row, f):
            return vecT[:, bass.ds(f + row, 1)]

        def ld_value(u):
            return 16 * sum(unit_dmas[u % RAW:u + 1:RAW])

        def unit_cols(u):
            if u < U_U:
                a, b = CHUNK[u // 4]
                return [(0, b - a), (512, 512 + b - a)]
            if U_DOWN <= u < U_PROJ and (u - U_DOWN) % 3 == 2:
                return [(0, DOWN_K[2] * P)]
            return [(0, UNIT)]

        BN = [TP - P * i for i in range(4)]
        BOFF = [0, 512, 896, 1152]
        BPS = [(0, 0), (1, 0), (2, 0), (1, 384)]

        def bz(h, i, c0=0, n=None):
            b, o = BPS[i]
            n = BN[i] - c0 if n is None else n
            return ps[:, 3 * (h % 2) + b, o + c0:o + c0 + n]

        block = ctx.enter_context(nc.Block())
        @block.sync
        def _(sp):
            sp.dma_start(con[:], t_in["con"]).then_inc(con_ld, 16)
            sp.dma_start(pages[:], t_in["page_table"].rearrange("b n -> (b n)").rearrange("(o n) -> o n", o=1)).then_inc(page_ld, 16)
            sp.dma_start(xy[:, 0:4, :], t_in["x_prompt"].rearrange("o (t p) d -> p (o t) d", p=P)).then_inc(x_ld, 16)
            sp.dma_start(xy[0:TS, 4, :], t_in["x_sample"].rearrange("b s d -> (b s) d")).then_inc(x_ld, 16)
            sp.wait_ge(page_ld, 16)
            with sp.Fori(0, LAYERS) as l:
                L = bass.ds(l, 1)

                def at(s, n):
                    return l * per_layer[s.name] + n

                def load_unit(u, i=0, per_turn=0):
                    sp.wait_ge(w_lo, at(w_lo, u + i * per_turn + 1))
                    hold(sp)
                    slot, raw = u % RAW, w_raw[u % RAW]
                    k8 = raw[:, :].rearrange("p (k n) -> p k n", k=8)
                    if u < U_U:
                        a, b = CHUNK[u // 4]
                        src = [(raw[:, :].rearrange("p (k n) -> p k n", k=2)[:, :, 0:b - a],
                                t_in["w_in"][L, 2 * P * (u % 4):2 * P * (u % 4 + 1), a:b].rearrange("o (k p) n -> p (o k) n", p=P))]
                    elif u < U_OUT:
                        c = U0 + P * (u - U_U)
                        src = [(k8, t_in["w_in"][L, :, c:c + P].rearrange("o (k p) n -> p (o k) n", p=P))]
                    elif u < U_UP:
                        m = u - U_OUT
                        w = t_in["w_out"][L, :, m * P:m * P + P]
                        src = [(k8[HD * n:HD * n + HD, 0:3, :],
                                w[:, 3 * HD * n:3 * HD * (n + 1), :].rearrange("o (j p) n -> p (o j) n", p=HD)) for n in range(2)]
                        src.append((k8[:, 3:8, :], w[:, 3 * P:, :].rearrange("o (k p) n -> p (o k) n", p=P)))
                    elif u < U_DOWN:
                        f2, val = (u - U_UP) // 2, (u - U_UP) % 2
                        cols = bass.ds(i * (P * per_turn // 2) + (f2 * P + val * DFF), P)
                        src = [(k8, t_in["w_up"][L, :, cols].rearrange("o (k p) n -> p (o k) n", p=P))]
                    elif u < U_PROJ:
                        m, part_ = divmod(u - U_DOWN, 3)
                        nk = DOWN_K[part_]
                        cols = bass.ds(i * (P * per_turn // 3) + m * P, P)
                        src = [(k8[:, 0:nk, :], t_in["w_down"][L, D * part_:D * part_ + nk * P, cols].rearrange("o (k p) n -> p (o k) n", p=P))]
                    elif u < U_GATE:
                        q = u - U_PROJ
                        src = [(raw[:, :].rearrange("p (k n) -> p k n", k=2),
                                t_in["w_ple_proj"][L, :, 512 * q:512 * q + 512].rearrange("o (k p) n -> p (o k) n", p=P))]
                    else:
                        cols = slice(P * (u - U_GATE), P * (u - U_GATE) + P)
                        src = [(k8, t_in["w_ple_gate"][L, :, cols].rearrange("o (k p) n -> p (o k) n", p=P))]
                    assert len(src) == unit_dmas[u]
                    for to, of in src:
                        sp.dma_start(to, of).then_inc(w_ld[slot], 16)

                sp.wait_ge(w_lo, at(w_lo, 1))
                hold(sp)
                for name, row, n in (("g_attn", V_ATTN, KD), ("g_ffn", V_FFN, KD), ("g_ple", V_PLE, KD),
                                     ("conv_b", V_CB, KF), ("pool_scale", V_PS, 2)):
                    sp.dma_start(vec_raw[row:row + n, :], t_in[name][L, :].rearrange("o (k p) -> (o k) p", p=P)).then_inc(vec_ld, 16)
                sp.dma_start(vec_raw[V_CW:V_CW + 3 * KF, :], t_in["conv_w"][L, :, :].rearrange("o j (k p) -> (o j k) p", p=P)).then_inc(vec_ld, 16)
                for u in range(RAW):
                    load_unit(u)
                sp.wait_ge(h_new, at(h_new, KD))
                sp.dma_start(dcon[:], t_in["dcon"]).then_inc(lay_ld, 16)
                sp.dma_start(gains[:, 0, :], t_in["g_q_a"][L, :].rearrange("o d -> (o d)").partition_broadcast(P)).then_inc(lay_ld, 16)
                sp.dma_start(gains[:, 1, :], t_in["g_k_a"][L, :].rearrange("o d -> (o d)").partition_broadcast(P)).then_inc(lay_ld, 16)
                for m in range(2):
                    sp.dma_start(w_pool[:, m, :], t_in["w_pool"][L, 2 * m:2 * m + 2].rearrange("o h c d -> (o h c) d")).then_inc(lay_ld, 16)
                sp.dma_start(pst_tok[0:NB * 15, :], t_in["state_pool"][L].rearrange("o b r c -> (o b r) c")).then_inc(lay_ld, 16)
                for u in range(RAW, U_OUT + RAW):
                    load_unit(u)
                sp.wait_ge(sel_ok, at(sel_ok, 3))
                hold(sp)

                def load_page(pg, parts):
                    r = sp.value_load(pages[0:1, pg:pg + 1], min_val=0, max_val=NPOOL - 1)
                    for name, inner, to, landed in parts:
                        sp.dma_start(to, t_in[name][L, bass.ds(r, 1)].rearrange(f"o a p {inner} -> (o a p) {'(n d)' if inner == 'n d' else 'd'}")).then_inc(landed, 16)

                for pg in range(NPAGES + 3):
                    if pg < NPAGES:
                        if pg >= 3:
                            sp.wait_ge(kt_mm, at(kt_mm, pg - 2))
                            hold(sp)
                        k, landed = KP[:, pg % 3, :], kp_ld[pg % 3]
                        load_page(pg, [("cache_a_k", "n d", k[:, 0:128], landed), ("cache_b_k", "n d", k[:, 128:512], landed),
                                       ("cache_idx_k", "d", k[:, 512:576], landed)])
                    if pg == 3:
                        sp.wait_ge(y_hi, at(y_hi, 2))
                        hold(sp)
                        sp.wait_ge(y_lo, at(y_lo, 2))
                        hold(sp)
                        sp.wait_ge(uo_out, at(uo_out, 32))
                        hold(sp)
                    if pg >= 3:
                        v, landed = VP[:, pg - 3, :], vp_ld[(pg - 3) // 4]
                        load_page(pg - 3, [("cache_a_v", "n d", v[:, 0:128], landed), ("cache_b_v", "n d", v[:, 128:512], landed)])
                sp.wait_ge(d_hi, at(d_hi, 2))
                hold(sp)
                sp.wait_ge(d_lo, at(d_lo, 2))
                hold(sp)
                sp.dma_start(st_tok[:], t_in["state_conv"][L].rearrange("o b r c -> (o b r) c")).then_inc(st_ld, 16)
                for u in range(U_OUT + RAW, U_UP):
                    load_unit(u)
                with sp.Fori(0, KF // 2) as i:
                    for j in range(4):
                        load_unit(U_UP + j, i, 4)
                with sp.Fori(0, 2) as i:
                    for j in range(12):
                        load_unit(U_DOWN + j, i, 12)
                for u in range(U_PROJ, U_PROJ + RAW):
                    load_unit(u)
                sp.wait_ge(w_used, at(w_used, SPLIT + U_PROJ))
                hold(sp)
                sp.dma_start(p_tok[:, 0:4, :], t_in["p_prompt"][L].rearrange("o b (t p) c -> p (o b t) c", p=P)).then_inc(p_ld, 16)
                sp.dma_start(p_tok[0:TS, 4, :], t_in["p_sample"][L].rearrange("o b s c -> (o b s) c")).then_inc(p_ld, 16)
                for u in range(U_PROJ + RAW, UNITS):
                    load_unit(u)
                sp.wait_ge(kp_out, at(kp_out, 32))
                hold(sp)
                sp.wait_ge(kv_out, at(kv_out, 10 * 16))
                hold(sp)
            for t in range(TILES):
                sp.wait_ge(y_ev, 2 * t + 2)
                if t < 4:
                    sp.dma_start(t_out["y_prompt"][0, P * t:P * t + P, :], xy[:, t, :]).then_inc(y_out, 16)
                else:
                    sp.dma_start(t_out["y_sample"].rearrange("b s d -> (b s) d"), xy[0:TS, 4, :]).then_inc(y_out, 16)
            sp.wait_ge(y_out, 16 * TILES)

        @block.gpsimd
        def _(pool):
            with pool.Fori(0, LAYERS) as l:
                L = bass.ds(l, 1)

                def at(s, n):
                    return l * per_layer[s.name] + n

                def store(name, t, inner, src, landed):
                    if t < 4:
                        to = t_out[name + "_p"][L, 0, P * t:P * t + P].rearrange(f"o p {inner} -> (o p) {'(n d)' if inner == 'n d' else 'd'}")
                    else:
                        to = t_out[name + "_s"][L].rearrange(f"o b s {inner} -> (o b s) {'(n d)' if inner == 'n d' else 'd'}")
                    pool.dma_start(to, src[0:TOKW[t]]).then_inc(landed, 16)

                pool.wait_ge(h_new, at(h_new, KD))
                hold(pool)
                pool.memset(u_p[:, :, 0:15], 0.0).then_inc(u_zero, 1)
                for t in range(TILES):
                    pool.wait_ge(rope_ok, at(rope_ok, t + 1))
                    hold(pool)
                    store("a_k", t, "n d", r_tok[:, t, 384:512], ak_out)
                for t in range(TILES):
                    pool.wait_ge(p_ev, at(p_ev, 5 + t + 1))
                    hold(pool)
                    store("a_v", t, "n d", V[:, t, 0:128], kv_out)
                    pool.wait_ge(rope_ok, at(rope_ok, 5 + t + 1))
                    hold(pool)
                    store("idx_k", t, "d", r_tok[:, t, 256:320], ix_out)
                def causal(t):
                    pool.wait_ge(i_sc, at(i_sc, 4 * t))
                    hold(pool)
                    blk = score[:, (t - 1) % 2, P * t:P * t + P]
                    pool.affine_select(out=blk, in_=blk, compare_op=ALU.is_ge, fill=MASKED, base=0,
                                       pattern=[[-1, P]], channel_multiplier=1).then_inc(i_diag, 1)

                for t in range(TILES):
                    pool.wait_ge(plain_ok, at(plain_ok, 5 + t + 1))
                    hold(pool)
                    store("b_k", t, "n d", r_tok[:, t, 0:384], bk_out)
                causal(1)
                for t in range(TILES):
                    pool.wait_ge(p_ev, at(p_ev, 10 + t + 1))
                    hold(pool)
                    store("b_v", t, "n d", V[:, t, 128:512], kv_out)
                causal(2)
                pool.wait_ge(uo_ev, at(uo_ev, 1))
                hold(pool)
                pool.dma_start(t_out["pool_s"][L].rearrange("o b r c -> (o b r) c"), u_tok[0:NB * 15, 0:256]).then_inc(uo_out, 16)
                pool.dma_start(t_out["pool_p"][L, 0].rearrange("o r c -> (o r) c"), u_tok[0:15, 256:512]).then_inc(uo_out, 16)

                def diag(h):
                    for i in range(4):
                        pool.wait_ge(b_max, at(b_max, 4 * h + i + 1))
                        hold(pool)
                        blk = Lb[:, h % 2, BOFF[i]:BOFF[i] + P]
                        pool.tensor_tensor(blk, blk, con[:, C_M01:C_M01 + P], ALU.mult).then_inc(b_diag, 1)

                diag(0)
                diag(1)
                causal(3)
                for h in range(6):
                    if h + 2 < 6:
                        diag(h + 2)
                pool.wait_ge(y_hi, at(y_hi, 2))
                hold(pool)
                pool.wait_ge(y_lo, at(y_lo, 2))
                hold(pool)
                pool.wait_ge(uo_out, at(uo_out, 32))
                hold(pool)
                pool.memset(qim[:], 0.0)
                pool.memset(qbm[:], 0.0)
                pool.memset(qam[:], 0.0).then_inc(d_zero, 1)
                pool.wait_ge(d_hi, at(d_hi, 2))
                hold(pool)
                pool.wait_ge(d_lo, at(d_lo, 2))
                hold(pool)
                pool.memset(G[:, :, 0:2], 0.0).then_inc(g_zero, 1)
                pool.wait_ge(st_ev, at(st_ev, 1))
                hold(pool)

                with pool.Fori(0, KF // 2) as i:
                    for slot in range(2):
                        f = 2 * i + slot
                        g_s = G[:, slot, 2 + TP:].rearrange("p (b s) -> p b s", s=6)
                        pool.wait_ge(v_mul, at(v_mul, f + 1))
                        hold(pool)
                        pool.tensor_copy(g_s[:, :, 0:2], stT[:, bass.ds(f, 1), :].rearrange("p o (b s) -> p (o b) s", s=2)).then_inc(g_pre, 1)
                        pool.wait_ge(g_ev, at(g_ev, f + 1))
                        hold(pool)
                        kf = keepT[:, bass.ds(f, 1), :].rearrange("p o n -> p (o n)")
                        pool.tensor_copy(kf[:, 0:2], G[:, slot, TP:TP + 2])
                        pool.tensor_copy(kf[:, 2:18].rearrange("p (b s) -> p b s", s=2), g_s[:, :, 4:6]).then_inc(g_keep, 1)
                pool.wait_ge(kp_ev, at(kp_ev, 6))
                hold(pool)
                pool.dma_start(t_out["conv_p"][L, 0].rearrange("o r c -> (o r) c"), keep_tok[0:2, :]).then_inc(kp_out, 16)
                pool.dma_start(t_out["conv_s"][L].rearrange("o b r c -> (o b r) c"), keep_tok[2:18, :]).then_inc(kp_out, 16)
                pool.wait_ge(kv_out, at(kv_out, 10 * 16))
                hold(pool)
                pool.wait_ge(kp_out, at(kp_out, 32))
                hold(pool)

        @block.scalar
        def _(act):
            with act.Fori(0, LAYERS) as l:
                steps = Steps(l, ACT_STEPS)

                def at(s, n):
                    return l * per_layer[s.name] + n

                def copy(out, in_, scale=1.0):
                    return act.activation(out, in_, ACT.Copy, scale=scale)

                def split(u, i=0, per_turn=0):
                    n = u + i * per_turn
                    act.wait_ge(w_ld[u % RAW], at(w_ld[u % RAW], (per_turn // RAW * 16) * i + ld_value(u)))
                    act.wait_ge(w_used, at(w_used, n + 1))
                    cols = unit_cols(u)
                    for a, b in cols:
                        ins = copy(w_H[u % SPLIT][:, a:b], w_raw[u % RAW][:, a:b])
                    ins.then_inc(w_hi, 1)

                def square(n, slot, h, turn=0, reused=True):
                    act.wait_ge(h_new, at(h_new, turn + n + 1))
                    if reused:
                        act.wait_ge(n_ss, at(n_ss, turn + n - 1))
                    act.activation(a_tmp[:, slot, :], h, ACT.Square).then_inc(n_sq, 1)

                def inverse(out, mean_sq, scale=1.0):
                    act.activation(out, mean_sq, ACT.Ln, bias=eps, scale=scale).then_inc(act_step, steps.step())
                    act.wait_ge(act_step, steps.value())
                    return act.activation(out, out, ACT.Exp, scale=-0.5)

                def root(i):
                    act.wait_ge(n_ss, at(n_ss, 8 * i + 8))
                    inverse(halves(r_all[:, :]), psh(SUM_BANK[i])).then_inc(n_rec, 1)

                def normed_hi(i, k0=0, k1=KD):
                    for k in range(k0, k1):
                        act.wait_ge(a_t, at(a_t, 8 * i + k + 1))
                        copy(aH[:, k, :], a_tmp[:, k % 2, :]).then_inc(a_hi, 1)

                act.wait_ge(vec_tr, at(vec_tr, 1))
                copy(vecT[:, :], ps[:, 0, 0:NV]).then_inc(vec_ev, 1)
                split(0)
                split(1)
                for k in range(KD):
                    square(k, k % 2, hT[:, k, :], reused=k >= 2)
                root(0)
                normed_hi(0)

                def relu(t, e0, e1):
                    for e in range(e0, e1):
                        n = 4 * (t - 1) + e
                        act.wait_ge(i_mm, at(i_mm, n + 1))
                        if n >= 2:
                            act.wait_ge(i_sc, at(i_sc, n - 1))
                        act.activation(relu_s[:, n % 2, 0:P * (t + 1)], ps[:, 7, 0:P * (t + 1)], ACT.Relu,
                                       scale=0.125).then_inc(i_relu, 1)

                for c in range(5):
                    for j in range(4):
                        u = 4 * c + j
                        if c >= 3 and j in (0, 2):
                            relu(c - 2, j, 2 if j == 0 else 3)
                        if c >= 1:
                            for t in range(TILES):
                                if GROUP_K[t] // 2 != j:
                                    continue
                                g, n = 5 * (c - 1) + t, TOKW[t]
                                f0, nb = CH_BLOCKS[c - 1]
                                act.wait_ge(t_mm, at(t_mm, g + 1))
                                out = featT[:, f0:f0 + nb, P * t:P * t + n]
                                in_ = ps[:, 7, 0:nb * P].rearrange("p (b q) -> p b q", q=P)[:, :, 0:n]
                                copy(out, in_, 0.125 if c == 3 else 1.0).then_inc(t_ev, 1)
                        if c >= 3 and j == 3:
                            relu(c - 2, 3, 4)
                        if j < 3:
                            split(u + 2)
                    width = CHUNK[c][1] - CHUNK[c][0]
                    for t in range(TILES):
                        i, n = 5 * c + t, TOKW[t]
                        if t < 4:
                            act.wait_ge(p_mm, at(p_mm, 4 * c + t + 1))
                        else:
                            act.wait_ge(w_used, at(w_used, 4 * c + 3 + SPLIT + 1))
                        src = ps[0:n, i % 7, :]
                        if c == 0:
                            copy(x_tok[0:n, t, :], src).then_inc(p_ev, 1)
                        elif c == 1:
                            act.wait_ge(rope_ok, at(rope_ok, t + 1))
                            copy(V[0:n, t, 0:128], src[:, 0:128])
                            copy(x_tok[0:n, t, 0:324], src[:, 128:452]).then_inc(p_ev, 1)
                        elif c == 2:
                            act.wait_ge(t_mm, at(t_mm, 5 + t + 1))
                            act.wait_ge(ix_out, at(ix_out, 5 * 16))
                            copy(r_tok[0:n, t, 0:384], src[:, 0:384]).then_inc(plain_ok, 1)
                        elif c == 3:
                            act.wait_ge(t_mm, at(t_mm, 10 + t + 1))
                            copy(r_tok[0:n, t, 0:384], src[:, 0:384]).then_inc(plain_ok, 1)
                        else:
                            copy(V[0:n, t, 128:512], src[:, 0:384]).then_inc(p_ev, 1)
                    split(4 * c + 5)
                    if c == 0:
                        act.wait_ge(hs_ss, at(hs_ss, 1))
                        inverse(hstat[:, :, :], hstat[:, :, :]).then_inc(hs_rec, 1)
                act.wait_ge(ph_tr, at(ph_tr, 1))
                for m in range(2):
                    ins = copy(u_s[:, m, :, 0:15], ps[:, 7, 128 * m:128 * m + 120].rearrange("p (b r) -> p b r", r=15))
                ins.then_inc(ph_ev, 1)
                for m in range(2):
                    act.wait_ge(w_used, at(w_used, U_U + m + SPLIT + 1))
                    b = U_BANK[m]
                    copy(u_p[:, m, 15:15 + HALF], ps[:, b[0], 0:HALF])
                    copy(u_p[:, m, 15 + HALF:15 + TP], ps[:, b[1], 0:TP - HALF])
                    copy(u_s[:, m, :, 15:19], ps[:, b[1], TP - HALF:HALF].rearrange("p (b s) -> p b s", s=NS)).then_inc(u_ev, 1)
                    split(U_U + m + 2)

                def softplus(h):
                    first = steps.n
                    for i in range(4):
                        blk = Lb[:, h % 2, BOFF[i]:BOFF[i] + BN[i]]
                        act.wait_ge(b_min, at(b_min, 4 * h + i + 1))
                        act.activation(blk, blk, ACT.Exp).then_inc(act_step, steps.step())
                    for i in range(4):
                        blk = Lb[:, h % 2, BOFF[i]:BOFF[i] + BN[i]]
                        act.wait_ge(act_step, steps.value(first + i + 1))
                        act.activation(blk, blk, ACT.Ln, bias=one).then_inc(b_ln, 1)

                for h in range(2):
                    relu(3, h, h + 1)
                    softplus(h)
                relu(3, 2, 4)
                for h in range(6):
                    act.wait_ge(b_tri, at(b_tri, h + 1))
                    if h >= 1:
                        act.wait_ge(b_o, at(b_o, h))
                    for i in range(4):
                        act.activation(Ab[:, BOFF[i]:BOFF[i] + BN[i]], bz(h, i), ACT.Exp).then_inc(b_exp, 1)
                    if h + 2 < 6:
                        softplus(h + 2)
                    half = slice(HD * (h % 2), HD * (h % 2) + HD)
                    act.wait_ge(b_o, at(b_o, h + 1))
                    copy(aH[half, 3 + h // 2, 0:TP], ps[half, 6, :]).then_inc(b_hi, 1)

                for m in range(24 + 2):
                    if m < 24:
                        t = m // 6
                        W = P * (t + 1)
                        act.wait_ge(q_max, at(q_max, m + 1))
                        if m >= SOFT:
                            act.wait_ge(pt_mm, at(pt_mm, m - SOFT + 1))
                        act.activation(prob[:, m % SOFT, 0:W], ps[:, SOFT_BANK[m % SOFT], 0:W], ACT.Exp, bias=stat[:, m % SOFT, 1:2],
                                       scale=0.125, accum_out=stat[:, m % SOFT, 2:3]).then_inc(q_exp, 1)
                    c = m - 2
                    if c >= 0:
                        t, g, j = c // 6, c // 3, c % 3
                        act.wait_ge(pt_mm, at(pt_mm, c + 1))
                        if j == 0 and g >= 1:
                            act.wait_ge(o_mm, at(o_mm, g))
                        copy(probT[:, 0:t + 1, j, :], ps[:, 2 + c % 2, 0:P * (t + 1)].rearrange("p (b q) -> p b q", q=P)).then_inc(pt_ev, 1)
                    if c >= 3 and c % 3 == 0 or c == 23:
                        g = c // 3 if c == 23 else c // 3 - 1
                        n = g % 2
                        half = slice(HD * n, HD * n + HD)
                        act.wait_ge(o_mm, at(o_mm, g + 1))
                        copy(aH[half, 0:3, P * (g // 2):P * (g // 2) + P],
                             ps[half, 4 + n, 0:384].rearrange("p (j q) -> p j q", q=P)).then_inc(o_hi, 1)

                for m in range(2):
                    act.wait_ge(y_mm, at(y_mm, m + 1))
                    act.activation(halves(aH[:, 6 + m, :]), psh(2 * m), ACT.Copy, scale=vec(V_PS + m)).then_inc(y_hi, 1)

                for pg in range(NPAGES):
                    act.wait_ge(kt_mm, at(kt_mm, pg + 1))
                    if pg == 0:
                        act.wait_ge(y_lo, at(y_lo, 2))
                    if pg >= 2:
                        act.wait_ge(kq_mm, at(kq_mm, pg - 1))
                    copy(KT[0:HD, pg % 2, 512:640], ps[0:HD, 7 - 3 * (pg % 2), 0:128])
                    copy(KT[:, pg % 2, 0:512], ps[:, 5 + pg % 2, :]).then_inc(kt_ev, 1)
                act.wait_ge(d_new, at(d_new, 1))
                act.activation(rel_d[:, :], ps[:, 0, 0:KEYS_S], ACT.Relu, scale=0.125).then_inc(d_relu, 1)
                act.wait_ge(d_min, at(d_min, 1))
                act.activation(L_d[:, :], L_d[:, :], ACT.Exp).then_inc(act_step, steps.step())
                act.activation(L_n[:, :], L_n[:, :], ACT.Exp).then_inc(act_step, steps.step())
                act.wait_ge(act_step, steps.value())
                act.activation(L_d[:, :], L_d[:, :], ACT.Ln, bias=one)
                act.activation(L_n[:, :], L_n[:, :], ACT.Ln, bias=con[0:TS, C_1:C_1 + 1]).then_inc(d_ln, 1)
                act.wait_ge(d_tri, at(d_tri, 1))
                act.activation(A_d[:, :], ps[:, 3, 0:384], ACT.Exp)
                act.activation(A_n[:, :], ps[0:TS, 4, 0:192], ACT.Exp).then_inc(d_A, 1)
                for n in range(2):
                    act.wait_ge(d_max, at(d_max, n + 1))
                    act.activation(P_d[:, n, :], ps[0:96, 1 + n, 0:KEYS_S], ACT.Exp, bias=st_d[:, n, 1:2], scale=0.125,
                                   accum_out=st_d[:, n, 2:3]).then_inc(d_exp, 1)
                act.wait_ge(d_ptm, at(d_ptm, 1))
                for n in range(2):
                    copy(PT_d[:, n, 0:2, :], ps[:, 5 + n, 0:192].rearrange("p (b q) -> p b q", q=96))
                    ins = copy(PT_d[0:TS, n, 2, :], ps[0:TS, 5 + n, 192:288])
                ins.then_inc(d_pte, 1)
                act.wait_ge(vp_use, at(vp_use, NPAGES))
                for n in range(2):
                    copy(aH[:, 3 * n:3 * n + 3, TP:T], ps[:, 3 * n, 0:96].rearrange("p (j q) -> p j q", q=TS)).then_inc(d_hi, 1)

                for m in range(KD):
                    split(U_OUT + m + 2)
                    square(KD + m, m % 2, hT[:, m, :])
                root(1)
                act.wait_ge(st_tr, at(st_tr, 1))
                copy(stT[:, :, :], ps[:, 5, 0:KF * 2 * NB].rearrange("p (f b) -> p f b", b=2 * NB)).then_inc(st_ev, 1)
                normed_hi(1)

                def ffn(slot, f, k, uo, i=0, per_turn=0):
                    split(U_UP + uo + 2, i, per_turn)
                    b = 4 * slot
                    act.wait_ge(w_used, at(w_used, 2 * f + U_UP + SPLIT + 1))
                    act.wait_ge(g_pre, at(g_pre, f + 1))
                    copy(G[:, slot, 2:2 + HALF], ps[:, b, 0:HALF])
                    copy(G[:, slot, 2 + HALF:2 + TP], ps[:, b + 1, 0:TP - HALF])
                    g_s = G[:, slot, 2 + TP:].rearrange("p (b s) -> p b s", s=6)
                    copy(g_s[:, :, 2:6], ps[:, b + 1, TP - HALF:HALF].rearrange("p (b s) -> p b s", s=NS)).then_inc(g_ev, 1)
                    act.wait_ge(g_ev, at(g_ev, f + 1))
                    act.activation(Cv[:, slot, :], G[:, slot, 0:GW - 2], ACT.Identity, bias=vec_at(V_CB, f),
                                   scale=vec_at(V_CW, f)).then_inc(c_1, 1)
                    act.wait_ge(c_3, at(c_3, f + 1))
                    act.wait_ge(g_keep, at(g_keep, f + 1))
                    act.activation(G[:, slot, 2:GW], Cv[:, slot, :], ACT.Sigmoid).then_inc(s_g, 1)
                    split(U_UP + uo + 3, i, per_turn)
                    act.wait_ge(v_mul, at(v_mul, f + 3))
                    copy(act_at(actH, f), a_tmp[:, slot, :]).then_inc(f_hi, 1)

                act.wait_ge(g_zero, at(g_zero, 1))
                with act.Fori(0, KF // 2) as i:
                    for j in range(2):
                        ffn(j, 2 * i + j, j, 2 * j, i, 4)
                with act.Fori(0, 2) as i:
                    for j in range(12):
                        split(U_DOWN + j + 2, i, 12)
                        if j % 3 == 2:
                            square(2 * KD + j // 3, j // 3 % 2, hT[:, bass.ds(4 * i + j // 3, 1), :].rearrange("p o n -> p (o n)"), 4 * i)

                root(2)
                act.wait_ge(pp_tr, at(pp_tr, 1))
                for b in range(3):
                    nt = 2 if b < 2 else 1
                    n = nt * P if b < 2 else TS
                    src = ps[:, PP_BANK[b], 0:nt * 256].rearrange("p (t k q) -> p k t q", k=2, q=P)
                    if b < 2:
                        ins = copy(pH[:, :, 256 * b:256 * b + 256].rearrange("p k (t q) -> p k t q", q=P), src)
                    else:
                        ins = copy(pH[:, :, TP:T], ps[:, PP_BANK[b], 0:256].rearrange("p (k q) -> p k q", q=P)[:, :, 0:TS])
                    ins.then_inc(pp_hi, 1)
                for q in range(2):
                    for mm in range(4):
                        m = 4 * q + mm
                        if mm < 3:
                            act.wait_ge(pr_mm, at(pr_mm, 3 * q + mm + 1))
                        else:
                            act.wait_ge(w_used, at(w_used, U_PROJ + q + SPLIT + 1))
                        copy(halves(projT[:, m, :]), psh(PROJ_BANK[m % 3])).then_inc(pr_ev, 1)
                        normed_hi(2, m, m + 1)
                    split(U_PROJ + q + 2)
                for m in range(KD):
                    if m + 2 < KD:
                        split(U_GATE + m + 2)
                    act.wait_ge(w_used, at(w_used, U_GATE + m + SPLIT + 1))
                    if m >= 2:
                        act.wait_ge(h_new, at(h_new, 3 * KD + m - 1))
                    act.activation(halves(sig[:, m % 2, :]), psh(2 * (m % 3)), ACT.Sigmoid).then_inc(gt_sig, 1)
                assert steps.n == ACT_STEPS, steps.n

        @block.vector
        def _(dve):

            dve.sem_inc(w_lo, RAW)
            dve.sem_inc(v_mul, 2)
            dve.wait_ge(con_ld, 16)
            dve.tensor_copy(con_bf[:, 0, :], ident)
            for j in range(3):
                dve.tensor_copy(id3_bf[:, TS * j:TS * j + TS], con[0:TS, C_ID:C_ID + TS])
            dve.tensor_scalar(con_bf[:, 3, :], ident, 0.0, None, ALU.mult)
            dve.tensor_copy(con_bf[:, 1, :], con[:, C_BB:C_BB + P])
            dve.tensor_copy(con_bf[:, 2, :], con[:, C_BA:C_BA + P]).then_inc(con_cast, 1)
            for t in range(TILES):
                for b in range(2):
                    i, n = 2 * t + b, TOKW[t]
                    dve.wait_ge(emb_tr, i + 1)
                    ins = dve.tensor_copy(hT[:, 4 * b:4 * b + 4, P * t:P * t + n],
                                          ps[:, i % 8, :].rearrange("p (k q) -> p k q", q=P)[:, :, 0:n])
                    ins.then_inc((emb_ev if i < 2 else h_new), 1)
            with dve.Fori(0, LAYERS) as l:
                steps = Steps(l, DVE_STEPS)

                def at(s, n):
                    return l * per_layer[s.name] + n

                def split(u, i=0, per_turn=0):
                    dve.wait_ge(w_hi, at(w_hi, u + i * per_turn + 1))
                    for a, b in unit_cols(u):
                        ins = dve.tensor_tensor(w_L[u % SPLIT][:, a:b], w_raw[u % RAW][:, a:b],
                                                w_H[u % SPLIT][:, a:b].bitcast(F32), ALU.subtract)
                    ins.then_inc(w_lo, 1)

                def lo(out, full, hi):
                    return dve.tensor_tensor(out, full, hi.bitcast(F32), ALU.subtract)

                def norm(i):
                    dve.wait_ge(n_rec, at(n_rec, i + 1))
                    for k in range(KD):
                        if k >= 2:
                            dve.wait_ge(a_lo, at(a_lo, 8 * i + k - 1))
                        dve.scalar_tensor_tensor(a_tmp[:, k % 2, :], hT[:, k, :], vec((V_ATTN, V_FFN, V_PLE)[i] + k), r_all[:, :],
                                                 ALU.mult, ALU.mult).then_inc(a_t, 1)
                        if k >= 1:
                            dve.wait_ge(a_hi, at(a_hi, 8 * i + k))
                            lo(aL[:, k - 1, :], a_tmp[:, (k - 1) % 2, :], aH[:, k - 1, :]).then_inc(a_lo, 1)
                        if i == 2 and k == 5:
                            split(U_PROJ + 2)
                    dve.wait_ge(a_hi, at(a_hi, 8 * i + 8))
                    lo(aL[:, 7, :], a_tmp[:, 1, :], aH[:, 7, :]).then_inc(a_lo, 1)

                split(0)
                split(1)
                dve.wait_ge(vec_ev, at(vec_ev, 1))
                norm(0)
                dve.memset(hstat[:, :, :], 1.0).then_inc(hs_one, 1)
                dve.wait_ge(lay_ld, at(lay_ld, 6 * 16))

                def head_squares(t):
                    n = TOKW[t]
                    dve.wait_ge(p_ev, at(p_ev, t + 1))
                    dve.scalar_tensor_tensor(t1[0:n, :], x_tok[0:n, t, :], 1.0 / HD, x_tok[0:n, t, :], ALU.mult, ALU.mult).then_inc(dve_step, steps.step())
                    dve.wait_ge(dve_step, steps.value())
                    total = dve.tensor_reduce(hstat[0:n, t, :], t1[0:n, :].rearrange("p (h d) -> p h d", d=HD), AX.X, ALU.add)
                    if t < TILES - 1:
                        total.then_inc(dve_step, steps.step())
                        dve.wait_ge(dve_step, steps.value())
                    else:
                        total.then_inc(hs_ss, 1)

                def rotate(t, heads, parts):
                    n = TOKW[t]
                    w = heads * HD
                    if (heads, t) != (8, 0):
                        dve.wait_ge(rope_ok, at(rope_ok, t if heads == 8 else 5 + t))
                    x = x_tok[0:n, t, 0:w].rearrange("p (h d) -> p h d", d=HD)
                    cs = dcon[0:n, D_COS + 64 * t:D_COS + 64 * t + 64].unsqueeze(1).to_broadcast([n, heads, HD])
                    sn = dcon[0:n, D_SIN + 64 * t:D_SIN + 64 * t + 64].unsqueeze(1)
                    a = t1[0:n, 0:w].rearrange("p (h d) -> p h d", d=HD)
                    b = t2[0:n, 0:w].rearrange("p (h d) -> p h d", d=HD)
                    dve.tensor_tensor(a, x, cs, ALU.mult)
                    dve.tensor_tensor(b[:, :, 0:32], x[:, :, 32:64], sn[:, :, 0:32].to_broadcast([n, heads, 32]), ALU.mult)
                    dve.tensor_tensor(b[:, :, 32:64], x[:, :, 0:32], sn[:, :, 32:64].to_broadcast([n, heads, 32]), ALU.mult).then_inc(dve_step, steps.step())
                    dve.wait_ge(dve_step, steps.value())
                    for out, a0, a1, order in parts:
                        i0, i1 = t1[0:n, a0:a1], t2[0:n, a0:a1]
                        if order:
                            i0, i1 = (v.rearrange("p (n j d) -> p n j d", n=2, j=3) for v in (i0, i1))
                            out = out.rearrange("p (j n d) -> p n j d", n=2, j=3)
                        ins = dve.tensor_tensor(out, i0, i1, ALU.add)
                    ins.then_inc(rope_ok, 1)

                def qk(t):
                    n = TOKW[t]
                    x = x_tok[0:n, t, :].rearrange("p (h d) -> p h d", d=HD)
                    dve.tensor_tensor(x, x, hstat[0:n, t, :].unsqueeze(2).to_broadcast([n, 8, HD]), ALU.mult).then_inc(dve_step, steps.step())
                    dve.wait_ge(dve_step, steps.value())
                    dve.tensor_tensor(x[:, 0:6, :], x[:, 0:6, :], gains[0:n, 0, :].unsqueeze(1).to_broadcast([n, 6, HD]), ALU.mult)
                    dve.tensor_tensor(x[:, 6:8, :], x[:, 6:8, :], gains[0:n, 1, :].unsqueeze(1).to_broadcast([n, 2, HD]), ALU.mult).then_inc(dve_step, steps.step())
                    dve.wait_ge(dve_step, steps.value())
                    rotate(t, 8, [(r_tok[0:n, t, 0:384], 0, 384, True), (r_tok[0:n, t, 384:512], 384, 512, False)])

                def index(t):
                    n = TOKW[t]
                    dve.wait_ge(t_mm, at(t_mm, t + 1))
                    if t == 0:
                        dve.wait_ge(ak_out, at(ak_out, 5 * 16))
                    dve.tensor_scalar(wi[0:n, t, :], x_tok[0:n, t, 320:324], 0.5, None, ALU.mult)
                    rotate(t, 5, [(r_tok[0:n, t, 0:320], 0, 320, False), (r_tok[0:n, t, 320:384], 256, 320, False)])

                def weigh(t, e0, e1):
                    W = P * (t + 1)
                    sc = score[:, (t - 1) % 2, 0:W]
                    for e in range(e0, e1):
                        n = 4 * (t - 1) + e
                        dve.wait_ge(i_relu, at(i_relu, n + 1))
                        if e == 0:
                            ins = dve.tensor_scalar(sc, relu_s[:, n % 2, 0:W], wi[:, t, 0:1], None, ALU.mult)
                        else:
                            dve.wait_ge(i_sc, at(i_sc, n))
                            ins = dve.scalar_tensor_tensor(sc, relu_s[:, n % 2, 0:W], wi[:, t, e:e + 1], sc, ALU.mult, ALU.add)
                        ins.then_inc(i_sc, 1)

                def select(t, r0, r1):
                    sc = score[:, (t - 1) % 2, 0:P * (t + 1)]
                    if r0 == r1:
                        return
                    if r0 == 0:
                        dve.wait_ge(i_diag, at(i_diag, t))
                    hold(dve)
                    for _ in range(r0, r1):
                        dve.max(m8[:, :], sc).then_inc(dve_step, steps.step())
                        dve.wait_ge(dve_step, steps.value())
                        hold(dve)
                        dve.match_replace(sc, m8[:, :], sc, TAKEN).then_inc(dve_step, steps.step())
                        dve.wait_ge(dve_step, steps.value())
                        hold(dve)
                    if r1 == ROUNDS:
                        dve.tensor_scalar(bias_p[:, t - 1, 0:P * (t + 1)], sc, CUT, NEG, ALU.is_gt, ALU.mult).then_inc(sel_ok, 1)

                for c in range(5):
                    for j in range(4):
                        if c >= 3 and j in (0, 2):
                            weigh(c - 2, j, 2 if j == 0 else 3)
                        if c == 4 and j >= 1:
                            select(1, 4 * (j - 1), 4 * j)
                        if c == 1:
                            for t in ((0,), (1,), (2,), (3, 4))[j]:
                                qk(t)
                        if c == 2:
                            for t in ((0,), (1,), (2,), (3, 4))[j]:
                                dve.wait_ge(p_ev, at(p_ev, 5 + t + 1))
                                index(t)
                        if j < 3:
                            split(4 * c + j + 2)
                    if c == 0:
                        dve.wait_ge(hs_one, at(hs_one, 1))
                        for t in range(TILES):
                            head_squares(t)
                    split(4 * c + 5)
                    if c >= 3:
                        weigh(c - 2, 3, 4)
                    if c == 0:
                        dve.wait_ge(hs_rec, at(hs_rec, 1))
                select(1, 12, 16)
                split(U_OUT)
                split(U_OUT + 1)
                dve.wait_ge(u_ev, at(u_ev, 2))
                dve.wait_ge(ph_ev, at(ph_ev, 1))
                for m in range(2):
                    ins = dve.tensor_copy(u_c[:, m, :].rearrange("p (b r) -> p b r", r=15), u_s[:, m, :, NS:])
                ins.then_inc(u_cp, 1)
                dve.wait_ge(uo_tr, at(uo_tr, 1))
                dve.tensor_copy(u_tok[0:NB * 15, 0:256], ps[0:NB * 15, 7, 0:256])
                dve.tensor_copy(u_tok[0:15, 256:512], ps[0:15, 7, 256:512]).then_inc(uo_ev, 1)

                def pool_means(m):
                    UN = 15 + TP
                    if m:
                        dve.wait_ge(pooled_ok, at(pooled_ok, m))
                    dve.wait_ge(u_ev, at(u_ev, m + 1))
                    dve.wait_ge(ph_ev, at(ph_ev, 1))
                    dve.wait_ge(u_zero, at(u_zero, 1))
                    up, us = u_p[:, m, :], u_s[:, m, :, :]

                    def view(x):
                        return x[:, 0:UN], x[:, UN:].rearrange("p (b r) -> p b r", r=19)

                    src = (up, us)
                    for s in range(2 * m + 2):
                        sh = 1 << s
                        dst = view(pw[s % 2])
                        keep_low = s == 2 * m + 1
                        rows = slice(HD, P) if keep_low else slice(0, P)
                        dve.tensor_tensor(dst[0][rows, 2 * sh - 1:], src[0][rows, 2 * sh - 1:], src[0][rows, sh - 1:UN - sh], ALU.add)
                        dve.tensor_tensor(dst[1][rows, :, 2 * sh - 1:], src[1][rows, :, 2 * sh - 1:], src[1][rows, :, sh - 1:19 - sh], ALU.add).then_inc(dve_step, steps.step())
                        dve.wait_ge(dve_step, steps.value())
                        low, src = src, dst
                    for rows, s2 in ((slice(0, HD), low), (slice(HD, P), src)):
                        dve.scalar_tensor_tensor(pooled[rows, m, 0:TP], s2[0][rows, 15:], con[rows, C_INVW + m:C_INVW + m + 1],
                                                 up[rows, 15:], ALU.mult, ALU.subtract)
                        dve.tensor_tensor(first16[rows, :], s2[0][rows, 15:31],
                                          con[rows, C_INV16 + 16 * m:C_INV16 + 16 * m + 16], ALU.mult).then_inc(dve_step, steps.step())
                        dve.scalar_tensor_tensor(pooled[rows, m, TP:].rearrange("p (b s) -> p b s", s=NS), s2[1][rows, :, 15:],
                                                 con[rows, C_INVW + m:C_INVW + m + 1], us[rows, :, 15:], ALU.mult, ALU.subtract).then_inc(dve_step, steps.step())
                        dve.wait_ge(dve_step, steps.value())
                        ins = dve.tensor_tensor(pooled[rows, m, 0:16], first16[rows, :], up[rows, 15:31], ALU.subtract)
                    ins.then_inc(pooled_ok, 1)

                def clamp(h):
                    dve.wait_ge(b_z, at(b_z, h + 1))
                    for i in range(4):
                        dve.tensor_scalar(Lb[:, h % 2, BOFF[i]:BOFF[i] + BN[i]], bz(h, i), 40.0, None, ALU.min).then_inc(b_min, 1)

                def soft_max0(h):
                    for i in range(4):
                        blk = Lb[:, h % 2, BOFF[i]:BOFF[i] + BN[i]]
                        dve.wait_ge(b_ln, at(b_ln, 4 * h + i + 1))
                        dve.tensor_tensor(blk, blk, bz(h, i), ALU.max).then_inc(b_max, 1)

                dve.wait_ge(bk_out, at(bk_out, 5 * 16))
                for h in range(2):
                    weigh(3, h, h + 1)
                    clamp(h)
                    select(2, 4 * h, 4 * h + 4)
                    soft_max0(h)
                weigh(3, 2, 4)
                for h in range(6):
                    t, r, step = {0: (2, 8, 4), 3: (3, 0, 2), 4: (3, 4, 2)}.get(h, (3, 0, 0))
                    if h + 2 < 6:
                        clamp(h + 2)
                    select(t, r, r + step)
                    if h + 2 < 6:
                        soft_max0(h + 2)
                    half = slice(HD * (h % 2), HD * (h % 2) + HD)
                    dve.wait_ge(b_hi, at(b_hi, h + 1))
                    lo(aL[half, 3 + h // 2, 0:TP], ps[half, 6, :], aH[half, 3 + h // 2, 0:TP]).then_inc(b_lo, 1)
                    select(t, r + step, r + 2 * step)
                    if h in (1, 2):
                        pool_means(h - 1)

                def row_max(m):
                    t, a = m // 6, m % SOFT
                    dve.wait_ge(q_mm, at(q_mm, m + 1))
                    if m >= SOFT:
                        dve.wait_ge(q_exp, at(q_exp, m - SOFT + 1))
                    dve.tensor_reduce(stat[:, a, 0:1], ps[:, SOFT_BANK[a], 0:P * (t + 1)], AX.X, ALU.max).then_inc(dve_step, steps.step())
                    dve.wait_ge(dve_step, steps.value())
                    dve.tensor_scalar(stat[:, a, 1:2], stat[:, a, 0:1], -0.125, None, ALU.mult).then_inc(q_max, 1)

                row_max(0)
                row_max(1)
                for m in range(24):
                    a = m % SOFT
                    if m + 2 < 24:
                        row_max(m + 2)
                    dve.wait_ge(q_exp, at(q_exp, m + 1))
                    if m >= SOFT:
                        dve.wait_ge(q_norm, at(q_norm, m - SOFT + 1))
                    dve.reciprocal(stat[:, a, 3:4], stat[:, a, 2:3]).then_inc(dve_step, steps.step())
                    dve.wait_ge(dve_step, steps.value())
                    pr = prob[:, a, 0:P * (m // 6 + 1)]
                    dve.tensor_scalar(pr, pr, stat[:, a, 3:4], None, ALU.mult).then_inc(q_norm, 1)
                    if 4 <= m < 12:
                        select(3, m + 4, m + 5)
                    if m >= 6 and m % 3 == 0:
                        g = m // 3 - 2
                        n = g % 2
                        half = slice(HD * n, HD * n + HD)
                        cols = slice(P * (g // 2), P * (g // 2) + P)
                        dve.wait_ge(o_hi, at(o_hi, g + 1))
                        lo(aL[half, 0:3, cols], ps[half, 4 + n, 0:384].rearrange("p (j q) -> p j q", q=P), aH[half, 0:3, cols]).then_inc(o_lo, 1)

                for g in range(6, 8):
                    half, n = slice(HD * (g % 2), HD * (g % 2) + HD), g % 2
                    dve.wait_ge(o_hi, at(o_hi, g + 1))
                    lo(aL[half, 0:3, P * 3:P * 4], ps[half, 4 + n, 0:384].rearrange("p (j q) -> p j q", q=P), aH[half, 0:3, P * 3:P * 4]).then_inc(o_lo, 1)
                for m in range(2):
                    dve.wait_ge(y_hi, at(y_hi, m + 1))
                    dve.scalar_tensor_tensor(halves(aL[:, 6 + m, :]), psh(2 * m), vec(V_PS + m), halves(aH[:, 6 + m, :]).bitcast(F32),
                                             ALU.mult, ALU.subtract).then_inc(y_lo, 1)

                dve.wait_ge(d_zero, at(d_zero, 1))
                flat_qi = qim[:, :, :].rearrange("p b n -> p (b n)")
                for e in range(4):
                    rows = slice(HD * (e % 2), HD * (e % 2) + HD)
                    dst = bass.AP(qim, flat_qi.offset + TS * e, [list(flat_qi.ap[0]), [P + NS, NB], [1, NS]])
                    dve.tensor_copy(dst, featT[rows, F_QI + e // 2, TP:T].rearrange("p (b s) -> p b s", s=NS))
                    dve.tensor_copy(wic[TS * e:TS * e + TS, :], wi[0:TS, 4, e:e + 1])
                flat_qa = qam[:, :, :].rearrange("p b n -> p (b n)")
                for j in range(3):
                    dst = bass.AP(qam, flat_qa.offset + TS * j, [list(flat_qa.ap[0]), [96 + NS, NB], [1, NS]])
                    ins = dve.tensor_copy(dst, featT[:, F_QA + j, TP:T].rearrange("p (b s) -> p b s", s=NS))
                for i in range(2):
                    rows = slice(HD * i, HD * i + HD)
                    dve.tensor_copy(qbm[rows, :, i, :], featT[rows, F_QB:F_QB + 3, TP:T])
                dve.tensor_copy(bb_n[:, :], dcon[0:TS, D_BB:D_BB + TS])
                dve.memset(m8d[:, :], PADDED)
                dve.memset(sco_d[:, KEYS_S:], PADDED).then_inc(dve_step, steps.step())
                dve.wait_ge(dve_step, steps.value())
                dve.tensor_copy(st_d[:, 0, 3:4], con[0:96, C_1:C_1 + 1]).then_inc(d_q, 1)
                dve.wait_ge(d_new, at(d_new, 1))
                dve.tensor_scalar(L_d[:, :], ps[:, 3, 0:384], 40.0, None, ALU.min)
                dve.tensor_scalar(L_n[:, :], ps[0:TS, 4, 0:192], 40.0, None, ALU.min).then_inc(d_min, 1)
                dve.wait_ge(d_relu, at(d_relu, 1))
                dve.tensor_scalar(rel_d[:, :], rel_d[:, :], wic[:, 0:1], None, ALU.mult).then_inc(d_rel, 1)
                dve.wait_ge(d_ln, at(d_ln, 1))
                dve.tensor_tensor(L_d[:, :], L_d[:, :], ps[:, 3, 0:384], ALU.max)
                dve.tensor_tensor(L_n[:, :], L_n[:, :], ps[0:TS, 4, 0:192], ALU.max).then_inc(dve_step, steps.step())
                dve.wait_ge(dve_step, steps.value())
                dve.tensor_tensor(L_n[:, :], L_n[:, :], dcon[0:TS, D_MB:D_MB + 192], ALU.mult).then_inc(d_sp, 1)
                dve.wait_ge(d_sum, at(d_sum, 1))
                dve.tensor_tensor(sco_d[:, 0:KEYS_S], ps[0:TS, 7, 0:KEYS_S], dcon[0:TS, D_MA:D_MA + KEYS_S], ALU.add).then_inc(dve_step, steps.step())
                dve.wait_ge(dve_step, steps.value())
                hold(dve)
                for _ in range(TOPK_S // 8):
                    dve.max(m8d[:, 0:8], sco_d[:, :]).then_inc(dve_step, steps.step())
                    dve.wait_ge(dve_step, steps.value())
                    hold(dve)
                    dve.match_replace(sco_d[:, :], m8d[:, 0:8], sco_d[:, :], TAKEN).then_inc(dve_step, steps.step())
                    dve.wait_ge(dve_step, steps.value())
                    hold(dve)
                dve.max(m8d[:, 0:8], sco_d[:, :]).then_inc(dve_step, steps.step())
                dve.wait_ge(dve_step, steps.value())
                hold(dve)
                dve.tensor_copy(m8d[:, 8:9], m8d[:, 0:1]).then_inc(dve_step, steps.step())
                dve.wait_ge(dve_step, steps.value())
                hold(dve)
                dve.match_replace(sco_d[:, :], m8d[:, 8:16], sco_d[:, :], TAKEN).then_inc(dve_step, steps.step())
                dve.wait_ge(dve_step, steps.value())
                hold(dve)
                dve.tensor_scalar(bias_d[:, :], sco_d[:, 0:KEYS_S], CUT, NEG, ALU.is_gt, ALU.mult).then_inc(d_bias, 1)
                dve.wait_ge(d_log, at(d_log, 1))
                for n in range(2):
                    dve.tensor_reduce(st_d[:, n, 0:1], ps[0:96, 1 + n, 0:KEYS_S], AX.X, ALU.max).then_inc(dve_step, steps.step())
                    dve.wait_ge(dve_step, steps.value())
                    dve.tensor_scalar(st_d[:, n, 1:2], st_d[:, n, 0:1], -0.125, None, ALU.mult).then_inc(d_max, 1)
                for n in range(2):
                    dve.wait_ge(d_exp, at(d_exp, n + 1))
                    dve.reciprocal(st_d[:, n, 3:4], st_d[:, n, 2:3]).then_inc(dve_step, steps.step())
                    dve.wait_ge(dve_step, steps.value())
                    dve.tensor_scalar(P_d[:, n, :], P_d[:, n, :], st_d[:, n, 3:4], None, ALU.mult).then_inc(d_nrm, 1)
                for n in range(2):
                    dve.wait_ge(d_hi, at(d_hi, n + 1))
                    lo(aL[:, 3 * n:3 * n + 3, TP:T], ps[:, 3 * n, 0:96].rearrange("p (j q) -> p j q", q=TS), aH[:, 3 * n:3 * n + 3, TP:T]).then_inc(d_lo, 1)

                for m in range(KD):
                    split(U_OUT + m + 2)
                    dve.wait_ge(w_used, at(w_used, U_OUT + m + SPLIT + 1))
                    dve.tensor_tensor(halves(hT[:, m, :]), halves(hT[:, m, :]), psh(2 * (m % 3)), ALU.add).then_inc(h_new, 1)
                norm(1)

                def ffn(slot, f, uo, i):
                    split(U_UP + uo + 2, i, 4)
                    dve.wait_ge(c_1, at(c_1, f + 1))
                    dve.scalar_tensor_tensor(Cv[:, slot, :], G[:, slot, 1:GW - 1], vec_at(V_CW + KF, f), Cv[:, slot, :],
                                             ALU.mult, ALU.add).then_inc(c_2, 1)
                    dve.wait_ge(c_2, at(c_2, f + 1))
                    dve.scalar_tensor_tensor(Cv[:, slot, :], G[:, slot, 2:GW], vec_at(V_CW + 2 * KF, f), Cv[:, slot, :],
                                             ALU.mult, ALU.add).then_inc(c_3, 1)
                    dve.wait_ge(s_g, at(s_g, f + 1))
                    dve.tensor_tensor(Cv[:, slot, :], Cv[:, slot, :], G[:, slot, 2:GW], ALU.mult).then_inc(s_mul, 1)
                    split(U_UP + uo + 3, i, 4)
                    dve.wait_ge(s_mul, at(s_mul, f + 1))
                    dve.wait_ge(w_used, at(w_used, 2 * f + U_UP + 1 + SPLIT + 1))
                    b = 4 * slot + 2
                    dve.tensor_tensor(a_tmp[:, slot, 0:HALF], Cv[:, slot, 0:HALF], ps[:, b, 0:HALF], ALU.mult)
                    dve.tensor_tensor(a_tmp[:, slot, HALF:TP], Cv[:, slot, HALF:TP], ps[:, b + 1, 0:TP - HALF], ALU.mult)
                    c_s = Cv[:, slot, TP:].rearrange("p (b s) -> p b s", s=6)
                    dve.tensor_tensor(a_tmp[:, slot, TP:T].rearrange("p (b s) -> p b s", s=NS), c_s[:, :, 2:6],
                                      ps[:, b + 1, TP - HALF:HALF].rearrange("p (b s) -> p b s", s=NS), ALU.mult).then_inc(v_mul, 1)
                    dve.wait_ge(f_hi, at(f_hi, f + 1))
                    lo(act_at(actL, f), a_tmp[:, slot, :], act_at(actH, f)).then_inc(f_lo, 1)

                with dve.Fori(0, KF // 2) as i:
                    for j in range(2):
                        ffn(j, 2 * i + j, 2 * j, i)
                with dve.Fori(0, 2) as i:
                    for j in range(4):
                        for q in range(3):
                            split(U_DOWN + 3 * j + q + 2, i, 12)
                        dve.wait_ge(w_used, at(w_used, 12 * i + U_DOWN + 3 * j + 2 + SPLIT + 1))
                        h = hT[:, bass.ds(4 * i + j, 1), :].rearrange("p o (h n) -> p (o h) n", h=2)
                        dve.tensor_tensor(h, h, psh(DOWN_BANK[j]), ALU.add).then_inc(h_new, 1)

                for b in range(3):
                    dve.wait_ge(pp_hi, at(pp_hi, b + 1))
                    if b < 2:
                        q = slice(256 * b, 256 * b + 256)
                        for k in range(2):
                            ins = lo(pL[:, k, q].rearrange("p (t q) -> p t q", q=P),
                                     ps[:, PP_BANK[b], :].rearrange("p (t k q) -> p k t q", k=2, q=P)[:, k],
                                     pH[:, k, q].rearrange("p (t q) -> p t q", q=P))
                    else:
                        ins = lo(pL[:, :, TP:T], ps[:, PP_BANK[b], 0:256].rearrange("p (k q) -> p k q", q=P)[:, :, 0:TS], pH[:, :, TP:T])
                    ins.then_inc(pp_lo, 1)

                def keep_out(b):
                    dve.wait_ge(kp_tr, at(kp_tr, b + 1))
                    w = 512 if b < 5 else 256
                    dve.tensor_copy(keep_tok[:, 512 * b:512 * b + w], ps[0:18, KEEP_BANK[b], 0:w]).then_inc(kp_ev, 1)

                norm(2)
                split(U_PROJ + 3)
                for m in range(KD):
                    if m + 2 < KD:
                        split(U_GATE + m + 2)
                    dve.wait_ge(gt_sig, at(gt_sig, m + 1))
                    dve.tensor_tensor(sig[:, m % 2, :], sig[:, m % 2, :], projT[:, m, :], ALU.mult).then_inc(dve_step, steps.step())
                    dve.wait_ge(dve_step, steps.value())
                    dve.tensor_tensor(hT[:, m, :], hT[:, m, :], sig[:, m % 2, :], ALU.add).then_inc(h_new, 1)
                    if m < 6:
                        keep_out(m)
                assert steps.n == DVE_STEPS, steps.n
            for i in range(2 * TILES):
                t, b, n = i // 2, i % 2, TOKW[i // 2]
                dve.wait_ge(y_tr, i + 1)
                dve.tensor_copy(xy[0:n, t, 512 * b:512 * b + 512], ps[0:n, i % 8, :]).then_inc(y_ev, 1)

        @block.tensor
        def _(pe):
            pe.sem_inc(w_used, SPLIT)
            pe.wait_ge(con_ld, 16)
            pe.wait_ge(x_ld, 32)
            for i in range(2 * TILES):
                t, b, n = i // 2, i % 2, TOKW[i // 2]
                if i >= 8:
                    pe.wait_ge(emb_ev, i - 7)
                for k in range(4):
                    mm = pe.transpose(ps[:, i % 8, P * k:P * k + n], xy[0:n, t, P * (4 * b + k):P * (4 * b + k) + P], ident[0:n, 0:n])
                mm.then_inc(emb_tr, 1)
            pe.wait_ge(con_cast, 1)
            with pe.Fori(0, LAYERS) as l:
                def at(s, n):
                    return l * per_layer[s.name] + n

                def tri_product(out, wh, wl, xh, xl, start, stop):
                    pe.matmul(out, wh, xh, start=start, stop=False)
                    pe.matmul(out, wh, xl, start=False, stop=False)
                    return pe.matmul(out, wl, xh, start=False, stop=stop)

                def dense(bank, u, blocks, xH, xL, first, last, c0=0, stride=P, norm_=None):
                    H, Lo = w_H[u % SPLIT], w_L[u % SPLIT]
                    for n, k in enumerate(blocks):
                        if norm_ is not None:
                            pe.wait_ge(a_lo, at(a_lo, 8 * norm_ + k + 1))
                        w = slice(c0 + stride * n, c0 + stride * n + P)
                        for half in range(2):
                            x = slice(HALF * half, HALF * half + HALF)
                            mm = tri_product(ps[:, bank + half, 0:HALF], H[:, w], Lo[:, w], xH[:, k, x], xL[:, k, x],
                                             first and n == 0, last and n == len(blocks) - 1)
                    return mm

                def square_sum(i, k, turn=0, start=False):
                    pe.wait_ge(n_sq, at(n_sq, turn + 8 * i + k + 1))
                    b = SUM_BANK[i]
                    pe.matmul(ps[:, b, 0:HALF], mean, a_tmp[:, k % 2, 0:HALF], start=start, stop=True, skip_group_check=True)
                    pe.matmul(ps[:, b + 1, 0:HALF], mean, a_tmp[:, k % 2, HALF:T], start=start, stop=True, skip_group_check=True).then_inc(n_ss, 1)

                pe.wait_ge(vec_ld, at(vec_ld, 6 * 16))
                pe.wait_ge(h_new, at(h_new, KD))
                pe.transpose(ps[:, 0, 0:NV], vec_raw[0:NV, :], ident[0:NV, 0:NV]).then_inc(vec_tr, 1)
                for k in range(KD):
                    square_sum(0, k, start=k == 0)

                def proj_free(i):
                    c, t = divmod(i, 5)
                    if c < 2:
                        pe.wait_ge(p_ev, at(p_ev, i + 1))
                    elif c < 4:
                        pe.wait_ge(plain_ok, at(plain_ok, i - 10 + 1))
                    else:
                        pe.wait_ge(p_ev, at(p_ev, 10 + t + 1))

                def turn(c, t):
                    g, n = 5 * c + t, TOKW[t]
                    if c < 2:
                        pe.wait_ge(rope_ok, at(rope_ok, 5 * c + t + 1))
                    else:
                        pe.wait_ge(plain_ok, at(plain_ok, 5 * (c - 2) + t + 1))
                    if g >= 1:
                        pe.wait_ge(t_ev, at(t_ev, g))
                    if c >= 2 and t in (0, 2) or g == 15:
                        hold(pe)
                        pe.wait_ge(i_relu, at(i_relu, 4 * (c - 2) + {0: 2, 2: 3}[t]))
                    if g == 0:
                        pe.wait_ge(n_rec, at(n_rec, 1))
                    if t == TILES - 1:
                        hold(pe)
                    for b in range(CH_BLOCKS[c][1]):
                        mm = pe.transpose(ps[:, 7, P * b:P * b + n], r_tok[0:n, t, P * b:P * b + P], ident[0:n, 0:n])
                    mm.then_inc(t_mm, 1)

                def index(t, e):
                    if t == 3:
                        if e == 0:
                            pe.wait_ge(uo_ev, at(uo_ev, 1))
                        else:
                            pe.wait_ge(i_relu, at(i_relu, 8 + e))
                    elif e == 1:
                        pe.wait_ge(i_relu, at(i_relu, 4 * (t - 1) + 1))
                    else:
                        pe.wait_ge(t_ev, at(t_ev, 5 * (t + 1) + {0: 0, 2: 2, 3: 5}[e]))
                    rows = slice(HD * (e % 2), HD * (e % 2) + HD)
                    pe.matmul(ps[:, 7, 0:P * (t + 1)], featT[rows, F_QI + e // 2, P * t:P * t + P], featT[rows, F_KI, 0:P * (t + 1)],
                              start=True, stop=True).then_inc(i_mm, 1)

                for c in range(5):
                    w = CHUNK[c][1] - CHUNK[c][0]
                    for k in range(KD):
                        u = 4 * c + k // 2
                        pe.wait_ge(w_lo, at(w_lo, RAW + u + 1))
                        if c == 0:
                            hold(pe)
                            pe.wait_ge(a_lo, at(a_lo, k + 1))
                        wh, wl = (x[u % SPLIT][:, 512 * (k % 2):512 * (k % 2) + w] for x in (w_H, w_L))
                        for t in range(TILES):
                            i, n = 5 * c + t, TOKW[t]
                            if k == 0:
                                if i >= 7:
                                    proj_free(i - 7)
                            tok = slice(P * t, P * t + n)
                            mm = tri_product(ps[0:n, i % 7, 0:w], aH[:, k, tok], aL[:, k, tok], wh, wl, k == 0, k == KD - 1)
                            if k == KD - 1 and t < TILES - 1:
                                mm.then_inc(p_mm, 1)
                        if k % 2:
                            mm.then_inc(w_used, 1)
                        if c >= 3 and k in (0, 1, 4):
                            index(c - 2, (0, 1, 4).index(k))
                        if c >= 1 and k in GROUP_K:
                            turn(c - 1, GROUP_K.index(k))
                        if c >= 3 and k == KD - 1:
                            index(c - 2, 3)
                pe.wait_ge(lay_ld, at(lay_ld, 6 * 16))
                pe.wait_ge(t_ev, at(t_ev, 20))
                pe.wait_ge(i_relu, at(i_relu, 8))
                for m in range(2):
                    mm = pe.transpose(ps[:, 7, P * m:P * m + 120], pst_tok[0:120, P * m:P * m + P], ident[0:120, 0:120])
                mm.then_inc(ph_tr, 1)
                for m in range(2):
                    u = U_U + m
                    pe.wait_ge(w_lo, at(w_lo, RAW + u + 1))
                    proj_free(19 if m == 0 else 24)
                    H, Lo = w_H[u % SPLIT], w_L[u % SPLIT]
                    for half in range(2):
                        x = slice(HALF * half, HALF * half + HALF)
                        for k in range(KD):
                            wk = slice(P * k, P * k + P)
                            mm = tri_product(ps[:, U_BANK[m][half], 0:HALF], H[:, wk], Lo[:, wk], aH[:, k, x], aL[:, k, x], k == 0, k == KD - 1)
                    mm.then_inc(w_used, 1)
                pe.wait_ge(u_cp, at(u_cp, 1))
                for m in range(2):
                    pe.transpose(ps[0:120, 7, P * m:P * m + P], u_c[:, m, :], ident)
                    mm = pe.transpose(ps[0:15, 7, 256 + P * m:256 + P * m + P], u_p[:, m, TP:TP + 15], ident)
                mm.then_inc(uo_tr, 1)

                def logits(h):
                    rows = slice(HD * (h % 2), HD * (h % 2) + HD)
                    if h >= 2:
                        pe.wait_ge(b_exp, at(b_exp, 4 * (h - 1)))
                    for i in range(4):
                        mm = pe.matmul(bz(h, i), featT[rows, F_KB + h // 2, P * i:P * i + P], featT[rows, F_QB + h // 2, P * i:TP],
                                       start=i != 3, stop=True, skip_group_check=True)
                    mm.then_inc(b_z, 1)

                def remainders(h):
                    pe.wait_ge(b_diag, at(b_diag, 4 * h + 4))
                    for i in range(4):
                        pe.matmul(bz(h, i), ntri, Lb[:, h % 2, BOFF[i]:BOFF[i] + BN[i]], start=False, stop=False, skip_group_check=True)
                        for j in range(i + 1, 4):
                            pe.matmul(bz(h, i, P * (j - i)), nones, Lb[:, h % 2, BOFF[j]:BOFF[j] + BN[j]], start=False, stop=False, skip_group_check=True)
                        mm = pe.matmul(bz(h, i, 0, P), id_bf, bb_bf, start=False, stop=True, skip_group_check=True)
                    mm.then_inc(b_tri, 1)

                def b_out(h):
                    if h >= 1:
                        pe.wait_ge(b_lo, at(b_lo, h))
                    for i in range(4):
                        pe.wait_ge(b_exp, at(b_exp, 4 * h + i + 1))
                        mm = pe.matmul(ps[HD * (h % 2):HD * (h % 2) + HD, 6, P * i:TP], V[:, i, P + HD * h:P + HD * h + HD],
                                       Ab[:, BOFF[i]:BOFF[i] + BN[i]], start=i == 0, stop=i == 3, skip_group_check=True)
                    mm.then_inc(b_o, 1)

                index(3, 0)
                logits(0)
                index(3, 1)
                logits(1)
                index(3, 2)
                remainders(0)
                index(3, 3)
                for h in range(6):
                    b_out(h)
                    if h + 2 < 6:
                        logits(h + 2)
                    if h + 1 < 6:
                        remainders(h + 1)

                def a_logits(m):
                    t, n, j = m // 6, m % 6 // 3, m % 3
                    rows, W = slice(HD * n, HD * n + HD), P * (t + 1)
                    if m >= SOFT:
                        pe.wait_ge(q_exp, at(q_exp, m - SOFT + 1))
                    elif m == 0:
                        pe.wait_ge(b_exp, at(b_exp, 24))
                    elif m == 2:
                        pe.wait_ge(b_lo, at(b_lo, 6))
                    b = SOFT_BANK[m % SOFT]
                    if m % 6 == 0 and t >= 1:
                        pe.wait_ge(sel_ok, at(sel_ok, t))
                    pe.matmul(ps[:, b, 0:W], featT[rows, F_QA + j, P * t:P * t + P], featT[rows, F_KA, 0:W], start=True, stop=False)
                    pe.matmul(ps[:, b, 0:W], id_bf, ba_bf if t == 0 else bias_p[:, t - 1, 0:W], start=False, stop=True).then_inc(q_mm, 1)

                def a_out(g):
                    t, n = g // 2, g % 2
                    pe.wait_ge(pt_ev, at(pt_ev, 3 * g + 3))
                    if g >= 2:
                        pe.wait_ge(o_lo, at(o_lo, g - 1))
                    for b in range(t + 1):
                        mm = pe.matmul(ps[HD * n:HD * n + HD, 4 + n, 0:384], V[:, b, HD * n:HD * n + HD], probT[:, b, :, :],
                                       start=b == 0, stop=b == t)
                    mm.then_inc(o_mm, 1)

                for m in range(SOFT):
                    a_logits(m)
                for m in range(24):
                    pe.wait_ge(q_norm, at(q_norm, m + 1))
                    if m >= 2:
                        pe.wait_ge(pt_ev, at(pt_ev, m - 1))
                    for b in range(m // 6 + 1):
                        mm = pe.transpose(ps[:, 2 + m % 2, P * b:P * b + P], prob[:, m % SOFT, P * b:P * b + P], ident)
                    mm.then_inc(pt_mm, 1)
                    if m + SOFT < 24:
                        a_logits(m + SOFT)
                    if m >= 3 and m % 3 == 0:
                        a_out(m // 3 - 1)
                a_out(7)
                for m in range(2):
                    pe.wait_ge(pooled_ok, at(pooled_ok, m + 1))
                    hold(pe)
                    for g in range(2):
                        rows = slice(HD * g, HD * g + HD)
                        for half in range(2):
                            mm = pe.matmul(ps[rows, 2 * m + half, 0:HALF], w_pool[rows, m, :], pooled[rows, m, HALF * half:HALF * half + HALF],
                                           start=True, stop=True)
                    mm.then_inc(y_mm, 1)

                pe.wait_ge(o_lo, at(o_lo, 8))
                pe.wait_ge(y_lo, at(y_lo, 2))

                def page_turn(pg):
                    pe.wait_ge(kp_ld[pg % 3], at(kp_ld[pg % 3], 48 * (pg // 3 + 1)))
                    hold(pe)
                    if pg >= 2:
                        pe.wait_ge(kt_ev, at(kt_ev, pg - 1))
                        hold(pe)
                    pe.transpose(ps[0:HD, 7 - 3 * (pg % 2), 0:P], KP[:, pg % 3, 512:576], ident)
                    for b in range(4):
                        mm = pe.transpose(ps[:, 5 + pg % 2, P * b:P * b + P], KP[:, pg % 3, P * b:P * b + P], ident)
                    mm.then_inc(kt_mm, 1)

                def page_logits(pg):
                    b, p = pg // 2, pg % 2
                    kt = KT[:, pg % 2, :]
                    pe.wait_ge(kt_ev, at(kt_ev, pg + 1))
                    cols = slice(P * p, P * p + P)
                    pe.matmul(ps[:, 0, cols], qim[:, b, :], kt[0:HD, 512:640], start=pg == 0, stop=True, skip_group_check=True)
                    for n in range(2):
                        rows = slice(HD * n, HD * n + HD)
                        pe.matmul(ps[0:96, 1 + n, cols], qam[rows, b, :], kt[rows, 0:128], start=pg == 0, stop=True, skip_group_check=True)
                    for j in range(3):
                        out = ps[:, 3, 192 * p + 2 * TS * j:192 * p + 2 * TS * j + 2 * TS].rearrange("p (i q) -> p i q", q=TS)
                        mm = pe.matmul(out[:, :, NS * b:NS * b + NS], kt[:, P + P * j:P + P * j + P], qbm[:, j, :, NS * b:NS * b + NS],
                                       start=pg == 0 and j == 0, stop=True, skip_group_check=True)
                    mm.then_inc(kq_mm, 1)

                page_turn(0)
                pe.wait_ge(d_q, at(d_q, 1))
                for pg in range(NPAGES):
                    if pg + 1 < NPAGES:
                        page_turn(pg + 1)
                    page_logits(pg)
                pe.wait_ge(kq_mm, at(kq_mm, NPAGES))
                hold(pe)
                for e in range(4):
                    rows = slice(HD * (e % 2), HD * (e % 2) + HD)
                    pe.matmul(ps[TS * e:TS * e + TS, 0, PAST:KEYS_S], featT[rows, F_QI + e // 2, TP:T], featT[rows, F_KI, TP:T],
                              start=False, stop=True, skip_group_check=True)
                for n in range(2):
                    rows = slice(HD * n, HD * n + HD)
                    for j in range(3):
                        pe.matmul(ps[TS * j:TS * j + TS, 1 + n, PAST:KEYS_S], featT[rows, F_QA + j, TP:T], featT[rows, F_KA, TP:T],
                                  start=False, stop=True, skip_group_check=True)
                for j in range(3):
                    mm = pe.matmul(ps[0:TS, 4, 2 * TS * j:2 * TS * j + 2 * TS], featT[:, F_KB + j, TP:T], qbm[:, j, :, :],
                                   start=j == 0, stop=True, skip_group_check=True)
                mm.then_inc(d_new, 1)
                pe.wait_ge(d_rel, at(d_rel, 1))
                for e in range(4):
                    mm = pe.matmul(ps[0:TS, 7, 0:KEYS_S], ident[:, TS * e:TS * e + TS], rel_d[:, :], start=e == 0, stop=e == 3)
                mm.then_inc(d_sum, 1)
                pe.wait_ge(d_sp, at(d_sp, 1))
                L0, L1 = L_d[:, 0:192], L_d[:, 192:384]
                z0, z1, zn = ps[:, 3, 0:192], ps[:, 3, 192:384], ps[0:TS, 4, 0:192]
                g = dict(start=False, stop=True, skip_group_check=True)
                pe.matmul(z1, ntri, L1, **g)
                pe.matmul(z1, nones[0:TS, :], L_n[:, :], **g)
                pe.matmul(z0, ntri, L0, **g)
                pe.matmul(z0, nones, L1, **g)
                pe.matmul(z0, nones[0:TS, :], L_n[:, :], **g)
                pe.matmul(zn, ntri[0:TS, 0:TS], L_n[:, :], **g)
                pe.matmul(zn.rearrange("p (h q) -> p h q", q=TS), id_bf[0:TS, 0:TS], bb_n[:, :].unsqueeze(1).to_broadcast([TS, 6, TS]), **g).then_inc(d_tri, 1)
                pe.wait_ge(d_A, at(d_A, 1))
                for h in range(6):
                    half, j = h % 2, h // 2
                    pe.matmul(ps[HD * half:HD * half + HD, 3, TS * j:TS * j + TS], V[0:TS, 4, P + HD * h:P + HD * h + HD],
                              A_n[:, TS * h:TS * h + TS], start=j == 0, stop=True, skip_group_check=True)
                for pg in range(NPAGES):
                    b, p = pg // 2, pg % 2
                    v = VP[:, pg, :]
                    if pg % 4 == 0:
                        pe.wait_ge(vp_ld[pg // 4], at(vp_ld[pg // 4], 4 * 32))
                    for h in range(6):
                        half, j = h % 2, h // 2
                        c, a = TS * j + NS * b, 192 * p + TS * h + NS * b
                        pe.matmul(ps[HD * half:HD * half + HD, 3, c:c + NS], v[:, P + HD * h:P + HD * h + HD], A_d[:, a:a + NS], **g)
                pe.wait_ge(d_bias, at(d_bias, 1))
                for n in range(2):
                    mm = pe.matmul(ps[0:96, 1 + n, 0:KEYS_S], id3_bf[:, :], bias_d[:, :], **g)
                mm.then_inc(d_log, 1)
                pe.wait_ge(d_nrm, at(d_nrm, 2))
                for n in range(2):
                    for p in range(2):
                        pe.transpose(ps[:, 5 + n, 96 * p:96 * p + 96], P_d[:, n, P * p:P * p + P], ident[0:96, 0:96])
                    mm = pe.transpose(ps[0:TS, 5 + n, 192:288], P_d[:, n, PAST:KEYS_S], ident[0:96, 0:96])
                mm.then_inc(d_ptm, 1)
                pe.wait_ge(d_pte, at(d_pte, 1))
                for n in range(2):
                    pe.matmul(ps[HD * n:HD * n + HD, 0, 0:96], V[0:TS, 4, HD * n:HD * n + HD], PT_d[0:TS, n, 2, :],
                              start=True, stop=True, skip_group_check=True)
                for pg in range(NPAGES):
                    b, p = pg // 2, pg % 2
                    v = VP[:, pg, :]
                    for n in range(2):
                        out = ps[HD * n:HD * n + HD, 0, 0:96].rearrange("p (j b s) -> p j b s", b=NB, s=NS)[:, :, b, :]
                        mm = pe.matmul(out, v[:, HD * n:HD * n + HD], PT_d[:, n, p, :].rearrange("p (j b s) -> p j b s", b=NB, s=NS)[:, :, b, :], **g)
                    mm.then_inc(vp_use, 1)
                pe.wait_ge(d_lo, at(d_lo, 2))
                for m in range(KD):
                    u = U_OUT + m
                    pe.wait_ge(w_lo, at(w_lo, RAW + u + 1))
                    if m >= 3:
                        pe.wait_ge(h_new, at(h_new, KD + m - 2))
                    dense(2 * (m % 3), u, range(KD), aH, aL, True, True).then_inc(w_used, 1)
                    if m >= 1:
                        square_sum(1, m - 1, start=m == 1)
                square_sum(1, KD - 1)
                pe.wait_ge(st_ld, at(st_ld, 16))
                hold(pe)
                for f in range(KF):
                    mm = pe.transpose(ps[:, 5, 16 * f:16 * f + 16], st_tok[:, P * f:P * f + P], ident[0:16, 0:16])
                mm.then_inc(st_tr, 1)
                pe.wait_ge(st_ev, at(st_ev, 1))
                hold(pe)
                with pe.Fori(0, KF // 2) as i:
                    for j in range(4):
                        n = 4 * i + j
                        pe.wait_ge(w_lo, at(w_lo, RAW + U_UP + n + 1))
                        if j % 2 == 0:
                            pe.wait_ge(v_mul, at(v_mul, 2 * i + j // 2 + 1))
                        dense(2 * j, j, range(KD), aH, aL, True, True, norm_=1 if j == 0 else None).then_inc(w_used, 1)
                pe.wait_ge(v_mul, at(v_mul, KF - 2 + 3))
                hold(pe)
                for b in range(2, 4):
                    pe.matmul(ps[:, b, 0:HALF], con_bf[:, 3, :], con_bf[:, :, :].rearrange("p a n -> p (a n)")[:, 0:HALF], start=True, stop=True)
                with pe.Fori(0, 2) as i:
                    for j in range(4):
                        for q in range(3):
                            u = U_DOWN + 3 * j + q
                            pe.wait_ge(w_lo, at(w_lo, i * 12 + RAW + u + 1))
                            if q == 0:
                                pe.wait_ge(h_new, at(h_new, 4 * i + 2 * KD + j - 1))
                            if j == 0:
                                hold(pe)
                                pe.wait_ge(f_lo, at(f_lo, 8 * q + DOWN_K[q]))
                            dense(DOWN_BANK[j], u, range(8 * q, 8 * q + DOWN_K[q]), actH, actL, q == 0, q == 2).then_inc(w_used, 1)
                            if q == 0 and j >= 1:
                                square_sum(2, j - 1, 4 * i)
                    square_sum(2, 3, 4 * i)
                pe.wait_ge(p_ld, at(p_ld, 32))
                pe.wait_ge(h_new, at(h_new, 3 * KD))
                hold(pe)
                for t in range(TILES):
                    n = TOKW[t]
                    for k in range(2):
                        c = 256 * (t % 2) + P * k
                        mm = pe.transpose(ps[:, PP_BANK[t // 2], c:c + n], p_tok[0:n, t, P * k:P * k + P], ident[0:n, 0:n])
                mm.then_inc(pp_tr, 1)
                pe.wait_ge(g_keep, at(g_keep, KF))

                def keep_turn(b):
                    for f in range(4 * b, min(4 * b + 4, KF)):
                        mm = pe.transpose(ps[0:18, KEEP_BANK[b], P * (f % 4):P * (f % 4) + P], keepT[:, f, :], ident)
                    mm.then_inc(kp_tr, 1)
                pe.wait_ge(pp_lo, at(pp_lo, 3))
                for q in range(2):
                    u = U_PROJ + q
                    pe.wait_ge(w_lo, at(w_lo, RAW + u + 1))
                    for mm_ in range(4):
                        m = 4 * q + mm_
                        if m >= 3:
                            pe.wait_ge(pr_ev, at(pr_ev, m - 2))
                        mm = dense(PROJ_BANK[m % 3], u, range(2), pH, pL, True, True, c0=P * mm_, stride=512)
                        mm.then_inc((w_used if mm_ == 3 else pr_mm), 1)
                for m in range(KD):
                    u = U_GATE + m
                    pe.wait_ge(w_lo, at(w_lo, RAW + u + 1))
                    if m >= 3:
                        pe.wait_ge(gt_sig, at(gt_sig, m - 2))
                    else:
                        hold(pe)
                        pe.wait_ge(pr_ev, at(pr_ev, 8))
                    dense(2 * (m % 3), u, range(KD), aH, aL, True, True, norm_=2 if m == 0 else None).then_inc(w_used, 1)
                    if m < 6:
                        if m >= 2:
                            pe.wait_ge(kp_ev, at(kp_ev, m - 1))
                            hold(pe)
                        keep_turn(m)
            pe.wait_ge(h_new, KD + LAYERS * per_layer[h_new.name])
            for i in range(2 * TILES):
                t, b, n = i // 2, i % 2, TOKW[i // 2]
                if i >= 8:
                    pe.wait_ge(y_ev, i - 7)
                for k in range(4):
                    mm = pe.transpose(ps[0:n, i % 8, P * k:P * k + P], hT[:, 4 * b + k, P * t:P * t + n], ident)
                mm.then_inc(y_tr, 1)


_INS = ["x_prompt", "x_sample", "cache_a_k", "cache_a_v", "cache_idx_k", "cache_b_k", "cache_b_v", "state_pool",
        "state_conv", "page_table", "p_prompt", "p_sample", "g_attn", "w_in", "g_q_a", "g_k_a", "w_pool",
        "pool_scale", "w_out", "g_ffn", "w_up", "conv_w", "conv_b", "w_down", "g_ple", "w_ple_gate", "w_ple_proj"]
_NEW = {"a_k": (2, HD), "a_v": (2, HD), "idx_k": (HD,), "b_k": (6, HD), "b_v": (6, HD)}


def _outputs():
    yield "y_prompt", (1, TP, D)
    yield "y_sample", (NB, NS, D)
    for kind, lead, rows in (("p", (LAYERS, 1), TP), ("s", (LAYERS, NB), NS)):
        for name, tail in _NEW.items():
            yield f"{name}_{kind}", lead + (rows,) + tail
        yield f"pool_{kind}", lead + (15, 256)
        yield f"conv_{kind}", lead + (2, DFF)


def kernel(**inputs):
    import concourse.bacc as bacc
    from concourse.bass_utils import run_bass_kernel_spmd

    nc = bacc.Bacc("TRN2", target_bir_lowering=False, num_devices=1)
    arrays, t_in, t_out = {}, {}, {}
    given = {name: np.ascontiguousarray(inputs[name]) for name in _INS}
    given["con"], given["dcon"] = shape_constants()
    for name, a in given.items():
        arrays[f"in_{name}"] = a
        t_in[name] = nc.dram_tensor(f"in_{name}", a.shape, mybir.dt.from_np(a.dtype), kind="ExternalInput").ap()
    for name, shape in _outputs():
        t_out[name] = nc.dram_tensor(f"out_{name}", shape, F32, kind="ExternalOutput").ap()
    build(nc, t_in, t_out)
    r = run_bass_kernel_spmd(nc, [arrays], core_ids=[0])
    return tuple(r.results[0][f"out_{name}"] for name, _ in _outputs())
```
